# Optimizing a Trainium2 kernel written in Bass

```python
import jax, jax.numpy as jnp
from jax import lax
import numpy as np

D_MODEL = 1024
BATCH = 1
SEQ = 512
DEPTH = 2
DEC_BATCH = 8
DEC_SEQ = 4
PAST_LEN = 2048
PAGE_SIZE = 128

HEAD_DIM = 64
GW = D_MODEL // 4
N_HEADS = GW // HEAD_DIM
SCALE = HEAD_DIM ** -0.5
MLSTM_CHUNK = 64
MLSTM_CONV = 4
M_INIT = -1e30
NSA_KV_HEADS = 2
NSA_GROUP = N_HEADS // NSA_KV_HEADS
KVW = NSA_KV_HEADS * HEAD_DIM
CMP_BLOCK = 32
CMP_STRIDE = 16
CMP_HIDDEN = HEAD_DIM
SLC_BLOCK = 64
N_SELECT = 16
WINDOW = 512
SLC_Q_BLOCK = 32
WIN_Q_BLOCK = 128
DECAY_LORA = 64
AAA_LORA = 64
RWKV_SHIFT = 3 * GW + DECAY_LORA + AAA_LORA
RWKV_LN_EPS = HEAD_DIM * 1e-5
N_MEM = 256
MEM_HEADS = 4
MEM_HEAD_DIM = GW // MEM_HEADS
ROPE_THETA = 10000.0
NORM_EPS = 1e-6
MLSTM_SIZES = (GW, GW, GW, N_HEADS, N_HEADS, GW, GW)
NSA_SIZES = (GW, KVW, KVW, KVW, KVW, KVW, KVW, 3 * N_HEADS, GW)
RWKV_SIZES = (RWKV_SHIFT, GW)
MEM_SIZES = (GW, GW)
GROUP_SIZES = (sum(MLSTM_SIZES), sum(NSA_SIZES), sum(RWKV_SIZES), sum(MEM_SIZES))
D_IN = sum(GROUP_SIZES)

kernel_name = 'hymba_mlstm_nsa_rwkv7_mem_step'

def _split(x, sizes):
    out, start = [], 0
    for s in sizes:
        out.append(x[..., start:start + s])
        start += s
    return out

def _stack_layers(states, i):
    return jnp.stack([s[i] for s in states])

def rms_norm(x, g, eps=NORM_EPS):
    xf = x.astype(jnp.float32)
    y = xf * lax.rsqrt(jnp.mean(xf * xf, -1, keepdims=True) + eps)
    return (y * g.astype(jnp.float32)).astype(x.dtype)

def rope(x, pos):
    half = HEAD_DIM // 2
    inv = ROPE_THETA ** (-jnp.arange(half, dtype=jnp.float32) / half)
    ang = pos.astype(jnp.float32)[:, None] * inv
    cos, sin = jnp.cos(ang)[:, None, :], jnp.sin(ang)[:, None, :]
    xf = x.astype(jnp.float32)
    x1, x2 = xf[..., :half], xf[..., half:]
    return jnp.concatenate([x1 * cos - x2 * sin, x1 * sin + x2 * cos], -1).astype(x.dtype)

def masked_softmax(s, mask):
    s = jnp.where(mask, s.astype(jnp.float32), -jnp.inf)
    m = jnp.max(s, -1, keepdims=True)
    e = jnp.exp(s - jnp.where(jnp.isfinite(m), m, 0.0))
    return e / jnp.maximum(jnp.sum(e, -1, keepdims=True), 1e-30)

def mlstm_chunkwise(q, k, v, log_i, log_f, C0, n0, m0):
    B, T, H, D = q.shape
    L = min(MLSTM_CHUNK, T)
    nc = T // L

    def chunks(a):
        return jnp.moveaxis(a.reshape((B, nc, L) + a.shape[2:]), (1, 3), (0, 2))

    causal = jnp.tril(jnp.ones((L, L), bool))

    def step(carry, xs):
        C, n, m = carry
        qc, kc, vc, lic, lfc = xs
        b = jnp.cumsum(lfc, -1)
        log_d = jnp.where(causal, b[..., :, None] - b[..., None, :] + lic[..., None, :], -jnp.inf)
        log_inter = b + m[..., None]
        m_t = jnp.maximum(jnp.max(log_d, -1), log_inter)
        s = jnp.einsum('bhtd,bhsd->bhts', qc, kc) * jnp.exp(log_d - m_t[..., None])
        w_inter = jnp.exp(log_inter - m_t)
        num = jnp.einsum('bhts,bhse->bhte', s, vc) + w_inter[..., None] * jnp.einsum('bhtd,bhde->bhte', qc, C)
        den = jnp.sum(s, -1) + w_inter * jnp.einsum('bhtd,bhd->bht', qc, n)
        h = num / jnp.maximum(jnp.abs(den), jnp.exp(-m_t))[..., None]
        b_end = b[..., -1]
        log_w = b_end[..., None] - b + lic
        m_new = jnp.maximum(b_end + m, jnp.max(log_w, -1))
        wk = jnp.exp(log_w - m_new[..., None])
        decay = jnp.exp(b_end + m - m_new)
        C = decay[..., None, None] * C + jnp.einsum('bhs,bhsd,bhse->bhde', wk, kc, vc)
        n = decay[..., None] * n + jnp.einsum('bhs,bhsd->bhd', wk, kc)
        return (C, n, m_new), h

    xs = tuple(chunks(a) for a in (q * D ** -0.5, k, v, log_i, log_f))
    (C, n, m), hs = lax.scan(step, (C0, n0, m0), xs)
    h = jnp.moveaxis(hs, (0, 2), (1, 3)).reshape(B, T, H, D)
    return h, C, n, m

def mlstm_mixer(p, conv_buf, C0, n0, m0, prm):
    B, T, _ = p.shape
    f32 = jnp.float32
    q, k, v, ig, fg, og, z = _split(p, MLSTM_SIZES)
    ext = jnp.concatenate([conv_buf.astype(p.dtype), jnp.concatenate([q, k], -1)], 1)
    w = prm['mlstm_conv_w']
    qk = jax.nn.silu(prm['mlstm_conv_b'] + sum(ext[:, j:j + T] * w[j] for j in range(MLSTM_CONV)))
    heads = lambda a: a.astype(f32).reshape(B, T, N_HEADS, HEAD_DIM)
    log_i = (ig + prm['mlstm_gate_b'][0]).astype(f32)
    log_f = jax.nn.log_sigmoid((fg + prm['mlstm_gate_b'][1]).astype(f32))
    h, C, n, m = mlstm_chunkwise(heads(qk[..., :GW]), heads(qk[..., GW:]), heads(v), log_i, log_f,
                                 C0.astype(f32), n0.astype(f32), m0.astype(f32))
    h = rms_norm(h, prm['mlstm_norm_g'].reshape(N_HEADS, HEAD_DIM)).reshape(B, T, GW).astype(p.dtype)
    out = jax.nn.sigmoid(og) * h * jax.nn.silu(z)
    return out, C, n, m, ext[:, -(MLSTM_CONV - 1):]

def gather_blocks(blocks, idx, blk0):
    B, Hkv = idx.shape[:2]
    bi = jnp.arange(B)[:, None, None, None, None]
    hi = jnp.arange(Hkv)[None, :, None, None, None]
    j = jnp.clip(idx - blk0, 0, blocks.shape[1] - 1)[..., None]
    return blocks[bi, j, jnp.arange(SLC_BLOCK), hi]

def gather_paged_blocks(cache, l, page_table, idx):
    bpp = PAGE_SIZE // SLC_BLOCK
    B, Hkv = idx.shape[:2]
    idx = jnp.clip(idx, 0, page_table.shape[1] * bpp - 1)
    phys = page_table[jnp.arange(B)[:, None, None, None], idx // bpp]
    tok = (idx % bpp)[..., None] * SLC_BLOCK + jnp.arange(SLC_BLOCK)
    hi = jnp.arange(Hkv)[None, :, None, None, None]
    return cache[l, phys[..., None], tok, hi]

def nsa_compressed(qn, rows, pos, prm):
    B, L = rows.shape[:2]
    R = CMP_BLOCK // CMP_STRIDE
    n_sub = max(-(-L // CMP_STRIDE), R)
    rows = jnp.pad(rows, ((0, 0), (0, n_sub * CMP_STRIDE - L), (0, 0), (0, 0), (0, 0)))
    sub = rows.reshape(B, n_sub, CMP_STRIDE, NSA_KV_HEADS, 2, HEAD_DIM)
    n_cmp = n_sub - R + 1
    w1 = prm['nsa_cmp_w1']
    hid = jnp.einsum('csd,csde->ce', prm['nsa_pe'], w1)[None, None, None]
    for r in range(R):
        hid = hid + jnp.einsum('bnshcd,csde->bnhce', sub[:, r:r + n_cmp],
                               w1[:, r * CMP_STRIDE:(r + 1) * CMP_STRIDE])
    kv = jnp.einsum('bnhce,ced->bnhcd', jax.nn.gelu(hid), prm['nsa_cmp_w2'])
    k_cmp = rms_norm(kv[..., 0, :], prm['nsa_qk_g'][1])
    qg = qn.reshape(B, -1, NSA_KV_HEADS, NSA_GROUP, HEAD_DIM)
    s = jnp.einsum('bthgd,bnhd->bhgtn', qg, k_cmp).astype(jnp.float32) * SCALE
    end = jnp.arange(n_cmp) * CMP_STRIDE + CMP_BLOCK - 1
    pr = masked_softmax(s, end[None, :] <= pos[:, None])
    o = jnp.einsum('bhgtn,bnhd->bthgd', pr, kv[..., 1, :].astype(jnp.float32))
    return o.reshape(qn.shape), pr

def nsa_select(p_cmp, pos, n_slc):
    imp = jnp.sum(p_cmp, 2)
    n_cmp = imp.shape[-1]
    start = jnp.arange(n_cmp)[:, None] * CMP_STRIDE
    blk = jnp.arange(n_slc)
    cover = ((start < (blk + 1) * SLC_BLOCK) & (start + CMP_BLOCK > blk * SLC_BLOCK)).astype(imp.dtype)
    imp = jnp.einsum('bhtn,ns->bhts', imp, cover)
    cur = (pos // SLC_BLOCK)[:, None]
    forced = (blk == 0) | (blk == cur) | (blk == cur - 1)
    imp = jnp.where(forced, jnp.inf, jnp.where(blk <= cur, imp, -jnp.inf))
    top, idx = lax.top_k(imp, min(N_SELECT, n_slc))
    return idx, top > -jnp.inf

def nsa_selected(q_rot, sel_idx, sel_ok, pos, read_blocks):
    B, T = q_rot.shape[:2]
    S = sel_idx.shape[-1]
    QB = min(SLC_Q_BLOCK, T)
    nb = T // QB
    qb = jnp.moveaxis(q_rot.reshape(B, nb, QB, NSA_KV_HEADS, NSA_GROUP, HEAD_DIM), 1, 0)
    ib = jnp.moveaxis(sel_idx.reshape(B, NSA_KV_HEADS, nb, QB, S), 2, 0)
    okb = jnp.moveaxis(sel_ok.reshape(B, NSA_KV_HEADS, nb, QB, S), 2, 0)
    pb = pos.reshape(nb, QB)

    def block(args):
        qc, ic, okc, pc = args
        kv = read_blocks(ic).reshape(B, NSA_KV_HEADS, QB, S * SLC_BLOCK, 2, HEAD_DIM)
        kpos = ic[..., None] * SLC_BLOCK + jnp.arange(SLC_BLOCK)
        mask = (okc[..., None] & (kpos <= pc[:, None, None])).reshape(B, NSA_KV_HEADS, 1, QB, S * SLC_BLOCK)
        s = jnp.einsum('bqhgd,bhqkd->bhgqk', qc, kv[..., 0, :]).astype(jnp.float32) * SCALE
        pr = masked_softmax(s, mask)
        return jnp.einsum('bhgqk,bhqkd->bqhgd', pr, kv[..., 1, :].astype(jnp.float32))

    o = lax.map(block, (qb, ib, okb, pb))
    return jnp.moveaxis(o, 0, 1).reshape(B, T, N_HEADS, HEAD_DIM)

def nsa_window(q_rot, win_ctx, pos0):
    B, T = q_rot.shape[:2]
    QB = min(WIN_Q_BLOCK, T)
    nb = T // QB
    rows = jnp.arange(nb)[:, None] * QB + jnp.arange(WINDOW + QB)
    kv = win_ctx[:, rows]
    qpos = pos0 + jnp.arange(T).reshape(nb, QB)
    kpos = pos0 - WINDOW + rows
    d = qpos[:, :, None] - kpos[:, None, :]
    mask = (d >= 0) & (d < WINDOW) & (kpos[:, None, :] >= 0)
    qg = q_rot.reshape(B, nb, QB, NSA_KV_HEADS, NSA_GROUP, HEAD_DIM)
    s = jnp.einsum('bcqhgd,bckhd->bhgcqk', qg, kv[..., 0, :]).astype(jnp.float32) * SCALE
    pr = masked_softmax(s, mask)
    o = jnp.einsum('bhgcqk,bckhd->bcqhgd', pr, kv[..., 1, :].astype(jnp.float32))
    return o.reshape(B, T, N_HEADS, HEAD_DIM)

def nsa_mixer(p, pos0, win_prefix, prm, past):
    B, T, _ = p.shape
    pos = pos0 + jnp.arange(T, dtype=jnp.int32)
    q, kc, vc, ks, vs, kw, vw, gates, z = _split(p, NSA_SIZES)
    g = prm['nsa_qk_g']
    kvh = lambda a: a.reshape(B, T, NSA_KV_HEADS, HEAD_DIM)
    qn = rms_norm(q.reshape(B, T, N_HEADS, HEAD_DIM), g[0])
    q_rot = rope(qn, pos)
    cmp_new = jnp.stack([kvh(kc), kvh(vc)], 3)
    slc_new = jnp.stack([rope(rms_norm(kvh(ks), g[2]), pos), kvh(vs)], 3)
    win_new = jnp.stack([rope(rms_norm(kvh(kw), g[3]), pos), kvh(vw)], 3)
    n_new_blk = -(-T // SLC_BLOCK)
    new_blocks = jnp.pad(slc_new, ((0, 0), (0, n_new_blk * SLC_BLOCK - T), (0, 0), (0, 0), (0, 0)))
    new_blocks = new_blocks.reshape(B, n_new_blk, SLC_BLOCK, NSA_KV_HEADS, 2, HEAD_DIM)
    blk0 = pos0 // SLC_BLOCK
    if past is None:
        cmp_rows = cmp_new
        read_blocks = lambda idx: gather_blocks(new_blocks, idx, blk0)
    else:
        cache_cmp, cache_slc, page_table, l = past
        past_rows = cache_cmp[l, page_table].reshape(B, pos0, NSA_KV_HEADS, 2, HEAD_DIM)
        cmp_rows = jnp.concatenate([past_rows, cmp_new], 1)

        def read_blocks(idx):
            old = gather_paged_blocks(cache_slc, l, page_table, idx)
            new = gather_blocks(new_blocks, idx, blk0)
            return jnp.where((idx < blk0)[..., None, None, None], old, new)
    o_cmp, p_cmp = nsa_compressed(qn, cmp_rows, pos, prm)
    sel_idx, sel_ok = nsa_select(p_cmp, pos, -(-(pos0 + T) // SLC_BLOCK))
    o_slc = nsa_selected(q_rot, sel_idx, sel_ok, pos, read_blocks)
    pad = WINDOW - win_prefix.shape[1]
    win_ctx = jnp.concatenate([jnp.pad(win_prefix.astype(win_new.dtype), ((0, 0), (pad, 0), (0, 0), (0, 0), (0, 0))),
                               win_new], 1)
    o_win = nsa_window(q_rot, win_ctx, pos0)
    gt = jax.nn.sigmoid(gates.astype(jnp.float32)).reshape(B, T, 3, N_HEADS, 1)
    o = gt[:, :, 0] * o_cmp + gt[:, :, 1] * o_slc + gt[:, :, 2] * o_win
    keep = win_prefix.shape[1] if past is not None else min(WINDOW, T)
    out = o.reshape(B, T, GW).astype(p.dtype) * jax.nn.silu(z)
    return out, cmp_new, slc_new, win_ctx[:, -keep:]

def rwkv7_scan(r, log_w, k, v, kk, a, S0):
    def step(S, xs):
        rt, wt, kt, vt, kkt, at = xs
        S = (S * jnp.exp(wt)[:, :, None, :]
             - jnp.einsum('bhvk,bhk->bhv', S, kkt)[..., None] * (kkt * at)[:, :, None, :]
             + vt[..., None] * kt[:, :, None, :])
        return S, jnp.einsum('bhvk,bhk->bhv', S, rt)
    S, ys = lax.scan(step, S0, tuple(jnp.moveaxis(t, 1, 0) for t in (r, log_w, k, v, kk, a)))
    return jnp.moveaxis(ys, 0, 1), S

def rwkv_mixer(p, shift_buf, S0, prm):
    B, T, _ = p.shape
    f32 = jnp.float32
    u, z = _split(p, RWKV_SIZES)
    prev = jnp.concatenate([shift_buf.astype(u.dtype), u[:, :-1]], 1)
    um = u + (prev - u) * prm['rwkv_mu']
    r, k, v, wl, al = _split(um, (GW, GW, GW, DECAY_LORA, AAA_LORA))
    heads = lambda t: t.astype(f32).reshape(B, T, N_HEADS, HEAD_DIM)
    w_pre = (prm['rwkv_w0'] + jnp.tanh(wl) @ prm['rwkv_w2']).astype(f32)
    log_w = -jnp.exp(-jax.nn.softplus(-w_pre) - 0.5)
    a = jax.nn.sigmoid((prm['rwkv_a0'] + al @ prm['rwkv_a2']).astype(f32))
    k_k, k_a, r_k = prm['rwkv_kk'][0], prm['rwkv_kk'][1], prm['rwkv_kk'][2]
    kk = heads(k.astype(f32) * k_k)
    kk = kk / jnp.maximum(jnp.sqrt(jnp.sum(kk * kk, -1, keepdims=True)), 1e-12)
    k_eff = heads(k.astype(f32) * (1.0 + (a - 1.0) * k_a))
    rh, vh = heads(r), heads(v)
    y, S = rwkv7_scan(rh, heads(log_w), k_eff, vh, kk, heads(a), S0.astype(f32))
    mu = jnp.mean(y, -1, keepdims=True)
    var = jnp.mean(jnp.square(y - mu), -1, keepdims=True)
    ln = prm['rwkv_ln'].reshape(2, N_HEADS, HEAD_DIM)
    y = (y - mu) * lax.rsqrt(var + RWKV_LN_EPS) * ln[0] + ln[1]
    y = y + jnp.sum(rh * k_eff * r_k.reshape(N_HEADS, HEAD_DIM), -1, keepdims=True) * vh
    out = y.reshape(B, T, GW).astype(p.dtype) * jax.nn.silu(z)
    return out, S, u[:, -1:]

def memory_kv(mem, prm):
    B = mem.shape[0]
    h = rms_norm(mem, prm['mem_norm_g'])
    kv = (h @ prm['w_mem_kv']).reshape(B, -1, 2, MEM_HEADS, MEM_HEAD_DIM)
    return jnp.stack([rms_norm(kv[:, :, 0], prm['mem_qk_g'][1]), kv[:, :, 1]], 3)

def memory_mixer(p, mem_kv, prm):
    B, T, _ = p.shape
    q, z = _split(p, MEM_SIZES)
    qn = rms_norm(q.reshape(B, T, MEM_HEADS, MEM_HEAD_DIM), prm['mem_qk_g'][0])
    s = jnp.einsum('bthd,bmhd->bhtm', qn, mem_kv[..., 0, :]).astype(jnp.float32) * MEM_HEAD_DIM ** -0.5
    pr = jax.nn.softmax(s, -1)
    o = jnp.einsum('bhtm,bmhd->bthd', pr, mem_kv[..., 1, :].astype(jnp.float32))
    return o.reshape(B, T, GW).astype(p.dtype) * jax.nn.silu(z)

def layer(x, pos0, st, mem_kv, prm, past):
    conv_buf, C0, n0, m0, S0, shift_buf, win_prefix = st
    h = rms_norm(x, prm['norm_g'])
    p_m, p_n, p_r, p_c = _split(h @ prm['w_in'], GROUP_SIZES)
    y_m, C, n, m, conv_new = mlstm_mixer(p_m, conv_buf, C0, n0, m0, prm)
    y_n, cmp_new, slc_new, win_new = nsa_mixer(p_n, pos0, win_prefix, prm, past)
    y_r, S, shift_new = rwkv_mixer(p_r, shift_buf, S0, prm)
    y_c = memory_mixer(p_c, mem_kv, prm)
    y = jnp.concatenate([y_m, y_n, y_r, y_c], -1) @ prm['w_out']
    return x + y, (cmp_new, slc_new, win_new, C, n, m, conv_new, S, shift_new)

def setup_inputs(seed: int = 0) -> dict:
    key = jax.random.key(seed)
    keys = iter(jax.random.split(key, 48))
    f32 = jnp.float32

    def nrm(shape, scale=1.0):
        return scale * jax.random.normal(next(keys), shape, f32)

    def uni(shape, lo, hi):
        return jax.random.uniform(next(keys), shape, f32, lo, hi)

    n_pages = PAST_LEN // PAGE_SIZE
    n_pool = (5 * DEC_BATCH * n_pages) // 4
    win_buf = min(WINDOW, PAST_LEN)
    perm = jax.random.permutation(next(keys), n_pool).astype(jnp.int32)
    return {
        'x_prompt': nrm((BATCH, SEQ, D_MODEL)),
        'x_sample': nrm((DEC_BATCH, DEC_SEQ, D_MODEL)),
        'cache_cmp_kv': nrm((DEPTH, n_pool, PAGE_SIZE, NSA_KV_HEADS, 2, HEAD_DIM)),
        'cache_slc_kv': nrm((DEPTH, n_pool, PAGE_SIZE, NSA_KV_HEADS, 2, HEAD_DIM)),
        'cache_win_kv': nrm((DEPTH, DEC_BATCH, win_buf, NSA_KV_HEADS, 2, HEAD_DIM)),
        'cache_mem_kv': nrm((DEPTH, DEC_BATCH, N_MEM, MEM_HEADS, 2, MEM_HEAD_DIM)),
        'state_mlstm_C': nrm((DEPTH, DEC_BATCH, N_HEADS, HEAD_DIM, HEAD_DIM), 0.1),
        'state_mlstm_n': jnp.abs(nrm((DEPTH, DEC_BATCH, N_HEADS, HEAD_DIM), 0.5)),
        'state_mlstm_m': nrm((DEPTH, DEC_BATCH, N_HEADS), 0.5),
        'state_mlstm_conv': nrm((DEPTH, DEC_BATCH, MLSTM_CONV - 1, 2 * GW)),
        'state_rwkv_S': nrm((DEPTH, DEC_BATCH, N_HEADS, HEAD_DIM, HEAD_DIM), 0.1),
        'state_rwkv_shift': nrm((DEPTH, DEC_BATCH, 1, RWKV_SHIFT)),
        'page_table': perm[:DEC_BATCH * n_pages].reshape(DEC_BATCH, n_pages),
        'mem_prompt': nrm((BATCH, N_MEM, D_MODEL)),
        'norm_g': 1.0 + nrm((DEPTH, D_MODEL), 0.02),
        'w_in': nrm((DEPTH, D_MODEL, D_IN), D_MODEL ** -0.5),
        'w_out': nrm((DEPTH, D_MODEL, D_MODEL), 0.5 * D_MODEL ** -0.5),
        'mlstm_conv_w': nrm((DEPTH, MLSTM_CONV, 2 * GW), MLSTM_CONV ** -0.5),
        'mlstm_conv_b': nrm((DEPTH, 2 * GW), 0.02),
        'mlstm_gate_b': jnp.concatenate([nrm((DEPTH, 1, N_HEADS), 0.1), uni((DEPTH, 1, N_HEADS), 3.0, 6.0)], 1),
        'mlstm_norm_g': 1.0 + nrm((DEPTH, GW), 0.02),
        'nsa_qk_g': 1.0 + nrm((DEPTH, 4, HEAD_DIM), 0.02),
        'nsa_pe': nrm((DEPTH, 2, CMP_BLOCK, HEAD_DIM), 0.1),
        'nsa_cmp_w1': nrm((DEPTH, 2, CMP_BLOCK, HEAD_DIM, CMP_HIDDEN), (CMP_BLOCK * HEAD_DIM) ** -0.5),
        'nsa_cmp_w2': nrm((DEPTH, 2, CMP_HIDDEN, HEAD_DIM), CMP_HIDDEN ** -0.5),
        'rwkv_mu': uni((DEPTH, RWKV_SHIFT), 0.0, 1.0),
        'rwkv_w0': uni((DEPTH, GW), -5.0, -0.5),
        'rwkv_w2': nrm((DEPTH, DECAY_LORA, GW), 0.5 * DECAY_LORA ** -0.5),
        'rwkv_a0': nrm((DEPTH, GW), 0.1),
        'rwkv_a2': nrm((DEPTH, AAA_LORA, GW), 0.5 * AAA_LORA ** -0.5),
        'rwkv_kk': jnp.concatenate([0.85 + nrm((DEPTH, 1, GW), 0.05), 1.0 + nrm((DEPTH, 1, GW), 0.05),
                                    nrm((DEPTH, 1, GW), 0.1)], 1),
        'rwkv_ln': jnp.concatenate([1.0 + nrm((DEPTH, 1, GW), 0.02), nrm((DEPTH, 1, GW), 0.02)], 1),
        'mem_norm_g': 1.0 + nrm((DEPTH, D_MODEL), 0.02),
        'w_mem_kv': nrm((DEPTH, D_MODEL, 2 * GW), D_MODEL ** -0.5),
        'mem_qk_g': 1.0 + nrm((DEPTH, 2, MEM_HEAD_DIM), 0.02),
    }

def reference(x_prompt, x_sample, cache_cmp_kv, cache_slc_kv, cache_win_kv, cache_mem_kv,
              state_mlstm_C, state_mlstm_n, state_mlstm_m, state_mlstm_conv, state_rwkv_S, state_rwkv_shift,
              page_table, mem_prompt,
              norm_g, w_in, w_out, mlstm_conv_w, mlstm_conv_b, mlstm_gate_b, mlstm_norm_g,
              nsa_qk_g, nsa_pe, nsa_cmp_w1, nsa_cmp_w2,
              rwkv_mu, rwkv_w0, rwkv_w2, rwkv_a0, rwkv_a2, rwkv_kk, rwkv_ln,
              mem_norm_g, w_mem_kv, mem_qk_g):
    f32 = jnp.float32
    B = x_prompt.shape[0]
    past_len = page_table.shape[1] * PAGE_SIZE
    xp, xs = x_prompt, x_sample
    new_p, new_s, new_mem = [], [], []
    for l in range(DEPTH):
        prm = {'norm_g': norm_g[l], 'w_in': w_in[l], 'w_out': w_out[l],
               'mlstm_conv_w': mlstm_conv_w[l], 'mlstm_conv_b': mlstm_conv_b[l],
               'mlstm_gate_b': mlstm_gate_b[l], 'mlstm_norm_g': mlstm_norm_g[l],
               'nsa_qk_g': nsa_qk_g[l], 'nsa_pe': nsa_pe[l], 'nsa_cmp_w1': nsa_cmp_w1[l],
               'nsa_cmp_w2': nsa_cmp_w2[l], 'rwkv_mu': rwkv_mu[l], 'rwkv_w0': rwkv_w0[l],
               'rwkv_w2': rwkv_w2[l], 'rwkv_a0': rwkv_a0[l], 'rwkv_a2': rwkv_a2[l],
               'rwkv_kk': rwkv_kk[l], 'rwkv_ln': rwkv_ln[l], 'mem_norm_g': mem_norm_g[l],
               'w_mem_kv': w_mem_kv[l], 'mem_qk_g': mem_qk_g[l]}
        mem_kv_p = memory_kv(mem_prompt, prm)
        st_p = (jnp.zeros((B, MLSTM_CONV - 1, 2 * GW), xp.dtype),
                jnp.zeros((B, N_HEADS, HEAD_DIM, HEAD_DIM), f32),
                jnp.zeros((B, N_HEADS, HEAD_DIM), f32),
                jnp.full((B, N_HEADS), M_INIT, f32),
                jnp.zeros((B, N_HEADS, HEAD_DIM, HEAD_DIM), f32),
                jnp.zeros((B, 1, RWKV_SHIFT), xp.dtype),
                jnp.zeros((B, 0, NSA_KV_HEADS, 2, HEAD_DIM), xp.dtype))
        xp, sp = layer(xp, 0, st_p, mem_kv_p, prm, None)
        st_s = (state_mlstm_conv[l], state_mlstm_C[l], state_mlstm_n[l], state_mlstm_m[l],
                state_rwkv_S[l], state_rwkv_shift[l], cache_win_kv[l])
        xs, ss = layer(xs, past_len, st_s, cache_mem_kv[l], prm, (cache_cmp_kv, cache_slc_kv, page_table, l))
        new_p.append(sp)
        new_s.append(ss)
        new_mem.append(mem_kv_p)
    return (xp, xs,
            _stack_layers(new_p, 0), _stack_layers(new_s, 0),
            _stack_layers(new_p, 1), _stack_layers(new_s, 1),
            _stack_layers(new_p, 2), _stack_layers(new_s, 2),
            jnp.stack(new_mem),
            _stack_layers(new_p, 3), _stack_layers(new_s, 3),
            _stack_layers(new_p, 4), _stack_layers(new_s, 4),
            _stack_layers(new_p, 5), _stack_layers(new_s, 5),
            _stack_layers(new_p, 6), _stack_layers(new_s, 6),
            _stack_layers(new_p, 7), _stack_layers(new_s, 7),
            _stack_layers(new_p, 8), _stack_layers(new_s, 8))


_drawn_inputs = setup_inputs


def setup_inputs(seed=0):
    import zlib

    import numpy as np

    out = dict(_drawn_inputs(seed))
    spreads = {}
    factors = {'cache_cmp_kv': 5.873,
     'cache_slc_kv': 8.0,
     'mlstm_norm_g': 8.0,
     'nsa_qk_g': 3.985,
     'nsa_pe': 8.0,
     'mem_norm_g': 2.815,
     'mem_qk_g': 3.645}
    for name, (base, spread) in spreads.items():
        noise = np.random.default_rng([zlib.crc32(name.encode()), seed]).standard_normal(out[name].shape)
        drawn = base * np.exp(spread * noise) if base else spread * noise
        out[name] = __import__('jax').numpy.asarray(drawn.astype(out[name].dtype))
    for name, factor in factors.items():
        out[name] = (out[name] * factor).astype(out[name].dtype)
    return out
```

```python
from contextlib import ExitStack

import numpy as np

import concourse.bass as bass
from concourse import mybir

ALU = mybir.AluOpType
ACT = mybir.ActivationFunctionType
F32 = mybir.dt.float32
I32 = mybir.dt.int32
AX = mybir.AxisListType

D = 1024
SEQ = 512
DEPTH = 2
DB, DS = 8, 4
PAST = 2048
PAGE = 128
HD = 64
GW = 256
NH = 4
WIN = 512
NMEM = 256
NPAGE = PAST // PAGE
NPOOL = 5 * DB * NPAGE // 4
CMP_STRIDE, CMP_BLOCK, SLC_BLOCK = 16, 32, 64
NCMP = (PAST - CMP_BLOCK) // CMP_STRIDE + 1
NSUB = PAST // CMP_STRIDE
NSLC = PAST // SLC_BLOCK + 1
PSUBS = SEQ // CMP_STRIDE
PCMP = PSUBS - 1
SCALE = HD ** -0.5
EPS = 1e-6
RW_EPS = HD * 1e-5
DECAY = float(np.exp(-0.5))
NEG = -1e30
DTOK = DB * DS
NT = SEQ + DTOK
TILES = 5
KT = D // 128
CH = 32
NRT = 7
SLOT = 4096
NSLOT = 3

CHUNKS = [("F0", 512), ("T0", 512), ("T1", 264), ("F1", 512), ("F2", 384), ("T2", 256),
          ("T3", 512), ("T4", 512), ("T5", 268), ("T6", 512)]


def rows(i):
    return 128 if i < 4 else DTOK


def tok(i):
    return slice(128 * i, 128 * i + rows(i))


def constants():
    p = np.arange(128)
    t = np.arange(128)
    f = np.float32
    c = {}
    c["idn"] = np.eye(128)
    c["onesbd"] = (p[:, None] // 64 == t[None] // 64)
    c["ones"] = np.ones((128, 128))
    c["caus"] = np.where(t[None] > p[:, None], NEG, 0.0)
    c["tri"] = t[None] >= p[:, None]
    same = p[:, None] // CH == t[None] // CH
    c["nSL"] = -1.0 * (same & (t[None] < p[:, None]))
    c["nSU"] = -1.0 * (same & (t[None] > p[:, None]))
    c["SU"] = same & (t[None] > p[:, None])
    c["IU"] = same & (t[None] >= p[:, None])
    q = np.arange(32)
    samed = (p[:, None] // DS == q[None] // DS) & (p[:, None] < 32)
    c["nSLd"] = -1.0 * (samed & (q[None] < p[:, None]))
    c["nSUd"] = -1.0 * (samed & (q[None] > p[:, None]))
    c["SUd"] = samed & (q[None] > p[:, None])
    c["IUd"] = samed & (q[None] >= p[:, None])
    c["endsel"] = samed & (q[None] % DS == DS - 1)
    c["chD"] = (p[:, None] // DS == np.arange(8)[None]) & (p[:, None] < 32)
    c["IDN2"] = (p[:, None] % 64 == np.arange(64)[None])
    half = HD // 2
    inv = (10000.0 ** (-np.arange(half) / half)).astype(np.float32)
    pos = np.zeros((128, TILES), np.float32)
    for i in range(4):
        pos[:, i] = 128 * i + p
    pos[:32, 4] = PAST + p[:32] % DS
    ang = (pos[:, :, None] * inv.astype(np.float32)).astype(np.float32)
    c["cos"] = np.cos(ang).reshape(128, -1)
    c["sin"] = np.sin(ang).reshape(128, -1)
    n = p[:, None] * CMP_STRIDE
    blk = np.arange(NSLC)[None]
    c["cover"] = (n < (blk + 1) * SLC_BLOCK) & (n + CMP_BLOCK > blk * SLC_BLOCK) & (p[:, None] < NCMP)
    c["expand"] = (p[:, None] == t[None] // 4) & (p[:, None] < NSLC)
    col = np.arange(16)
    tq = col % DS
    s = np.arange(4)
    j = p[:, None] * 4 + s[None]
    c["winb"] = np.where(j[:, :, None] > tq[None, None], 0.0, NEG).reshape(128, -1)
    q = np.arange(128)
    c["newb"] = np.where((p[:, None] // DS == q[None] // 16) & (p[:, None] % DS <= q[None] % DS), 0.0, NEG)
    e = np.arange(32)
    cb = np.zeros((128, 4, 32))
    for i in range(4):
        cb[:, i] = np.where((e[None] < PCMP) & (e[None] * CMP_STRIDE + CMP_BLOCK - 1 <= 128 * i + p[:, None]), 0.0, NEG)
    c["cmpb"] = cb.reshape(128, -1)
    fo = np.zeros((128, NSLC))
    fo[:, 0], fo[:, NSLC - 1], fo[:, NSLC - 2] = 3e30, 2e30, 1e30
    c["forced"] = fo
    m = np.zeros((128, 8))
    m[:, 0], m[:, 1], m[:, 2], m[:, 3] = EPS, 1.0, RW_EPS, 10 * np.log(2.0)
    c["misc"] = m
    offs, parts, o = {}, [], 0
    for k, v in c.items():
        v = np.asarray(v, f)
        offs[k] = (o, v.shape[1])
        parts.append(v)
        o += v.shape[1]
    return np.ascontiguousarray(np.concatenate(parts, 1)), offs


CONST, COFF = constants()

PARAMS = [("g", 8), ("mg", 8), ("cw", 16), ("cb", 4), ("gb", 8), ("mlg", 256), ("qkg", 512), ("kcg", 1),
          ("mqg", 64), ("mkg", 64), ("mu", 7), ("w0", 2), ("a0", 2), ("kk", 2), ("ka", 2), ("rk", 2),
          ("ln0", 256), ("ln1", 256), ("lora", 256), ("w2", 128), ("pe", 32), ("w1p", 2048)]
POFF = {}
_o = 0
for _n, _w in PARAMS:
    POFF[_n] = (_o, _w)
    _o += _w
NPRM = _o

OUTS = {
    "y": (128, TILES, D), "cmp": (DEPTH, 128, TILES, 256), "slc": (DEPTH, 128, TILES, 256),
    "win": (DEPTH, 128, TILES, 256), "winpast": (DEPTH, DB, WIN - DS, 256), "mem": (DEPTH, 128, 2, 512),
    "mC": (DEPTH, 128, 2, 65), "mCd": (DEPTH, 128, 2, 8, 64), "mnd": (DEPTH, 128, 2, 8), "mm": (DEPTH, 128, TILES, NH),
    "mconv": (DEPTH, 128, 4, 9, 3), "rS": (DEPTH, 128, 9, 128), "rsh": (DEPTH, 128, NRT, 9),
}
INS = ["const", "prm", "x", "memx", "wmem", "win_", "wout", "w1f", "ptab", "cmpL", "slcK", "slcV", "wmL", "winraw",
       "mC0", "mn0", "mm0", "mconv0", "rS0", "rsh0"]


class Line:

    def __init__(self, plan, eng, key, chained=True):
        self.plan, self.eng, self.key, self.chained = plan, eng, key, chained
        self.n = 0
        self.seen = {}
        self.done = plan.sems.get(key)

    def wait_ge(self, sem, value):
        if not self.plan.counting and self.seen.get(id(sem), 0) < value:
            self.seen[id(sem)] = value
            self.eng.wait_ge(sem, value)

    def __call__(self, ins, *name):
        self.n += 1
        if self.chained:
            self.wait_ge(self.done, self.n)
        if name:
            self.plan.at[name] = (self.key, self.n)
        return ins

    def name(self, *name):
        self.plan.at[name] = (self.key, self.n)

    def dma(self, sem, ins, *name):
        self.plan.dmas[sem] = self.plan.dmas.get(sem, 0) + 16
        if name:
            self.plan.at[name] = (sem, self.plan.dmas[sem])

    def fence(self, ins):
        self(ins)
        self.wait_ge(self.done, self.n)

    def open(self, *key):
        p = self.plan
        k = len(p.opened)
        p.opened.append(key)
        if k >= 8 and not p.counting:
            key8, value = p.at[("free", *p.opened[k - 8])]
            self.wait_ge(p.sems[key8], value)
        p.bank[key] = k % 8
        return p.banks[k % 8]

    def full(self, ins, *key):
        self(ins, "full", *key)

    def free(self, *key):
        self.name("free", *key)


class Plan:
    def __init__(self):
        self.at, self.bank = {}, {}
        self.counting = True
        self.reset()

    def reset(self):
        self.opened, self.dmas, self.sems, self.banks = [], {}, {}, []


def build(nc, io, plan, debug=None):
    ctx = ExitStack()
    with ctx:
        def sb(name, n, dt=F32):
            return ctx.enter_context(nc.sbuf_tensor(name, [128, n], dt))

        cst = sb("cst", CONST.shape[1])
        prm = sb("prm", NPRM)
        X = sb("X", TILES * D)[:, :].rearrange("p (i c) -> p i c", i=TILES)
        hT = sb("hT", KT * NT)[:, :].rearrange("p (k t) -> p k t", k=KT)
        YT = sb("YT", KT * NT)[:, :].rearrange("p (k t) -> p k t", k=KT)
        stream = sb("stream", NSLOT * SLOT)
        MKV = sb("MKV", 2 * 512)[:, :].rearrange("p (i c) -> p i c", i=2)
        MKT = sb("MKT", 2 * 256)[:, :].rearrange("p (i c) -> p i c", i=2)
        ptab = ctx.enter_context(nc.sbuf_tensor("ptab", [1, DB * NPAGE], I32))
        AREA = 19264
        area = sb("area", AREA)
        plan.reset()
        plan.banks = [ctx.enter_context(nc.psum_tensor(f"bank{i}", [128, 512], F32)) for i in range(8)]
        names = ["pe", "dve", "act", "pool", "const", "x", "prm0", "prm1", "memx0", "memx1", "ptab",
                 "st_end"] + [f"slot{i}" for i in range(NSLOT)]
        names += [f"{a}{g}{l}" for a in ("st", "ld") for g in "EMRN" for l in range(DEPTH)]
        for n in names:
            plan.sems[n] = ctx.enter_context(nc.semaphore("s_" + n))

        pe_done, dve_done, act_done, pool_done = (plan.sems[n] for n in ("pe", "dve", "act", "pool"))
        done = {n: plan.sems[n] for n in ("pe", "dve", "act", "pool")}
        const_in, ptab_in, x_in, y_stored = (plan.sems[n] for n in ("const", "ptab", "x", "st_end"))
        prm_in, memx_in = ([plan.sems[f"{n}{l}"] for l in range(DEPTH)] for n in ("prm", "memx"))
        slot_in = [plan.sems[f"slot{i}"] for i in range(NSLOT)]
        stored, loaded = ({g: [plan.sems[f"{n}{g}{l}"] for l in range(DEPTH)] for g in "EMRN"} for n in ("st", "ld"))

        def at(*name):
            return 0 if plan.counting else plan.at[name][1]

        def bank(*key):
            return plan.banks[plan.bank.get(key, 0)]

        def sem_of_slot(*item):
            return slot_in[slot_of[item]]

        def C(name, r=128):
            o, w = COFF[name]
            return cst[0:r, o:o + w]

        def Q(name):
            o, w = POFF[name]
            return prm[:, o:o + w]

        def bc(ap, axis, n):
            ap = ap.unsqueeze(axis)
            shape = list(ap.shape)
            shape[axis] = n
            return ap.broadcast_to(shape)

        class Carve:

            def __init__(self):
                self.o = 0

            def __call__(self, n):
                a = area[:, self.o:self.o + n]
                self.o += n
                assert self.o <= AREA, self.o
                return a

        eps, one_c, rweps, ln2_10 = (C("misc")[:, i:i + 1] for i in range(4))
        idn = C("idn")

        def selh(h, n):
            return idn[0:4, h:h + 1].broadcast_to([4, n])

        items = []
        for l in range(DEPTH):
            items += [("wmem", l)] + [("w", l, n) for n, _ in CHUNKS[:6]]
            items += [("w", l, n) for n, _ in CHUNKS[6:8]] + [("w1f", l)] + [("cmp", l, b) for b in range(DB)]
            items += [("w", l, n) for n, _ in CHUNKS[8:]]
            for b in range(DB):
                items += [("slc", l, b), ("wm", l, b)]
            items += [("wout", l, 0), ("wout", l, 1)]
        slot_of = {it: k % NSLOT for k, it in enumerate(items)}
        coff = {}
        o = 0
        for n, w in CHUNKS:
            coff[n] = (o, w)
            o += w

        def slot(*item):
            s = slot_of[item]
            return stream[:, s * SLOT:(s + 1) * SLOT]

        def sync_stream(sp):
            for k, it in enumerate(items):
                if k >= NSLOT:
                    sp.wait_ge(pe_done, at("used", *items[k - NSLOT]))
                s, sem, l = slot(*it), f"slot{k % NSLOT}", it[1]
                nm = ("here",) + it
                if it[0] == "wmem":
                    sp.dma(sem, sp.eng.dma_start(s, io["wmem"][l]).then_inc(slot_in[k % NSLOT], 16), *nm)
                elif it[0] == "w":
                    o, w = coff[it[2]]
                    sp.dma(sem, sp.eng.dma_start(s[:, 0:KT * w], io["win_"][l, :, KT * o:KT * (o + w)]).then_inc(slot_in[k % NSLOT], 16), *nm)
                elif it[0] == "w1f":
                    sp.dma(sem, sp.eng.dma_start(s, io["w1f"][l]).then_inc(slot_in[k % NSLOT], 16), *nm)
                elif it[0] == "wout":
                    sp.dma(sem, sp.eng.dma_start(s, io["wout"][l, it[2]]).then_inc(slot_in[k % NSLOT], 16), *nm)
                elif it[0] == "wm":
                    sp.dma(sem, sp.eng.dma_start(s[:, 0:2048], io["wmL"][l, it[2]]).then_inc(slot_in[k % NSLOT], 16), *nm)
                else:
                    if k == items.index(("cmp", 0, 0)):
                        sp.wait_ge(ptab_in, at("ptab"))
                    b = it[2]
                    for pg in range(NPAGE):
                        j = b * NPAGE + pg
                        page = sp.eng.value_load(ptab[0:1, j:j + 1], min_val=0, max_val=NPOOL - 1)
                        if it[0] == "cmp":
                            sp.dma(sem, sp.eng.dma_start(s[:, pg * 256:(pg + 1) * 256], io["cmpL"][l, bass.DynSlice(page, 1)].rearrange("a p c -> (a p) c")).then_inc(slot_in[k % NSLOT], 16), *nm)
                        else:
                            sp.dma(sem, sp.eng.dma_start(s[:, pg * 128:(pg + 1) * 128], io["slcK"][l, bass.DynSlice(page, 1)].rearrange("a p c -> (a p) c")).then_inc(slot_in[k % NSLOT], 16), *nm)
                            sp.dma(sem, sp.eng.dma_start(s[8 * pg:8 * pg + 8, 2048:4096], io["slcV"][l, bass.DynSlice(page, 1)].rearrange("a p c -> (a p) c")).then_inc(slot_in[k % NSLOT], 16), *nm)

        cv = Carve()
        E = {"junk": cv(1024), "xn": [cv(1024), cv(1024)], "memx": cv(2048).rearrange("p (i c) -> p i c", i=2),
             "hm": cv(2048).rearrange("p (k t) -> p k t", k=KT), "ss": cv(8), "rs": cv(8), "kj": cv(512), "ks": cv(8), "kr": cv(8)}

        def src_tile(l, i):
            return X[:, i, :] if i < TILES else E["memx"][:, i - TILES, :]

        def act_norm(act, l):
            act.wait_ge(const_in, at("const"))
            for i in range(7):
                if i == 0:
                    act.wait_ge(dve_done if l else x_in, at("x", l))
                if i == TILES:
                    act.wait_ge(memx_in[l], at("memx", l))
                act(nc.scalar.activation(E["junk"], src_tile(l, i), ACT.Square, accum_out=E["ss"][:, i:i + 1]).then_inc(act_done, 1))
            act(nc.scalar.activation(E["rs"][:, 0:7], E["ss"][:, 0:7], ACT.Ln, bias=eps, scale=1.0 / D).then_inc(act_done, 1))
            act(nc.scalar.activation(E["rs"][:, 0:7], E["rs"][:, 0:7], ACT.Exp, scale=-0.5).then_inc(act_done, 1), "rstd", l)

        def dve_norm(dve, l):
            dve.wait_ge(act_done, at("rstd", l))
            dve.wait_ge(prm_in[l], at("prm", l))
            for i in range(7):
                n = rows(i) if i < TILES else 128
                if i >= 2:
                    dve.wait_ge(pe_done, at("xnT", l, i - 2))
                dve(nc.vector.tensor_scalar(E["xn"][i % 2], src_tile(l, i), E["rs"][:, i:i + 1], None, ALU.mult).then_inc(dve_done, 1), "xn", l, i)
                for hf in range(2):
                    dve.wait_ge(pe_done, at("full", "xt", l, i, hf))
                    ps = bank("xt", l, i, hf)
                    g = Q("g" if i < TILES else "mg")[:, 4 * hf:4 * hf + 4]
                    dst = hT[:, 4 * hf:4 * hf + 4, tok(i)] if i < TILES else \
                        E["hm"][:, 4 * hf:4 * hf + 4, 128 * (i - TILES):128 * (i - TILES) + 128]
                    dve(nc.vector.tensor_tensor(dst, ps[:, 0:4 * n].rearrange("p (k t) -> p k t", k=4), bc(g, 2, n), ALU.mult).then_inc(dve_done, 1),
                      "hT", l, i, hf)
                    dve.free("xt", l, i, hf)

        def pe_norm(pe, l):
            pe.wait_ge(const_in, at("const"))
            for i in range(7):
                n = rows(i) if i < TILES else 128
                pe.wait_ge(dve_done, at("xn", l, i))
                for hf in range(2):
                    ps = pe.open("xt", l, i, hf)
                    for k in range(4):
                        kk = 4 * hf + k
                        last = nc.tensor.transpose(ps[:, k * n:(k + 1) * n], E["xn"][i % 2][0:n, 128 * kk:128 * kk + 128], idn[0:n, 0:n])
                    pe.full(last.then_inc(pe_done, 1), "xt", l, i, hf)
                pe.name("xnT", l, i)

        def pe_memkv(pe, l):
            pe.wait_ge(dve_done, at("hT", l, 6, 1))
            pe.wait_ge(sem_of_slot("wmem", l), at("here", "wmem", l))
            w = slot("wmem", l).rearrange("p (k c) -> p k c", k=KT)
            for i in range(2):
                ps = pe.open("mk", l, i)
                for k in range(KT):
                    last = nc.tensor.matmul(ps[:, :], E["hm"][:, k, 128 * i:128 * i + 128], w[:, k, :], start=(k == 0), stop=(k == KT - 1))
                pe.full(last.then_inc(pe_done, 1), "mk", l, i)
            pe.name("used", "wmem", l)
            pe.wait_ge(dve_done, at("mkn", l))
            ps = pe.open("mkt", l)
            for i in range(2):
                for pr in range(2):
                    last = nc.tensor.transpose(ps[:, pr * 256 + 128 * i:pr * 256 + 128 * i + 128], MKV[:, i, 128 * pr:128 * pr + 128], idn)
            pe.full(last.then_inc(pe_done, 1), "mkt", l)
            phase_end(pe, "E", l)

        def dve_memkv(dve, l):
            for i in range(2):
                dve.wait_ge(pe_done, at("full", "mk", l, i))
                ps = bank("mk", l, i)
                dve(nc.vector.tensor_copy(MKV[:, i, :], ps[:, :]).then_inc(dve_done, 1))
                dve.free("mk", l, i)
            k = MKV[:, :, 0:256].rearrange("p i (h d) -> p i h d", d=HD)
            kj = E["kj"].rearrange("p (i h d) -> p i h d", i=2, d=HD)
            dve(nc.vector.tensor_tensor(kj, k, k, ALU.mult).then_inc(dve_done, 1))
            dve(nc.vector.reduce_sum(E["ks"], E["kj"].rearrange("p (j d) -> p j d", d=HD), axis=AX.X).then_inc(dve_done, 1), "mks", l)
            dve.wait_ge(act_done, at("mkr", l))
            dve(nc.vector.tensor_tensor(k, k, bc(E["kr"].rearrange("p (i h) -> p i h", i=2), 3, HD), ALU.mult).then_inc(dve_done, 1))
            dve(nc.vector.tensor_tensor(k, k, bc(bc(Q("mkg"), 1, NH), 1, 2), ALU.mult).then_inc(dve_done, 1), "mkn", l)
            dve.wait_ge(pe_done, at("full", "mkt", l))
            ps = bank("mkt", l)
            dve(nc.vector.tensor_copy(MKT, ps[:, :].rearrange("p (i c) -> p i c", i=2)).then_inc(dve_done, 1), "MKT", l)
            dve.free("mkt", l)

        def act_memkv(act, l):
            act.wait_ge(dve_done, at("mks", l))
            act(nc.scalar.activation(E["kr"], E["ks"], ACT.Ln, bias=eps, scale=1.0 / HD).then_inc(act_done, 1))
            act(nc.scalar.activation(E["kr"], E["kr"], ACT.Exp, scale=-0.5).then_inc(act_done, 1), "mkr", l)

        def pe_project_tm(pe, l, name):
            pe.wait_ge(dve_done, at("hT", l, 4, 1))
            pe.wait_ge(sem_of_slot("w", l, name), at("here", "w", l, name))
            w = coff[name][1]
            ws = slot("w", l, name)[:, 0:KT * w].rearrange("p (k c) -> p k c", k=KT)
            for i in range(TILES):
                ps = pe.open(name, l, i)
                for k in range(KT):
                    last = nc.tensor.matmul(ps[0:rows(i), 0:w], hT[:, k, tok(i)], ws[:, k, :], start=(k == 0), stop=(k == KT - 1))
                pe.full(last.then_inc(pe_done, 1), name, l, i)
            pe.name("used", "w", l, name)

        def take_project_tm(L, l, name, dst, copy):
            w = coff[name][1]
            for i in range(TILES):
                L.wait_ge(pe_done, at("full", name, l, i))
                ps = bank(name, l, i)
                L(copy(dst[0:rows(i), i, 0:w], ps[0:rows(i), 0:w]).then_inc(L.done, 1))
                L.free(name, l, i)
            L.name("P" + name, l)

        def pe_project_fm(pe, l, name):
            pe.wait_ge(dve_done, at("hT", l, 4, 1))
            pe.wait_ge(sem_of_slot("w", l, name), at("here", "w", l, name))
            w = coff[name][1]
            ws = slot("w", l, name)[:, 0:KT * w].rearrange("p (k c) -> p k c", k=KT)
            nf = w // 128
            for f in range(nf):
                ps = pe.open(name, l, f)
                for k in range(KT):
                    last = nc.tensor.matmul(ps[:, :], ws[:, k, 128 * f:128 * f + 128], hT[:, k, 0:SEQ], start=(k == 0), stop=(k == KT - 1))
                pe.full(last.then_inc(pe_done, 1), name, l, f)
            ps = pe.open(name, l, "d")
            for f in range(nf):
                for k in range(KT):
                    last = nc.tensor.matmul(ps[:, DTOK * f:DTOK * f + DTOK], ws[:, k, 128 * f:128 * f + 128], hT[:, k, SEQ:NT],
                                            start=(k == 0), stop=(k == KT - 1))
            pe.full(last.then_inc(pe_done, 1), name, l, "d")
            pe.name("used", "w", l, name)

        def pe_yT(pe, l, src, t0):
            pe.wait_ge(dve_done, at("y", l, t0))
            for f in range(2):
                ps = pe.open("yt", l, t0 + f, 0)
                for i in range(4):
                    last = nc.tensor.transpose(ps[:, tok(i)], src[:, i, 128 * f:128 * f + 128], idn)
                pe.full(last.then_inc(pe_done, 1), "yt", l, t0 + f, 0)
            ps = pe.open("yt", l, t0, 1)
            for f in range(2):
                last = nc.tensor.transpose(ps[:, DTOK * f:DTOK * f + DTOK], src[0:DTOK, 4, 128 * f:128 * f + 128], idn[0:DTOK, 0:DTOK])
            pe.full(last.then_inc(pe_done, 1), "yt", l, t0, 1)

        def dve_yT(dve, l, t0):
            for f in range(2):
                dve.wait_ge(pe_done, at("full", "yt", l, t0 + f, 0))
                ps = bank("yt", l, t0 + f, 0)
                dve(nc.vector.tensor_copy(YT[:, t0 + f, 0:SEQ], ps[:, :]).then_inc(dve_done, 1))
                dve.free("yt", l, t0 + f, 0)
            dve.wait_ge(pe_done, at("full", "yt", l, t0, 1))
            ps = bank("yt", l, t0, 1)
            dve(nc.vector.tensor_copy(YT[:, t0:t0 + 2, SEQ:NT], ps[:, 0:2 * DTOK].rearrange("p (f t) -> p f t", f=2)).then_inc(dve_done, 1), "YT", l, t0)
            dve.free("yt", l, t0, 1)

        def barrier(L, prev):
            for who in ("pe", "dve", "act", "pool"):
                if (who, *prev) in plan.at:
                    L.wait_ge(done[who], at(who, *prev))

        def phase_end(L, *ph):
            L.name(L.key, *ph)

        cv = Carve()
        XE = cv(4 * 515).rearrange("p (f t) -> p f t", f=4)
        XD = cv(4 * 56).rearrange("p (f b t) -> p f b t", f=4, b=DB)
        QK = cv(4 * NT).rearrange("p (f t) -> p f t", f=4)
        PM = cv(TILES * 776).rearrange("p (i c) -> p i c", i=TILES)
        Ktok = cv(TILES * 256).rearrange("p (i c) -> p i c", i=TILES)
        VX = cv(TILES * 260).rearrange("p (i h e) -> p i h e", i=TILES, h=NH)
        EJ = [cv(1280), cv(1280)]
        EOFF = [0, 512, 896, 1152]
        KW = cv(1024).rearrange("p (j c) -> p j c", j=4)
        HH = cv(TILES * 256).rearrange("p (i c) -> p i c", i=TILES)
        HSQ = EJ[0]
        gx, gax, LF, LI, Bt, AA, Mt, EM, DEN, hss, hrs = (cv(20).rearrange("p (i h) -> p i h", i=TILES) for _ in range(11))
        R = [cv(768), cv(768)]
        RD = cv(40).rearrange("p (b t) -> p b t", b=8)
        MDc, WIr, = (cv(32).rearrange("p (b t) -> p b t", b=8) for _ in range(2))
        WIt, WKD, dtmp = cv(4), cv(4), cv(4)
        ED, EDt = (EJ[1][:, o:o + 128].rearrange("p (h t) -> p h t", h=4) for o in (768, 896))
        KWD = EJ[1][:, 512:768].rearrange("p (h d) -> p h d", h=4)
        QCs = cv(64)
        QNp = cv(64).rearrange("p (f b t) -> p f b t", f=2, b=8)
        VXe = EJ[1][:, 0:512].rearrange("p (b e) -> p b e", b=8)
        C0 = cv(1024).rearrange("p (f b e) -> p f b e", f=2, b=8)
        n0, Nn, DCs = (cv(16).rearrange("p (f b) -> p f b", f=2) for _ in range(3))
        CP = cv(130).rearrange("p (f e) -> p f e", f=2)
        m0 = cv(8)
        CI = cv(96).rearrange("p (f b t) -> p f b t", f=4, b=8)
        CS = cv(108).rearrange("p (f b t) -> p f b t", f=4, b=9)

        def pool_m(pool, l):
            barrier(pool, ("E", l))
            pool.dma(f"stE{l}", pool.eng.dma_start(io["mem"][l], MKV).then_inc(stored["E"][l], 16), "stE", l)
            pool.dma(f"ldM{l}", pool.eng.dma_start(CI, io["mconv0"][l]).then_inc(loaded["M"][l], 16))
            pool.dma(f"ldM{l}", pool.eng.dma_start(C0, io["mC0"][l]).then_inc(loaded["M"][l], 16))
            pool.dma(f"ldM{l}", pool.eng.dma_start(n0, io["mn0"][l]).then_inc(loaded["M"][l], 16))
            pool.dma(f"ldM{l}", pool.eng.dma_start(m0[0:4], io["mm0"][l]).then_inc(loaded["M"][l], 16), "ldM", l)
            pool.wait_ge(dve_done, at("CS", l))
            pool.dma(f"stM{l}", pool.eng.dma_start(io["mconv"][l], CS).then_inc(stored["M"][l], 16))
            pool.wait_ge(dve_done, at("CP", l))
            pool.dma(f"stM{l}", pool.eng.dma_start(io["mC"][l], CP).then_inc(stored["M"][l], 16))
            pool.dma(f"stM{l}", pool.eng.dma_start(io["mm"][l], Mt).then_inc(stored["M"][l], 16))
            pool.wait_ge(dve_done, at("Cn", l))
            pool.dma(f"stM{l}", pool.eng.dma_start(io["mCd"][l], C0).then_inc(stored["M"][l], 16))
            pool.dma(f"stM{l}", pool.eng.dma_start(io["mnd"][l], Nn).then_inc(stored["M"][l], 16), "stM", l)

        def pe_m(pe, l):
            pe_project_fm(pe, l, "F0")
            pe_project_tm(pe, l, "T0")
            pe_project_tm(pe, l, "T1")
            pe.wait_ge(dve_done, at("LF", l))
            ps = pe.open("cb", l)
            nc.tensor.matmul(ps[0:32, 16:20], C("IUd", 32), LF[0:32, 4, :], start=True, stop=True)
            nc.tensor.matmul(ps[:, 0:16], C("tri"), LF[:, 0:4, :], start=True, stop=False)
            for j in range(3):
                last = nc.tensor.matmul(ps[:, 4 * (j + 1):16], C("ones"), bc(LF[:, j, :], 1, 3 - j), start=False, stop=(j == 2))
            pe.full(last.then_inc(pe_done, 1), "cb", l)
            pe.wait_ge(dve_done, at("AA", l))
            ps = pe.open("at", l)
            for i in range(4):
                last = nc.tensor.transpose(ps[0:4, tok(i)], AA[:, i, :], idn)
            pe.full(last.then_inc(pe_done, 1), "at", l)
            ps = pe.open("ad", l)
            pe.full(nc.tensor.transpose(ps[0:4, 0:32], AA[0:32, 4, :], idn[0:32, 0:32]).then_inc(pe_done, 1), "ad", l)
            pe.wait_ge(dve_done, at("qk", l))
            for f in range(2):
                ps = pe.open("kt", l, f)
                for i in range(4):
                    last = nc.tensor.transpose(ps[:, tok(i)], QK[:, 2 + f, tok(i)], idn)
                pe.full(last.then_inc(pe_done, 1), "kt", l, f)
            ps = pe.open("kt", l, 2)
            for f in range(2):
                last = nc.tensor.transpose(ps[0:32, 128 * f:128 * f + 128], QK[:, 2 + f, SEQ:NT], idn)
            pe.full(last.then_inc(pe_done, 1), "kt", l, 2)
            pe.wait_ge(loaded["M"][l], at("ldM", l))
            pe.wait_ge(dve_done, at("QNp", l))
            ps = pe.open("qc", l)
            for h in range(NH):
                hh, hp = h % 2, h // 2
                for b in range(DB):
                    o = 32 * hp + 4 * b
                    last = nc.tensor.matmul(ps[64 * hh:64 * hh + 64, o:o + 4], C0[64 * hh:64 * hh + 64, hp, b, :],
                                            QK[64 * hh:64 * hh + 64, hp, SEQ + 4 * b:SEQ + 4 * b + 4], start=True, stop=True)
            pe.full(last.then_inc(pe_done, 1), "qc", l)
            ps = pe.open("qn", l)
            for hp in range(2):
                last = nc.tensor.matmul(ps[0:32, 2 * hp:2 * hp + 2], QNp[:, hp, :, :], C("onesbd")[:, 0:128:64], start=True, stop=True)
            pe.full(last.then_inc(pe_done, 1), "qn", l)
            pe.wait_ge(dve_done, at("QCs", l))
            ps = pe.open("qct", l)
            for hp in range(2):
                last = nc.tensor.transpose(ps[0:32, 128 * hp:128 * hp + 128], QCs[:, 32 * hp:32 * hp + 32], idn)
            pe.full(last.then_inc(pe_done, 1), "qct", l)
            pe.wait_ge(dve_done, at("Mrow", l))
            pe.wait_ge(act_done, at("WIr", l))
            ps = pe.open("mt", l)
            for i in range(4):
                nc.tensor.transpose(ps[:, 4 * i:4 * i + 4], R[1][0:4, 256 + 128 * i:384 + 128 * i], idn[0:4, 0:4])
            nc.tensor.transpose(ps[0:32, 16:20], MDc[0:4], idn[0:4, 0:4])
            pe.full(nc.tensor.transpose(ps[0:32, 20:24], WIr[0:4], idn[0:4, 0:4]).then_inc(pe_done, 1), "mt", l)
            ps = pe.open("md", l)
            for h in range(NH):
                last = nc.tensor.matmul(ps[0:32, 32 * h:32 * h + 32], selh(h, 32), MDc[0:4], start=True, stop=True)
            pe.full(last.then_inc(pe_done, 1), "md", l)
            ps = pe.open("sd", l)
            for h in (0, 2, 1, 3):
                hs = slice(64 * (h % 2), 64 * (h % 2) + 64)
                if h == 1:
                    pe.fence(last.then_inc(pe_done, 1))
                last = nc.tensor.matmul(ps[0:32, 32 * h:32 * h + 32], QK[hs, 2 + h // 2, SEQ:NT], QK[hs, h // 2, SEQ:NT], start=True, stop=True)
            pe.full(last.then_inc(pe_done, 1), "sd", l)
            ps = pe.open("dc", l)
            for h in range(NH):
                hs = slice(64 * (h % 2), 64 * (h % 2) + 64)
                last = nc.tensor.matmul(ps[hs, 8 * (h // 2):8 * (h // 2) + 8], selh(h, 64), WIr[0:4, :, 3], start=True, stop=True)
            pe.full(last.then_inc(pe_done, 1), "dc", l)
            pe.wait_ge(dve_done, at("ED", l))
            ps = pe.open("pd", l)
            for h in range(NH):
                last = nc.tensor.matmul(ps[0:32, 65 * h:65 * h + 65], ED[0:32, h, :], VX[0:32, 4, h, :], start=True, stop=True)
            pe.full(last.then_inc(pe_done, 1), "pd", l)
            ps = pe.open("nu", l)
            for h in range(NH):
                hs = slice(64 * (h % 2), 64 * (h % 2) + 64)
                last = nc.tensor.matmul(ps[hs, 8 * (h // 2):8 * (h // 2) + 8], KWD[0:32, h, :], C("chD", 32), start=True, stop=True)
            pe.full(last.then_inc(pe_done, 1), "nu", l)
            for h in range(NH):
                hs = slice(64 * (h % 2), 64 * (h % 2) + 64)
                pe.wait_ge(dve_done, at("VXe", l, h))
                if h % 2 == 0:
                    ps = pe.open("cu", l, h // 2)
                last = nc.tensor.matmul(ps[hs, :], KWD[0:32, h, :], VXe[0:32], start=True, stop=True)
                pe(last.then_inc(pe_done, 1), "cuh", l, h)
                if h % 2:
                    pe.name("full", "cu", l, h // 2)
            cf = None
            for h in range(NH):
                hs = slice(64 * (h % 2), 64 * (h % 2) + 64)
                ps = pe.open("mb", l, h)
                pe.full(nc.tensor.matmul(ps[:, :], selh(h, 128), R[1][0:4, 256:768], start=True, stop=True).then_inc(pe_done, 1), "mb", l, h)
                for j in range(4):
                    ps = pe.open("st", l, h, j)
                    pe.full(nc.tensor.matmul(ps[:, 0:512 - 128 * j], QK[hs, 2 + h // 2, tok(j)], QK[hs, h // 2, 128 * j:SEQ], start=True, stop=True).then_inc(pe_done, 1),
                           "st", l, h, j)
                pe.wait_ge(dve_done, at("PJ", l, h))
                ps = pe.open("pv", l, h)
                for i in range(4):
                    for j in range(i + 1):
                        o = EOFF[j] + 128 * (i - j)
                        last = nc.tensor.matmul(ps[:, 65 * i:65 * i + 65], EJ[h % 2][:, o:o + 128], VX[:, j, h, :], start=(j == 0), stop=(j == i))
                pe.full(last.then_inc(pe_done, 1), "pv", l, h)
            ps = pe.open("cf", l)
            for h in range(NH):
                hs = slice(64 * (h % 2), 64 * (h % 2) + 64)
                for j in range(4):
                    last = nc.tensor.matmul(ps[hs, 65 * (h // 2):65 * (h // 2) + 65], KW[:, j, 64 * h:64 * h + 64], VX[:, j, h, :],
                                            start=(j == 0), stop=(j == 3))
            pe.full(last.then_inc(pe_done, 1), "cf", l)
            pe_yT(pe, l, PM[:, :, 512:768], 0)
            phase_end(pe, "M", l)

        def act_m(act, l):
            barrier(act, ("E", l))
            take_project_tm(act, l, "T0", PM[:, :, 0:512], nc.scalar.copy)
            take_project_tm(act, l, "T1", PM[:, :, 512:776], nc.scalar.copy)
            act.wait_ge(dve_done, at("gax", l))
            act(nc.scalar.activation(gax, gax, ACT.Exp, scale=-1.0).then_inc(act_done, 1))
            act(nc.scalar.activation(gax, gax, ACT.Ln, bias=one_c).then_inc(act_done, 1), "gln", l)
            act.wait_ge(dve_done, at("mtails", l))
            act.wait_ge(dve_done, at("conv", l))
            act(nc.scalar.activation(QK[:, :, :], QK[:, :, :], ACT.Silu).then_inc(act_done, 1), "silu", l)
            act(nc.scalar.activation(PM[:, :, 512:768], PM[:, :, 512:768], ACT.Silu).then_inc(act_done, 1))
            act(nc.scalar.activation(PM[:, :, 256:512], PM[:, :, 256:512], ACT.Tanh, scale=0.5).then_inc(act_done, 1), "ogz", l)
            act.wait_ge(dve_done, at("WIx", l))
            act(nc.scalar.activation(WIr[0:4], WIr[0:4], ACT.Exp).then_inc(act_done, 1), "WIr", l)
            act.wait_ge(dve_done, at("Mt", l))
            act(nc.scalar.activation(EM, Mt, ACT.Exp, scale=-1.0).then_inc(act_done, 1), "EM", l)
            act.wait_ge(dve_done, at("EDx", l))
            act(nc.scalar.activation(ED[0:32], ED[0:32], ACT.Exp, scale=-1.0).then_inc(act_done, 1), "EDe", l)
            for h in range(NH):
                act.wait_ge(dve_done, at("EJx", l, h))
                act(nc.scalar.activation(EJ[h % 2], EJ[h % 2], ACT.Exp, scale=-1.0).then_inc(act_done, 1), "EJe", l, h)
            act.wait_ge(dve_done, at("hss", l))
            act(nc.scalar.activation(hrs, hss, ACT.Ln, bias=eps, scale=1.0 / HD).then_inc(act_done, 1))
            act(nc.scalar.activation(hrs, hrs, ACT.Exp, scale=-0.5).then_inc(act_done, 1), "hrs", l)
            phase_end(act, "M", l)

        def dve_m(dve, l):
            barrier(dve, ("E", l))
            dve(nc.vector.memset(XE[:, :, 0:3], 0.0).then_inc(dve_done, 1))
            dve(nc.vector.memset(VX[:, :, :, 64:65], 1.0).then_inc(dve_done, 1))
            dve(nc.vector.memset(HH[:, 4, :], 0.0).then_inc(dve_done, 1))
            dve(nc.vector.memset(DEN[:, 4, :], 1.0).then_inc(dve_done, 1))
            dve(nc.vector.memset(Mt[:, 4, :], 0.0).then_inc(dve_done, 1))
            dve(nc.vector.memset(R[0][0:4, 0:256], NEG).then_inc(dve_done, 1))
            dve(nc.vector.memset(R[1][0:4, 0:256], NEG).then_inc(dve_done, 1))
            dve(nc.vector.memset(PM[:, 4, :], 0.0).then_inc(dve_done, 1), "mtails", l)
            dve.wait_ge(loaded["M"][l], at("ldM", l))
            dve(nc.vector.tensor_copy(XD[:, :, :, 0:3], CI).then_inc(dve_done, 1))
            dve(nc.vector.tensor_copy(RD[0:4, :, 0], m0[0:4]).then_inc(dve_done, 1))
            for f in range(4):
                dve.wait_ge(pe_done, at("full", "F0", l, f))
                ps = bank("F0", l, f)
                dve(nc.vector.tensor_copy(XE[:, f, 3:515], ps[:, :]).then_inc(dve_done, 1))
                dve.free("F0", l, f)
            dve.wait_ge(pe_done, at("full", "F0", l, "d"))
            ps = bank("F0", l, "d")
            dve(nc.vector.tensor_copy(XD[:, :, :, 3:7], ps[:, 0:128].rearrange("p (f b t) -> p f b t", f=4, b=DB)).then_inc(dve_done, 1))
            dve.free("F0", l, "d")
            cw = Q("cw").rearrange("p (f j) -> p f j", f=4)
            for f in range(4):
                for src, dst in ((lambda j: XE[:, f, j:j + SEQ], QK[:, f, 0:SEQ]),
                                 (lambda j: XD[:, f, :, j:j + DS], QK[:, f, SEQ:NT].rearrange("p (b t) -> p b t", b=DB))):
                    dve(nc.vector.tensor_scalar(dst, src(0), cw[:, f, 0:1], Q("cb")[:, f:f + 1], ALU.mult, ALU.add).then_inc(dve_done, 1))
                    for j in range(1, 4):
                        dve(nc.vector.scalar_tensor_tensor(dst, src(j), cw[:, f, j:j + 1], dst, ALU.mult, ALU.add).then_inc(dve_done, 1))
            dve.name("conv", l)
            dve(nc.vector.tensor_copy(CS[:, :, 0, :], XE[:, :, 512:515]).then_inc(dve_done, 1))
            dve(nc.vector.tensor_copy(CS[:, :, 1:9, :], XD[:, :, :, 4:7]).then_inc(dve_done, 1), "CS", l)
            dve.wait_ge(act_done, at("PT1", l))
            dve.wait_ge(act_done, at("PT0", l))
            dve(nc.vector.tensor_tensor(gx, PM[:, :, 772:776], bc(Q("gb")[:, 4:8], 1, TILES), ALU.add).then_inc(dve_done, 1))
            dve(nc.vector.scalar_tensor_tensor(gax, gx, -1.0, gx, ALU.mult, ALU.max).then_inc(dve_done, 1), "gax", l)
            dve(nc.vector.tensor_tensor(LI, PM[:, :, 768:772], bc(Q("gb")[:, 0:4], 1, TILES), ALU.add).then_inc(dve_done, 1))
            dve.wait_ge(act_done, at("gln", l))
            dve(nc.vector.scalar_tensor_tensor(LF, gx, 0.0, gax, ALU.min, ALU.subtract).then_inc(dve_done, 1), "LF", l)
            dve.wait_ge(pe_done, at("full", "cb", l))
            ps = bank("cb", l)
            dve(nc.vector.tensor_copy(Bt[:, 0:4, :], ps[:, 0:16].rearrange("p (i h) -> p i h", i=4)).then_inc(dve_done, 1))
            dve(nc.vector.memset(Bt[:, 4, :], 0.0).then_inc(dve_done, 1))
            dve(nc.vector.tensor_copy(Bt[0:32, 4, :], ps[0:32, 16:20]).then_inc(dve_done, 1))
            dve.free("cb", l)
            dve(nc.vector.tensor_tensor(AA, LI, Bt, ALU.subtract).then_inc(dve_done, 1), "AA", l)
            dve.wait_ge(pe_done, at("full", "at", l))
            ps = bank("at", l)
            dve(nc.vector.tensor_copy(R[0][0:4, 256:768], ps[0:4, :]).then_inc(dve_done, 1))
            dve.free("at", l)
            for n in range(9):
                k = 1 << n
                dve(nc.vector.tensor_tensor(R[(n + 1) % 2][0:4, 256:768], R[n % 2][0:4, 256:768], R[n % 2][0:4, 256 - k:768 - k], ALU.max).then_inc(dve_done, 1))
            dve.name("Mrow", l)
            dve.wait_ge(pe_done, at("full", "ad", l))
            ps = bank("ad", l)
            dve(nc.vector.tensor_copy(RD[0:4, :, 1:5], ps[0:4, 0:32].rearrange("p (b t) -> p b t", b=DB)).then_inc(dve_done, 1))
            dve.free("ad", l)
            for t in range(1, 5):
                dve(nc.vector.tensor_tensor(RD[0:4, :, t], RD[0:4, :, t - 1], RD[0:4, :, t], ALU.max).then_inc(dve_done, 1))
            dve(nc.vector.tensor_copy(MDc[0:4], RD[0:4, :, 1:5]).then_inc(dve_done, 1))
            dve(nc.vector.tensor_tensor(WIr[0:4], RD[0:4, :, 0:1].broadcast_to([4, 8, 4]), MDc[0:4], ALU.subtract).then_inc(dve_done, 1), "WIx", l)
            dve.wait_ge(act_done, at("silu", l))
            dve(nc.vector.tensor_scalar(QK[:, 0:2, :], QK[:, 0:2, :], SCALE, None, ALU.mult).then_inc(dve_done, 1), "qk", l)
            dve(nc.vector.tensor_tensor(QNp, QK[:, 0:2, SEQ:NT].rearrange("p f (b t) -> p f b t", b=DB), bc(n0, 3, DS), ALU.mult).then_inc(dve_done, 1), "QNp", l)
            dve(nc.vector.tensor_copy(VX[:, 0:4, :, 0:64], PM[:, 0:4, 0:256].rearrange("p i (h e) -> p i h e", h=NH)).then_inc(dve_done, 1))
            dve(nc.vector.tensor_copy(VX[0:32, 4, :, 0:64], PM[0:32, 4, 0:256].rearrange("p (h e) -> p h e", h=NH)).then_inc(dve_done, 1))
            for f in range(2):
                dve.wait_ge(pe_done, at("full", "kt", l, f))
                ps = bank("kt", l, f)
                dve(nc.vector.tensor_copy(Ktok[:, 0:4, 128 * f:128 * f + 128], ps[:, :].rearrange("p (i c) -> p i c", i=4)).then_inc(dve_done, 1))
                dve.free("kt", l, f)
            dve.wait_ge(pe_done, at("full", "kt", l, 2))
            ps = bank("kt", l, 2)
            dve(nc.vector.tensor_copy(Ktok[0:32, 4, :], ps[0:32, 0:256]).then_inc(dve_done, 1))
            dve.free("kt", l, 2)
            dve.wait_ge(pe_done, at("full", "qc", l))
            ps = bank("qc", l)
            dve(nc.vector.tensor_copy(QCs, ps[:, 0:64]).then_inc(dve_done, 1), "QCs", l)
            dve.free("qc", l)
            dve.wait_ge(pe_done, at("full", "mt", l))
            ps = bank("mt", l)
            dve(nc.vector.tensor_tensor(Mt[:, 0:4, :], Bt[:, 0:4, :], ps[:, 0:16].rearrange("p (i h) -> p i h", i=4), ALU.add).then_inc(dve_done, 1))
            dve(nc.vector.tensor_tensor(Mt[0:32, 4, :], Bt[0:32, 4, :], ps[0:32, 16:20], ALU.add).then_inc(dve_done, 1), "Mt", l)
            dve(nc.vector.tensor_copy(WIt[0:32], ps[0:32, 20:24]).then_inc(dve_done, 1))
            dve.free("mt", l)
            dve.wait_ge(pe_done, at("full", "md", l))
            ps = bank("md", l)
            dve(nc.vector.tensor_tensor(ED[0:32], ps[0:32, 0:128].rearrange("p (h t) -> p h t", h=NH), bc(AA[0:32, 4, :], 2, 32), ALU.subtract).then_inc(dve_done, 1))
            dve.free("md", l)
            dve(nc.vector.tensor_scalar(ED[0:32], ED[0:32], 0.0, None, ALU.max).then_inc(dve_done, 1), "EDx", l)
            dve.wait_ge(act_done, at("EDe", l))
            dve(nc.vector.tensor_tensor(ED[0:32], ED[0:32], bc(C("IUd", 32), 1, NH), ALU.mult).then_inc(dve_done, 1))
            dve(nc.vector.tensor_tensor(EDt[0:32], ED[0:32], bc(C("endsel", 32), 1, NH), ALU.mult).then_inc(dve_done, 1))
            dve(nc.vector.reduce_sum(WKD[0:32], EDt[0:32], axis=AX.X).then_inc(dve_done, 1))
            dve(nc.vector.tensor_tensor(KWD[0:32], Ktok[0:32, 4, :].rearrange("p (h d) -> p h d", h=NH), bc(WKD[0:32], 2, HD), ALU.mult).then_inc(dve_done, 1))
            dve.wait_ge(pe_done, at("full", "sd", l))
            ps = bank("sd", l)
            dve(nc.vector.tensor_tensor(ED[0:32], ED[0:32], ps[0:32, 0:128].rearrange("p (h t) -> p h t", h=NH), ALU.mult).then_inc(dve_done, 1), "ED", l)
            dve.free("sd", l)
            dve.wait_ge(pe_done, at("full", "dc", l))
            ps = bank("dc", l)
            dve(nc.vector.tensor_copy(DCs, ps[:, 0:16].rearrange("p (f b) -> p f b", f=2)).then_inc(dve_done, 1))
            dve.free("dc", l)
            dve.wait_ge(pe_done, at("full", "pd", l))
            pd = bank("pd", l)
            pdv = pd[0:32, 0:260].rearrange("p (h e) -> p h e", h=NH)
            hd = HH[0:32, 4, :].rearrange("p (h e) -> p h e", h=NH)
            dve.wait_ge(pe_done, at("full", "qct", l))
            qct = bank("qct", l)
            dve(nc.vector.tensor_tensor(hd, bc(WIt[0:32], 2, HD), qct[0:32, 0:256].rearrange("p (h e) -> p h e", h=NH), ALU.mult).then_inc(dve_done, 1))
            dve.free("qct", l)
            dve(nc.vector.tensor_tensor(hd, hd, pdv[:, :, 0:64], ALU.add).then_inc(dve_done, 1))
            dve.wait_ge(pe_done, at("full", "qn", l))
            qn = bank("qn", l)
            dve(nc.vector.tensor_tensor(dtmp[0:32], WIt[0:32], qn[0:32, 0:4], ALU.mult).then_inc(dve_done, 1))
            dve.free("qn", l)
            dve(nc.vector.tensor_tensor(DEN[0:32, 4, :], dtmp[0:32], pdv[:, :, 64], ALU.add).then_inc(dve_done, 1))
            dve.free("pd", l)
            dve.wait_ge(pe_done, at("full", "nu", l))
            ps = bank("nu", l)
            dve(nc.vector.tensor_tensor(Nn, n0, DCs, ALU.mult).then_inc(dve_done, 1))
            dve(nc.vector.tensor_tensor(Nn, Nn, ps[:, 0:16].rearrange("p (f b) -> p f b", f=2), ALU.add).then_inc(dve_done, 1))
            dve.free("nu", l)
            for h in range(NH):
                if h:
                    dve.wait_ge(pe_done, at("cuh", l, h - 1))
                dve(nc.vector.tensor_tensor(VXe[0:32], bc(VX[0:32, 4, h, 0:64], 1, DB), bc(C("chD", 32), 2, HD), ALU.mult).then_inc(dve_done, 1), "VXe", l, h)
            for hp in range(2):
                dve.wait_ge(pe_done, at("full", "cu", l, hp))
                ps = bank("cu", l, hp)
                dve(nc.vector.tensor_tensor(C0[:, hp], C0[:, hp], bc(DCs[:, hp, :], 2, HD), ALU.mult).then_inc(dve_done, 1))
                dve(nc.vector.tensor_tensor(C0[:, hp], C0[:, hp], ps[:, :].rearrange("p (b e) -> p b e", b=DB), ALU.add).then_inc(dve_done, 1), "Cn", l)
                dve.free("cu", l, hp)
            for h in range(NH):
                EE = EJ[h % 2]
                dve.wait_ge(pe_done, at("full", "mb", l, h))
                ps = bank("mb", l, h)
                for j in range(4):
                    dve(nc.vector.tensor_scalar(EE[:, EOFF[j]:EOFF[j] + 512 - 128 * j], ps[:, 128 * j:512], AA[:, j, h:h + 1], 0.0,
                                              ALU.subtract, ALU.max).then_inc(dve_done, 1))
                dve.name("EJx", l, h)
                dve.free("mb", l, h)
                dve.wait_ge(act_done, at("EJe", l, h))
                for j in range(4):
                    e = EE[:, EOFF[j]:EOFF[j] + 512 - 128 * j]
                    dve(nc.vector.tensor_scalar(KW[:, j, 64 * h:64 * h + 64], Ktok[:, j, 64 * h:64 * h + 64], e[:, 511 - 128 * j:512 - 128 * j],
                                              None, ALU.mult).then_inc(dve_done, 1))
                    dve.wait_ge(pe_done, at("full", "st", l, h, j))
                    ps = bank("st", l, h, j)
                    dve(nc.vector.tensor_tensor(e, e, ps[:, 0:512 - 128 * j], ALU.mult).then_inc(dve_done, 1))
                    dve.free("st", l, h, j)
                    dve(nc.vector.tensor_tensor(e[:, 0:128], e[:, 0:128], C("tri"), ALU.mult).then_inc(dve_done, 1))
                dve.name("PJ", l, h)
                dve.wait_ge(pe_done, at("full", "pv", l, h))
                pv = bank("pv", l, h)
                pvv = pv[:, 0:260].rearrange("p (i e) -> p i e", i=4)
                dve(nc.vector.tensor_copy(HH[:, 0:4, 64 * h:64 * h + 64], pvv[:, :, 0:64]).then_inc(dve_done, 1))
                dve(nc.vector.tensor_copy(DEN[:, 0:4, h:h + 1], pvv[:, :, 64:65]).then_inc(dve_done, 1))
                dve.free("pv", l, h)
            dve.wait_ge(pe_done, at("full", "cf", l))
            ps = bank("cf", l)
            dve(nc.vector.tensor_copy(CP, ps[:, 0:130].rearrange("p (f e) -> p f e", f=2)).then_inc(dve_done, 1), "CP", l)
            dve.free("cf", l)
            dve.wait_ge(act_done, at("EM", l))
            dve(nc.vector.scalar_tensor_tensor(DEN, DEN, -1.0, DEN, ALU.mult, ALU.max).then_inc(dve_done, 1))
            dve(nc.vector.tensor_tensor(DEN, DEN, EM, ALU.max).then_inc(dve_done, 1))
            dve(nc.vector.reciprocal(DEN, DEN).then_inc(dve_done, 1))
            H20 = HH.rearrange("p i (h e) -> p (i h) e", h=NH)
            dve(nc.vector.tensor_tensor(H20, H20, bc(DEN.rearrange("p i h -> p (i h)"), 2, HD), ALU.mult).then_inc(dve_done, 1))
            dve(nc.vector.tensor_tensor(HSQ.rearrange("p (i c) -> p i c", i=TILES), HH, HH, ALU.mult).then_inc(dve_done, 1))
            dve(nc.vector.reduce_sum(hss, HSQ.rearrange("p (i h e) -> p i h e", i=TILES, h=NH), axis=AX.X).then_inc(dve_done, 1), "hss", l)
            dve.wait_ge(act_done, at("hrs", l))
            dve(nc.vector.tensor_tensor(H20, H20, bc(hrs.rearrange("p i h -> p (i h)"), 2, HD), ALU.mult).then_inc(dve_done, 1))
            dve(nc.vector.tensor_tensor(HH, HH, bc(Q("mlg"), 1, TILES), ALU.mult).then_inc(dve_done, 1))
            dve.wait_ge(act_done, at("ogz", l))
            dve(nc.vector.scalar_tensor_tensor(HH, PM[:, :, 256:512], 1.0, HH, ALU.add, ALU.mult).then_inc(dve_done, 1))
            dve(nc.vector.scalar_tensor_tensor(PM[:, :, 512:768], HH, 0.5, PM[:, :, 512:768], ALU.mult, ALU.mult).then_inc(dve_done, 1), "y", l, 0)
            dve_yT(dve, l, 0)
            phase_end(dve, "M", l)

        cv = Carve()
        UX = cv(NRT * 513).rearrange("p (f t) -> p f t", f=NRT)
        UD = cv(NRT * 40).rearrange("p (f b t) -> p f b t", f=NRT, b=DB)
        UC = cv(NRT * 32).rearrange("p (f t) -> p f t", f=NRT)
        SHI = cv(NRT * 8).rearrange("p (f b) -> p f b", f=NRT)
        SHO = cv(NRT * 9).rearrange("p (f b) -> p f b", f=NRT)
        LW, AG = (cv(2 * NT).rearrange("p (f t) -> p f t", f=2) for _ in range(2))
        DTm = cv(512)
        YR = cv(TILES * 256).rearrange("p (i c) -> p i c", i=TILES)
        BN, s4, v4 = cv(4), cv(4), cv(4)
        HWA = cv(4)
        Cc, E1, E2, E3, E4, KK, KE, Bv, RT_, KH, TQ, RX, YY, YF = (cv(256).rearrange("p (f t) -> p f t", f=2) for _ in range(14))
        LWT = cv(256)
        TOK = cv(768).rearrange("p (a c) -> p a c", a=3)
        NNb = cv(2048)
        Nb = [NNb[:, 512 * i:512 * i + 512].rearrange("p (h t) -> p h t", h=NH) for i in range(2)]
        Tb = [NNb[:, 1024 + 512 * i:1536 + 512 * i].rearrange("p (h t) -> p h t", h=NH) for i in range(2)]
        GT, HT_, Zb = (cv(512).rearrange("p (h t) -> p h t", h=NH) for _ in range(3))
        MT = cv(512)
        MTc = MT.rearrange("p (c f k) -> p c f k", c=4, f=2)
        MTd = MT.rearrange("p (c k) -> p c k", c=8)
        WTb = MT.rearrange("p (h t) -> p h t", h=NH)
        ZS = cv(512)
        ZSc = ZS.rearrange("p (c k) -> p c k", c=4)
        ZSd = ZS.rearrange("p (c k) -> p c k", c=8)
        STt = cv(5 * 128).rearrange("p (c k) -> p c k", c=5)
        SD = cv(8 * 128).rearrange("p (b k) -> p b k", b=DB)
        BhE, VE, YE = (NNb[:, 512 * i:512 * i + 512].rearrange("p (c k) -> p c k", c=8) for i in range(3))
        RZ = NNb[:, 0:1280].rearrange("p (i c) -> p i c", i=TILES)

        def um(m, f, ps=slice(0, 128)):
            return UX[ps, f, 1 + 128 * m:129 + 128 * m] if m < 4 else UC[ps, f, :]

        def levels(m):
            return 5 if m < 4 else 2

        def hsl(h):
            return slice(64 * (h % 2), 64 * (h % 2) + 64)

        def pool_r(pool, l):
            barrier(pool, ("M", l))
            pool.wait_ge(stored["M"][l], at("stM", l))
            pool.dma(f"ldR{l}", pool.eng.dma_start(SHI, io["rsh0"][l]).then_inc(loaded["R"][l], 16))
            pool.dma(f"ldR{l}", pool.eng.dma_start(SD, io["rS0"][l]).then_inc(loaded["R"][l], 16), "ldR", l)
            pool.wait_ge(dve_done, at("SHO", l))
            pool.dma(f"stR{l}", pool.eng.dma_start(io["rsh"][l], SHO).then_inc(stored["R"][l], 16))
            pool.wait_ge(dve_done, at("SDn", l))
            pool.dma(f"stR{l}", pool.eng.dma_start(io["rS"][l, :, 8, :], STt[:, 4, :]).then_inc(stored["R"][l], 16))
            pool.dma(f"stR{l}", pool.eng.dma_start(io["rS"][l, :, 0:8, :], SD).then_inc(stored["R"][l], 16), "stR", l)

        def pe_r(pe, l):
            pe_project_fm(pe, l, "F1")
            pe_project_fm(pe, l, "F2")
            pe.wait_ge(act_done, at("tanhw", l))
            lora = Q("lora")
            for key, ps_, in (("lw", slice(0, 64)), ("la", slice(64, 128))):
                for f in range(2):
                    ps = pe.open(key, l, f)
                    pe.full(nc.tensor.matmul(ps[:, :], lora[ps_, 128 * f:128 * f + 128], UX[ps_, 6, 1:513], start=True, stop=True).then_inc(pe_done, 1), key, l, f)
                ps = pe.open(key, l, "d")
                for f in range(2):
                    last = nc.tensor.matmul(ps[:, 32 * f:32 * f + 32], lora[ps_, 128 * f:128 * f + 128], UC[ps_, 6, :], start=True, stop=True)
                pe.full(last.then_inc(pe_done, 1), key, l, "d")
            for m in range(TILES):
                pe_r_block(pe, l, m)
            pe_project_tm(pe, l, "T2")
            pe_yT(pe, l, YR, 4)
            phase_end(pe, "R", l)

        def pe_r_block(pe, l, m):
            n = rows(m)
            pe.wait_ge(dve_done, at("LW", l))
            ps = pe.open("lt", l, m)
            for f in range(2):
                last = nc.tensor.transpose(ps[0:n, 128 * f:128 * f + 128], LW[:, f, tok(m)], idn)
            pe.full(last.then_inc(pe_done, 1), "lt", l, m)
            pe.wait_ge(dve_done, at("LWT", l, m))
            ps = pe.open("cc", l, m)
            for f in range(2):
                last = nc.tensor.matmul(ps[:, n * f:n * f + n], LWT[0:n, 128 * f:128 * f + 128], C("IU") if m < 4 else C("IUd", 32), start=True, stop=True)
            pe.full(last.then_inc(pe_done, 1), "cc", l, m)
            pe.wait_ge(dve_done, at("kk2", l, m))
            ps = pe.open("ns", l, m)
            for f in range(2):
                last = nc.tensor.matmul(ps[:, n * f:n * f + n], C("onesbd"), TQ[:, f, 0:n], start=True, stop=True)
            pe.full(last.then_inc(pe_done, 1), "ns", l, m)
            pe.wait_ge(dve_done, at("fm", l, m))
            for key, srcs in (("t1", (E4, KH)), ("t2", (None, E1))):
                ps = pe.open(key, l, m)
                for a, s in enumerate(srcs):
                    for f in range(2):
                        o = 256 * a + 128 * f
                        src = s[:, f, 0:n] if s is not None else um(m, 4 + f)
                        last = nc.tensor.transpose(ps[0:n, o:o + 128], src, idn)
                pe.full(last.then_inc(pe_done, 1), key, l, m)
            ps = pe.open("bn", l, m)
            for f in range(2):
                last = nc.tensor.matmul(ps[0:n, 2 * f:2 * f + 2], TQ[:, f, 0:n], C("onesbd")[:, 0:128:64], start=True, stop=True)
            pe.full(last.then_inc(pe_done, 1), "bn", l, m)
            pairs = (("pN", E1, E2), ("pT", E2, E1), ("pW", Cc, E1), ("pG", E2, RT_), ("pH", Cc, RT_))
            bank = [pe.open(key, l, m) for key, _, _ in pairs]
            for odd in range(2):
                for (key, a, b), ps in zip(pairs, bank):
                    for hp in range(2):
                        o = n * (2 * hp + odd)
                        last = nc.tensor.matmul(ps[0:n, o:o + n], a[hsl(odd), hp, 0:n], b[hsl(odd), hp, 0:n], start=True, stop=True)
                    if odd:
                        pe.full(last.then_inc(pe_done, 1), key, l, m)
                if not odd:
                    pe.fence(last.then_inc(pe_done, 1))
            pe.wait_ge(dve_done, at("WT", l, m))
            ps = pe.open("wv", l, m)
            for h in range(NH):
                last = nc.tensor.matmul(ps[0:n, 64 * h:64 * h + 64], WTb[0:n, h, 0:n], TOK[0:n, 2, 64 * h:64 * h + 64], start=True, stop=True)
            pe.full(last.then_inc(pe_done, 1), "wv", l, m)
            for lev in range(levels(m)):
                Nl, Tl = Nb[lev % 2], Tb[lev % 2]
                pe.wait_ge(dve_done, at("Nlev", l, m, lev))
                if lev < levels(m) - 1:
                    if lev < levels(m) - 2:
                        ps = pe.open("sq", l, m, lev)
                        for h in range(NH):
                            last = nc.tensor.matmul(ps[0:n, n * h:n * h + n], Tl[0:n, h, 0:n], Nl[0:n, h, 0:n], start=True, stop=True)
                        pe.full(last.then_inc(pe_done, 1), "sq", l, m, lev)
                    ps = pe.open("sqt", l, m, lev)
                    for h in range(NH):
                        last = nc.tensor.matmul(ps[0:n, n * h:n * h + n], Nl[0:n, h, 0:n], Tl[0:n, h, 0:n], start=True, stop=True)
                    pe.full(last.then_inc(pe_done, 1), "sqt", l, m, lev)
                pe.wait_ge(dve_done, at("Z", l, m, lev))
                ps = pe.open("za", l, m, lev)
                for h in range(NH):
                    last = nc.tensor.matmul(ps[0:n, 128 * h:128 * h + 128], Tl[0:n, h, 0:n], Zb[0:n, h, :], start=True, stop=True)
                pe.full(last.then_inc(pe_done, 1), "za", l, m, lev)
            pe.wait_ge(dve_done, at("Z", l, m, levels(m)))
            ps = pe.open("rx", l, m)
            for h in range(NH):
                last = nc.tensor.matmul(ps[hsl(h), n * (h // 2):n * (h // 2) + n], Zb[0:n, h, 0:64], GT[0:n, h, 0:n], start=True, stop=True)
            pe.full(last.then_inc(pe_done, 1), "rx", l, m)
            ps = pe.open("yy", l, m)
            for h in range(NH):
                o = ps[hsl(h), n * (h // 2):n * (h // 2) + n]
                nc.tensor.matmul(o, TOK[0:n, 2, 64 * h:64 * h + 64], HT_[0:n, h, 0:n], start=True, stop=False)
                last = nc.tensor.matmul(o, Zb[0:n, h, 64:128], GT[0:n, h, 0:n], start=False, stop=True)
            pe.full(last.then_inc(pe_done, 1), "yy", l, m)
            if m < 4:
                for c in range(4):
                    r = slice(32 * c, 32 * c + 32)
                    ps = pe.open("mc", l, m, c)
                    for h in range(NH):
                        o = 64 * (h // 2)
                        nc.tensor.matmul(ps[hsl(h), o:o + 64], Zb[r, h, 0:64], TOK[r, 0, 64 * h:64 * h + 64], start=True, stop=True)
                        o += 128
                        nc.tensor.matmul(ps[hsl(h), o:o + 64], TOK[r, 1, 64 * h:64 * h + 64], TOK[r, 2, 64 * h:64 * h + 64], start=True, stop=False)
                        last = nc.tensor.matmul(ps[hsl(h), o:o + 64], TOK[r, 0, 64 * h:64 * h + 64], Zb[r, h, 64:128], start=False, stop=True)
                    pe.full(last.then_inc(pe_done, 1), "mc", l, m, c)
                for c in range(4):
                    pe.wait_ge(dve_done, at("S", l, m, c))
                    ps = pe.open("sc", l, m, c)
                    for h in range(NH):
                        last = nc.tensor.matmul(ps[hsl(h), 64 * (h // 2):64 * (h // 2) + 64], MTc[hsl(h), c, h // 2, :],
                                                STt[hsl(h), c, 64 * (h // 2):64 * (h // 2) + 64], start=True, stop=True)
                    pe.full(last.then_inc(pe_done, 1), "sc", l, m, c)
            pe.wait_ge(dve_done, at("RX", l, m))
            pe.wait_ge(loaded["R"][l], at("ldR", l))
            ps = pe.open("yr", l, m)
            nch, cl = (4, 32) if m < 4 else (8, DS)
            Ssrc = STt if m < 4 else SD
            for h in range(NH):
                for c in range(nch):
                    o = n * (h // 2) + cl * c
                    last = nc.tensor.matmul(ps[hsl(h), o:o + cl], Ssrc[hsl(h), c, 64 * (h // 2):64 * (h // 2) + 64],
                                            RX[hsl(h), h // 2, cl * c:cl * c + cl], start=True, stop=True)
            pe.full(last.then_inc(pe_done, 1), "yr", l, m)
            if m == 4:
                for hp in range(2):
                    pm, pz = pe.open("md4", l, hp), pe.open("zd4", l, hp)
                    for hh in range(2):
                        h = 2 * hp + hh
                        pe.wait_ge(dve_done, at("exp", l, h))
                        nc.tensor.matmul(pm[hsl(h), :], Zb[0:32, h, 0:64], BhE[0:32], start=True, stop=True)
                        nc.tensor.matmul(pz[hsl(h), :], TOK[0:32, 1, 64 * h:64 * h + 64], VE[0:32], start=True, stop=False)
                        pe(nc.tensor.matmul(pz[hsl(h), :], TOK[0:32, 0, 64 * h:64 * h + 64], YE[0:32], start=False, stop=True).then_inc(pe_done, 1), "expu", l, h)
                    pe.name("full", "md4", l, hp)
                    pe.name("full", "zd4", l, hp)
                    pe.wait_ge(dve_done, at("MTd", l, hp))
                    ps = pe.open("sd4", l, hp)
                    for b in range(DB):
                        for hh in range(2):
                            last = nc.tensor.matmul(ps[hsl(hh), 64 * b:64 * b + 64], MTd[hsl(hh), b, :], SD[hsl(hh), b, 64 * hp:64 * hp + 64],
                                                    start=True, stop=True)
                    pe.full(last.then_inc(pe_done, 1), "sd4", l, hp)
            pe.wait_ge(dve_done, at("YF", l, m))
            ps = pe.open("yt2", l, m)
            for f in range(2):
                last = nc.tensor.transpose(ps[0:n, 128 * f:128 * f + 128], YF[:, f, 0:n], idn)
            pe.full(last.then_inc(pe_done, 1), "yt2", l, m)

        def act_r(act, l):
            barrier(act, ("M", l))
            act.wait_ge(dve_done, at("um", l))
            act(nc.scalar.activation(UX[0:64, 6, 1:513], UX[0:64, 6, 1:513], ACT.Tanh).then_inc(act_done, 1))
            act(nc.scalar.activation(UC[0:64, 6, :], UC[0:64, 6, :], ACT.Tanh).then_inc(act_done, 1), "tanhw", l)
            for key, dst, o in (("lw", LW, 0), ("la", AG, 2)):
                for f in range(2):
                    act.wait_ge(pe_done, at("full", key, l, f))
                    ps = bank(key, l, f)
                    act(nc.scalar.activation(dst[:, f, 0:SEQ], ps[:, :], ACT.Tanh, bias=HWA[:, o + f:o + f + 1], scale=0.5).then_inc(act_done, 1))
                    act.free(key, l, f)
                act.wait_ge(pe_done, at("full", key, l, "d"))
                ps = bank(key, l, "d")
                for f in range(2):
                    act(nc.scalar.activation(dst[:, f, SEQ:NT], ps[:, 32 * f:32 * f + 32], ACT.Tanh, bias=HWA[:, o + f:o + f + 1], scale=0.5).then_inc(act_done, 1))
                act.free(key, l, "d")
                act.name("th" + key, l)
            for m in range(TILES):
                n = rows(m)
                act.wait_ge(dve_done, at("Ex", l, m))
                act(nc.scalar.activation(E1[:, :, 0:n], E1[:, :, 0:n], ACT.Exp).then_inc(act_done, 1))
                act(nc.scalar.activation(E2[:, :, 0:n], Cc[:, :, 0:n], ACT.Exp, scale=-1.0).then_inc(act_done, 1))
                act(nc.scalar.activation(E3[:, :, 0:n], Cc[:, :, 0:n], ACT.Exp).then_inc(act_done, 1))
                act(nc.scalar.activation(E4[:, :, 0:n], E4[:, :, 0:n], ACT.Exp).then_inc(act_done, 1), "E", l, m)
                act.wait_ge(dve_done, at("ss", l, m))
                act(nc.scalar.activation(TQ[:, :, 0:n], TQ[:, :, 0:n], ACT.Ln, scale=float(2 ** 20)).then_inc(act_done, 1))
                act(nc.scalar.activation(TQ[:, :, 0:n], TQ[:, :, 0:n], ACT.Exp, bias=ln2_10, scale=-0.5).then_inc(act_done, 1), "ri", l, m)
                act.wait_ge(dve_done, at("v4", l, m))
                act(nc.scalar.activation(v4[0:n], v4[0:n], ACT.Ln, bias=rweps[0:n], scale=1.0 / HD).then_inc(act_done, 1))
                act(nc.scalar.activation(v4[0:n], v4[0:n], ACT.Exp, scale=-0.5).then_inc(act_done, 1), "lnr", l, m)
            for i in range(TILES):
                act.wait_ge(pe_done, at("full", "T2", l, i))
                ps = bank("T2", l, i)
                if i == 0:
                    act.wait_ge(dve_done, at("rblocks", l))
                act(nc.scalar.activation(RZ[0:rows(i), i, :], ps[0:rows(i), 0:256], ACT.Silu).then_inc(act_done, 1))
                act.free("T2", l, i)
            act.name("RZ", l)
            phase_end(act, "R", l)

        def dve_r(dve, l):
            barrier(dve, ("M", l))
            dve.wait_ge(stored["M"][l], at("stM", l))
            dve(nc.vector.memset(UX[:, :, 0:1], 0.0).then_inc(dve_done, 1))
            dve(nc.vector.memset(STt[:, 4, :], 0.0).then_inc(dve_done, 1))
            dve(nc.vector.tensor_scalar(HWA[:, 0:2], Q("w0"), 0.5, None, ALU.mult).then_inc(dve_done, 1))
            dve(nc.vector.tensor_scalar(HWA[:, 2:4], Q("a0"), 0.5, None, ALU.mult).then_inc(dve_done, 1))
            dve.wait_ge(loaded["R"][l], at("ldR", l))
            dve(nc.vector.tensor_copy(UD[:, :, :, 0], SHI).then_inc(dve_done, 1))
            for name, f0, nf in (("F1", 0, 4), ("F2", 4, 3)):
                for f in range(nf):
                    dve.wait_ge(pe_done, at("full", name, l, f))
                    ps = bank(name, l, f)
                    dve(nc.vector.tensor_copy(UX[:, f0 + f, 1:513], ps[:, :]).then_inc(dve_done, 1))
                    dve.free(name, l, f)
                dve.wait_ge(pe_done, at("full", name, l, "d"))
                ps = bank(name, l, "d")
                dve(nc.vector.tensor_copy(UD[:, f0:f0 + nf, :, 1:5], ps[:, 0:32 * nf].rearrange("p (f b t) -> p f b t", f=nf, b=DB)).then_inc(dve_done, 1))
                dve.free(name, l, "d")
            dve(nc.vector.tensor_copy(SHO[:, :, 8:9], UX[:, :, 512:513]).then_inc(dve_done, 1))
            dve(nc.vector.tensor_copy(SHO[:, :, 0:8], UD[:, :, :, 4]).then_inc(dve_done, 1), "SHO", l)
            mu = Q("mu")
            for f in range(NRT):
                dve(nc.vector.tensor_tensor(DTm, UX[:, f, 0:512], UX[:, f, 1:513], ALU.subtract).then_inc(dve_done, 1))
                dve(nc.vector.scalar_tensor_tensor(UX[:, f, 1:513], DTm, mu[:, f:f + 1], UX[:, f, 1:513], ALU.mult, ALU.add).then_inc(dve_done, 1))
                dd = DTm[:, 0:32].rearrange("p (b t) -> p b t", b=DB)
                dve(nc.vector.tensor_tensor(dd, UD[:, f, :, 0:4], UD[:, f, :, 1:5], ALU.subtract).then_inc(dve_done, 1))
                dve(nc.vector.scalar_tensor_tensor(UC[:, f, :].rearrange("p (b t) -> p b t", b=DB), dd, mu[:, f:f + 1], UD[:, f, :, 1:5],
                                                 ALU.mult, ALU.add).then_inc(dve_done, 1))
            dve.name("um", l)
            dve.wait_ge(act_done, at("thlw", l))
            dve(nc.vector.tensor_scalar(LW, LW, -0.5 * DECAY, -0.5 * DECAY, ALU.mult, ALU.add).then_inc(dve_done, 1), "LW", l)
            dve.wait_ge(act_done, at("thla", l))
            dve(nc.vector.tensor_scalar(AG, AG, 0.5, 0.5, ALU.mult, ALU.add).then_inc(dve_done, 1))
            for m in range(TILES):
                dve_r_block(dve, l, m)
            dve.name("rblocks", l)
            dve.wait_ge(act_done, at("RZ", l))
            dve(nc.vector.tensor_tensor(YR[:, 0:4, :], YR[:, 0:4, :], RZ[:, 0:4, :], ALU.mult).then_inc(dve_done, 1))
            dve(nc.vector.tensor_tensor(YR[0:32, 4, :], YR[0:32, 4, :], RZ[0:32, 4, :], ALU.mult).then_inc(dve_done, 1), "y", l, 4)
            dve_yT(dve, l, 4)
            phase_end(dve, "R", l)

        def dve_r_block(dve, l, m):
            n = rows(m)
            nch, cl = (4, 32) if m < 4 else (8, DS)
            mk = (lambda s: C(s)) if m < 4 else (lambda s: C(s + "d", 32))
            c2 = lambda b: b[:, :, 0:n]
            r, k = (um_pair(m, f) for f in (0, 2))
            lw, ag = LW[:, :, tok(m)], AG[:, :, tok(m)]
            dve.wait_ge(pe_done, at("full", "lt", l, m))
            ps = bank("lt", l, m)
            dve(nc.vector.tensor_copy(LWT[0:n], ps[0:n, 0:256]).then_inc(dve_done, 1), "LWT", l, m)
            dve.free("lt", l, m)
            dve.wait_ge(pe_done, at("full", "cc", l, m))
            ps = bank("cc", l, m)
            dve(nc.vector.tensor_copy(c2(Cc), ps[:, 0:2 * n].rearrange("p (f t) -> p f t", f=2)).then_inc(dve_done, 1))
            dve.free("cc", l, m)
            dve(nc.vector.tensor_tensor(c2(E1), c2(Cc), lw, ALU.subtract).then_inc(dve_done, 1))
            cend = c2(Cc).rearrange("p f (c t) -> p f c t", t=cl)
            for f in range(2):
                dve(nc.vector.tensor_tensor(c2(E4).rearrange("p f (c t) -> p f c t", t=cl)[:, f], cend[:, f, :, cl - 1:cl].broadcast_to([128, nch, cl]),
                                          cend[:, f], ALU.subtract).then_inc(dve_done, 1))
            dve.name("Ex", l, m)
            dve(nc.vector.tensor_tensor(c2(KK), k, bc(Q("kk"), 2, n), ALU.mult).then_inc(dve_done, 1))
            dve(nc.vector.tensor_tensor(c2(TQ), c2(KK), c2(KK), ALU.mult).then_inc(dve_done, 1), "kk2", l, m)
            dve.wait_ge(pe_done, at("full", "ns", l, m))
            ps = bank("ns", l, m)
            dve(nc.vector.tensor_scalar(c2(TQ), ps[:, 0:2 * n].rearrange("p (f t) -> p f t", f=2), 1e-24, None, ALU.max).then_inc(dve_done, 1), "ss", l, m)
            dve.free("ns", l, m)
            dve(nc.vector.scalar_tensor_tensor(c2(KE), ag, -1.0, bc(Q("ka"), 2, n), ALU.add, ALU.mult).then_inc(dve_done, 1))
            dve(nc.vector.scalar_tensor_tensor(c2(KE), c2(KE), 1.0, k, ALU.add, ALU.mult).then_inc(dve_done, 1))
            dve.wait_ge(act_done, at("ri", l, m))
            dve(nc.vector.tensor_tensor(c2(KK), c2(KK), c2(TQ), ALU.mult).then_inc(dve_done, 1))
            dve(nc.vector.tensor_tensor(c2(Bv), c2(KK), ag, ALU.mult).then_inc(dve_done, 1))
            dve.wait_ge(act_done, at("E", l, m))
            dve(nc.vector.tensor_tensor(c2(E1), c2(E1), c2(KK), ALU.mult).then_inc(dve_done, 1))
            dve(nc.vector.tensor_tensor(c2(Cc), c2(KE), c2(E2), ALU.mult).then_inc(dve_done, 1))
            dve(nc.vector.tensor_tensor(c2(E2), c2(E2), c2(Bv), ALU.mult).then_inc(dve_done, 1))
            dve(nc.vector.tensor_tensor(c2(KH), c2(KE), c2(E4), ALU.mult).then_inc(dve_done, 1))
            dve(nc.vector.tensor_tensor(c2(E4), c2(E4), c2(Bv), ALU.mult).then_inc(dve_done, 1))
            dve(nc.vector.tensor_tensor(c2(RT_), r, c2(E3), ALU.mult).then_inc(dve_done, 1))
            dve(nc.vector.tensor_tensor(c2(TQ), r, c2(KE), ALU.mult).then_inc(dve_done, 1))
            dve(nc.vector.tensor_tensor(c2(TQ), c2(TQ), bc(Q("rk"), 2, n), ALU.mult).then_inc(dve_done, 1), "fm", l, m)
            dve.wait_ge(pe_done, at("full", "t1", l, m))
            ps = bank("t1", l, m)
            dve(nc.vector.tensor_copy(TOK[0:n, 0:2, :], ps[0:n, :].rearrange("p (a c) -> p a c", a=2)).then_inc(dve_done, 1))
            dve.free("t1", l, m)
            dve.wait_ge(pe_done, at("full", "t2", l, m))
            ps = bank("t2", l, m)
            dve(nc.vector.tensor_copy(TOK[0:n, 2, :], ps[0:n, 0:256]).then_inc(dve_done, 1))
            dve(nc.vector.tensor_scalar(Zb[0:n, :, 0:64], ps[0:n, 256:512].rearrange("p (h d) -> p h d", h=NH), -1.0, None, ALU.mult).then_inc(dve_done, 1))
            dve.free("t2", l, m)
            dve.wait_ge(pe_done, at("full", "bn", l, m))
            ps = bank("bn", l, m)
            dve(nc.vector.tensor_copy(BN[0:n], ps[0:n, 0:4]).then_inc(dve_done, 1))
            dve.free("bn", l, m)
            v4n = lambda p: p[0:n, 0:4 * n].rearrange("p (h t) -> p h t", h=NH)
            for key, dst, mask in (("pN", Nb[0], "nSL"), ("pT", Tb[0], "nSU"), ("pW", WTb, "SU"), ("pG", GT, "IU"), ("pH", HT_, "IU")):
                dve.wait_ge(pe_done, at("full", key, l, m))
                ps = bank(key, l, m)
                dve(nc.vector.tensor_tensor(dst[0:n, :, 0:n], v4n(ps), bc(mk(mask), 1, NH), ALU.mult).then_inc(dve_done, 1))
                dve.free(key, l, m)
                if key == "pT":
                    dve.name("Nlev", l, m, 0)
                if key == "pW":
                    dve.name("WT", l, m)
            dve.wait_ge(pe_done, at("full", "wv", l, m))
            ps = bank("wv", l, m)
            dve(nc.vector.tensor_scalar(Zb[0:n, :, 64:128], ps[0:n, 0:256].rearrange("p (h d) -> p h d", h=NH), -1.0, None, ALU.mult).then_inc(dve_done, 1), "Z", l, m, 0)
            dve.free("wv", l, m)
            for lev in range(levels(m)):
                if lev < levels(m) - 1:
                    if lev < levels(m) - 2:
                        dve.wait_ge(pe_done, at("full", "sq", l, m, lev))
                        ps = bank("sq", l, m, lev)
                        dve(nc.vector.tensor_copy(Nb[(lev + 1) % 2][0:n, :, 0:n], v4n(ps)).then_inc(dve_done, 1))
                        dve.free("sq", l, m, lev)
                    dve.wait_ge(pe_done, at("full", "sqt", l, m, lev))
                    ps = bank("sqt", l, m, lev)
                    dve(nc.vector.tensor_copy(Tb[(lev + 1) % 2][0:n, :, 0:n], v4n(ps)).then_inc(dve_done, 1), "Nlev", l, m, lev + 1)
                    dve.free("sqt", l, m, lev)
                dve.wait_ge(pe_done, at("full", "za", l, m, lev))
                ps = bank("za", l, m, lev)
                dve(nc.vector.tensor_tensor(Zb[0:n], ps[0:n, :].rearrange("p (h d) -> p h d", h=NH), Zb[0:n], ALU.add).then_inc(dve_done, 1), "Z", l, m, lev + 1)
                dve.free("za", l, m, lev)
            dve.wait_ge(pe_done, at("full", "rx", l, m))
            ps = bank("rx", l, m)
            dve(nc.vector.tensor_tensor(c2(RX), ps[:, 0:2 * n].rearrange("p (f t) -> p f t", f=2), c2(RT_), ALU.add).then_inc(dve_done, 1), "RX", l, m)
            dve.free("rx", l, m)
            dve.wait_ge(pe_done, at("full", "yy", l, m))
            ps = bank("yy", l, m)
            dve(nc.vector.tensor_copy(c2(YY), ps[:, 0:2 * n].rearrange("p (f t) -> p f t", f=2)).then_inc(dve_done, 1))
            dve.free("yy", l, m)
            if m < 4:
                dve(nc.vector.tensor_copy(STt[:, 0, :], STt[:, 4, :]).then_inc(dve_done, 1), "S", l, m, 0)
                for c in range(4):
                    dve(nc.vector.tensor_tensor(MTc[:, c], bc(C("IDN2"), 1, 2), E3[:, :, 32 * c + 31:32 * c + 32].broadcast_to([128, 2, 64]), ALU.mult).then_inc(dve_done, 1))
                    dve.wait_ge(pe_done, at("full", "mc", l, m, c))
                    ps = bank("mc", l, m, c)
                    dve(nc.vector.tensor_tensor(MTc[:, c], MTc[:, c], ps[:, 0:128].rearrange("p (f k) -> p f k", f=2), ALU.add).then_inc(dve_done, 1))
                    dve(nc.vector.tensor_copy(ZSc[:, c], ps[:, 128:256]).then_inc(dve_done, 1), "S", l, m, 0)
                    dve.free("mc", l, m, c)
                for c in range(4):
                    dve.wait_ge(pe_done, at("full", "sc", l, m, c))
                    ps = bank("sc", l, m, c)
                    dve(nc.vector.tensor_tensor(STt[:, c + 1, :], ps[:, 0:128], ZSc[:, c], ALU.add).then_inc(dve_done, 1), "S", l, m, c + 1)
                    dve.free("sc", l, m, c)
            dve.wait_ge(pe_done, at("full", "yr", l, m))
            ps = bank("yr", l, m)
            dve(nc.vector.tensor_tensor(c2(YF), ps[:, 0:2 * n].rearrange("p (f t) -> p f t", f=2), c2(YY), ALU.add).then_inc(dve_done, 1), "YF", l, m)
            dve.free("yr", l, m)
            if m == 4:
                for hp in range(2):
                    for hh in range(2):
                        h = 2 * hp + hh
                        if h:
                            dve.wait_ge(pe_done, at("expu", l, h - 1))
                        for dst, src in ((BhE, TOK[0:32, 0, 64 * h:64 * h + 64]), (VE, TOK[0:32, 2, 64 * h:64 * h + 64]), (YE, Zb[0:32, h, 64:128])):
                            dve(nc.vector.tensor_tensor(dst[0:32], bc(src, 1, DB), bc(C("chD", 32), 2, HD), ALU.mult).then_inc(dve_done, 1))
                        dve.name("exp", l, h)
                    dve.wait_ge(pe_done, at("full", "md4", l, hp))
                    dve.wait_ge(pe_done, at("full", "zd4", l, hp))
                    pm, pz = bank("md4", l, hp), bank("zd4", l, hp)
                    e3 = E3[:, hp, 0:32].rearrange("p (b t) -> p b t", t=DS)[:, :, DS - 1:DS].broadcast_to([128, DB, 64])
                    dve(nc.vector.tensor_tensor(MTd, bc(C("IDN2"), 1, DB), e3, ALU.mult).then_inc(dve_done, 1))
                    dve(nc.vector.tensor_tensor(MTd, MTd, pm[:, :].rearrange("p (c k) -> p c k", c=8), ALU.add).then_inc(dve_done, 1))
                    dve(nc.vector.tensor_copy(ZSd, pz[:, :].rearrange("p (c k) -> p c k", c=8)).then_inc(dve_done, 1), "MTd", l, hp)
                    dve.free("md4", l, hp)
                    dve.free("zd4", l, hp)
                    dve.wait_ge(pe_done, at("full", "sd4", l, hp))
                    ps = bank("sd4", l, hp)
                    dve(nc.vector.tensor_tensor(SD[:, :, 64 * hp:64 * hp + 64], ps[:, :].rearrange("p (c k) -> p c k", c=8), ZSd, ALU.add).then_inc(dve_done, 1), "SDn", l)
                    dve.free("sd4", l, hp)
            dve.wait_ge(pe_done, at("full", "yt2", l, m))
            ps = bank("yt2", l, m)
            yb = YR[0:n, m, :].rearrange("p (h d) -> p h d", h=NH)
            sq = LWT[0:n].rearrange("p (h d) -> p h d", h=NH)
            dve(nc.vector.tensor_copy(YR[0:n, m, :], ps[0:n, 0:256]).then_inc(dve_done, 1))
            dve.free("yt2", l, m)
            dve(nc.vector.reduce_sum(s4[0:n], yb, axis=AX.X).then_inc(dve_done, 1))
            dve(nc.vector.tensor_scalar(s4[0:n], s4[0:n], -1.0 / HD, None, ALU.mult).then_inc(dve_done, 1))
            dve(nc.vector.tensor_tensor(yb, yb, bc(s4[0:n], 2, HD), ALU.add).then_inc(dve_done, 1))
            dve(nc.vector.tensor_tensor(sq, yb, yb, ALU.mult).then_inc(dve_done, 1))
            dve(nc.vector.reduce_sum(v4[0:n], sq, axis=AX.X).then_inc(dve_done, 1), "v4", l, m)
            dve(nc.vector.tensor_tensor(sq, TOK[0:n, 2, :].rearrange("p (h d) -> p h d", h=NH), bc(BN[0:n], 2, HD), ALU.mult).then_inc(dve_done, 1))
            dve.wait_ge(act_done, at("lnr", l, m))
            dve(nc.vector.tensor_tensor(yb, yb, bc(v4[0:n], 2, HD), ALU.mult).then_inc(dve_done, 1))
            dve(nc.vector.tensor_tensor(YR[0:n, m, :], YR[0:n, m, :], Q("ln0")[0:n], ALU.mult).then_inc(dve_done, 1))
            dve(nc.vector.tensor_tensor(YR[0:n, m, :], YR[0:n, m, :], Q("ln1")[0:n], ALU.add).then_inc(dve_done, 1))
            dve(nc.vector.tensor_tensor(YR[0:n, m, :], YR[0:n, m, :], LWT[0:n], ALU.add).then_inc(dve_done, 1))

        def um_pair(m, f):
            return UX[:, f:f + 2, 1 + 128 * m:129 + 128 * m] if m < 4 else UC[:, f:f + 2, :]

        cv = Carve()
        PN = cv(TILES * 1804).rearrange("p (i c) -> p i c", i=TILES)
        QR = cv(TILES * 256).rearrange("p (i c) -> p i c", i=TILES)
        KC = cv(DB * 128 + 32)
        VC = cv(DB * 128).rearrange("p (b c) -> p b c", b=DB)
        VBD = cv(256)
        nss, mss, ncs, nmx = cv(40), cv(20), cv(16), cv(16)
        GS = cv(60).rearrange("p (i c) -> p i c", i=TILES)
        PP = [cv(512), cv(512)]
        PT = [cv(512), cv(512)]
        pm2, ps2 = [cv(2), cv(2)], [cv(2), cv(2)]
        CO = cv(128)
        PEH, peb = cv(2), cv(2)
        SHB = cv(4128)
        TMP, HID = SHB[:, 0:512], SHB[:, 512:1024]
        Gb = [SHB[:, 1024:1536], SHB[:, 1536:2048]]
        KVT = SHB[:, 2048:3072].rearrange("p (c t) -> p c t", c=2)
        KQ = SHB[:, 3072:4128]
        RT = [PT[0][:, 0:256], PT[0][:, 256:512], PT[1][:, 0:256], PT[1][:, 256:512]]
        sh_o = [0]

        def shc(n):
            sh_o[0] += n
            assert sh_o[0] <= 4128
            return SHB[:, sh_o[0] - n:sh_o[0]]

        QNZ, QBD, QBDM = (shc(256) for _ in range(3))
        QN2, PR, PRT, PG, BT, SELB = (shc(128) for _ in range(6))
        IM, BI = shc(NSLC), shc(NSLC)
        mx8 = shc(16)
        SB, EB = (shc(384).rearrange("p (s c) -> p s c", s=24) for _ in range(2))
        DEN3 = shc(384).rearrange("p (b c) -> p b c", b=DB)
        OTA = shc(192).rearrange("p (r g t) -> p r g t", r=3, g=2)
        OTM = shc(64).rearrange("p (g t) -> p g t", g=2)
        MX, DG, ES = (shc(48) for _ in range(3))
        m48, cmn, csm = (shc(1) for _ in range(3))
        FT = hT
        FQN, FQR, FMQ, FKS, FKW = 0, 2, 4, 6, 7
        GR3 = ((0, 17), (17, 22), (22, 24))
        DT = slice(SEQ, NT)

        def half(h):
            return slice(64 * h, 64 * h + 64)

        def pool_n(pool, l):
            pool.dma(f"stN{l}", pool.eng.dma_start(io["winpast"][l], io["winraw"][l, :, DS:WIN, :]).then_inc(stored["N"][l], 16))
            pool.wait_ge(act_done, at("PT4", l))
            pool.dma(f"stN{l}", pool.eng.dma_start(io["cmp"][l], PN[:, :, 512:768]).then_inc(stored["N"][l], 16))
            pool.wait_ge(dve_done, at("rope", l, 4))
            pool.dma(f"stN{l}", pool.eng.dma_start(io["slc"][l, :, :, 0:128], PN[:, :, 256:384]).then_inc(stored["N"][l], 16))
            pool.dma(f"stN{l}", pool.eng.dma_start(io["slc"][l, :, :, 128:256], PN[:, :, 768:896]).then_inc(stored["N"][l], 16))
            pool.dma(f"stN{l}", pool.eng.dma_start(io["win"][l, :, :, 0:128], PN[:, :, 384:512]).then_inc(stored["N"][l], 16))
            pool.dma(f"stN{l}", pool.eng.dma_start(io["win"][l, :, :, 128:256], PN[:, :, 896:1024]).then_inc(stored["N"][l], 16), "stN", l)

        CJ = ["p"] + list(range(DB))

        def pe_n(pe, l):
            pe_project_tm(pe, l, "T3")
            pe_project_tm(pe, l, "T4")
            w1p = Q("w1p").rearrange("p (c j e) -> p c j e", c=2, j=8)
            ps = pe.open("ph", l)
            for c in range(2):
                for j in range(8):
                    last = nc.tensor.matmul(ps[:, 2 * c:2 * c + 2], w1p[:, c, j, :], Q("pe").rearrange("p (c r j) -> p c r j", c=2, r=2)[:, c, :, j],
                                            start=(j == 0), stop=(j == 7))
            pe.full(last.then_inc(pe_done, 1), "ph", l)
            pe.wait_ge(act_done, at("PT4", l))
            for c in range(2):
                ps = pe.open("kvt", l, c)
                for i in range(4):
                    last = nc.tensor.transpose(ps[:, tok(i)], PN[:, i, 512 + 128 * c:640 + 128 * c], idn)
                pe.full(last.then_inc(pe_done, 1), "kvt", l, c)
            for k, b in enumerate(CJ):
                if b == "p":
                    pe.wait_ge(dve_done, at("KVT", l))
                    pe.wait_ge(sem_of_slot("w1f", l), at("here", "w1f", l))
                    wf = slot("w1f", l).rearrange("p (c s e) -> p c s e", c=2, s=16)
                    kv = KVT.rearrange("p c (n s) -> p c n s", s=16)
                    for h in range(2):
                        ps = pe.open("ab", l, b, h)
                        for c in range(2):
                            for s in range(16):
                                last = nc.tensor.matmul(ps[:, 32 * c:32 * c + 32], wf[half(h), c, s, :], kv[half(h), c, :, s],
                                                        start=(s == 0), stop=(s == 15))
                        pe.full(last.then_inc(pe_done, 1), "ab", l, b, h)
                    pe.name("used", "w1f", l)
                else:
                    pe.wait_ge(sem_of_slot("cmp", l, b), at("here", "cmp", l, b))
                    cs = slot("cmp", l, b).rearrange("p (g j c h n) -> p g j c h n", g=NPAGE, j=8, c=2, h=2)
                    ps = pe.open("ab", l, b)
                    for c in range(2):
                        for h in range(2):
                            for j in range(8):
                                o = 256 * c + 128 * h
                                last = nc.tensor.matmul(ps[:, o:o + 128], w1p[:, c, j, :], cs[:, :, j, c, h, :], start=(j == 0), stop=(j == 7))
                    pe.full(last.then_inc(pe_done, 1), "ab", l, b)
                    pe.name("used", "cmp", l, b)
                if k:
                    pe_cmp_kv(pe, l, k - 1)
            pe_cmp_kv(pe, l, DB)
            pe.wait_ge(dve_done, at("KQ", l))
            for k, (o, n) in enumerate(((0, 512), (512, 512), (1024, 32))):
                ps = pe.open("kn", l, k)
                pe.full(nc.tensor.matmul(ps[:, 0:n], C("onesbd"), KQ[:, o:o + n], start=True, stop=True).then_inc(pe_done, 1), "kn", l, k)
            pe_project_tm(pe, l, "T5")
            pe_project_tm(pe, l, "T6")
            pe.wait_ge(dve_done, at("mqn", l))
            pe.wait_ge(dve_done, at("rope", l, 4))
            for i in range(TILES):
                n = rows(i)
                ps = pe.open("fa", l, i)
                for a in range(4):
                    src = PN[0:n, i, 128 * a:128 * a + 128] if a < 2 else QR[0:n, i, 128 * a - 256:128 * a - 128]
                    last = nc.tensor.transpose(ps[:, n * a:n * a + n], src, idn[0:n, 0:n])
                pe.full(last.then_inc(pe_done, 1), "fa", l, i)
                ps = pe.open("fb", l, i)
                for a, o in enumerate((1292, 1420, 256, 384)):
                    last = nc.tensor.transpose(ps[:, n * a:n * a + n], PN[0:n, i, o:o + 128], idn[0:n, 0:n])
                pe.full(last.then_inc(pe_done, 1), "fb", l, i)
            pe_decode_cmp(pe, l)
            for b in range(DB):
                pe_decode_row(pe, l, b)
            pe.wait_ge(dve_done, at("OTn", l))
            ps = pe.open("oa", l)
            for a in range(4):
                last = nc.tensor.transpose(ps[0:32, 128 * a:128 * a + 128], OTA[:, a // 2, a % 2, :], idn)
            pe.full(last.then_inc(pe_done, 1), "oa", l)
            ps = pe.open("ob", l)
            for a in range(4):
                last = nc.tensor.transpose(ps[0:32, 128 * a:128 * a + 128], OTA[:, 2, a, :] if a < 2 else OTM[:, a - 2, :], idn)
            pe.full(last.then_inc(pe_done, 1), "ob", l)
            pe_prompt(pe, l)
            pe_yT(pe, l, PN[:, :, 0:256], 2)
            pe_yT(pe, l, PN[:, :, 1292:1548], 6)
            phase_end(pe, "N", l)

        def pe_cmp_kv(pe, l, k):
            b, n = CJ[k], (32 if k == 0 else 128)
            w2 = Q("w2")
            g = Gb[k % 2][0:64, 0:4 * n].rearrange("p (c h n) -> p c h n", c=2, h=2)
            pe.wait_ge(act_done, at("G", l, k))
            ps = pe.open("kv", l, k)
            for h in range(2):
                nc.tensor.matmul(ps[half(h), 0:n], w2[0:64, 0:64], g[:, 0, h, :], start=True, stop=True)
            for h in range(2):
                last = nc.tensor.matmul(ps[0:n, 128 + 64 * h:192 + 64 * h], g[:, 1, h, :], w2[0:64, 64:128], start=True, stop=True)
            pe.full(last.then_inc(pe_done, 1), "kv", l, k)

        def pe_decode_cmp(pe, l):
            pe.wait_ge(dve_done, at("QZ", l))
            ps = pe.open("cs", l)
            for b in range(DB):
                last = nc.tensor.matmul(ps[32 * (b // 2):32 * (b // 2) + 32, 0:NCMP], QNZ[:, 32 * b:32 * b + 32], KC[:, 128 * b:128 * b + NCMP],
                                        start=(b % 2 == 0), stop=(b % 2 == 1))
            pe.full(last.then_inc(pe_done, 1), "cs", l)
            pe.wait_ge(dve_done, at("PR", l))
            ps = pe.open("ct", l)
            pe.full(nc.tensor.transpose(ps[:, 0:128], PR, idn).then_inc(pe_done, 1), "ct", l)
            pe.wait_ge(dve_done, at("PG", l))
            ps = pe.open("im", l)
            pe.full(nc.tensor.matmul(ps[:, 0:NSLC], PG, C("cover"), start=True, stop=True).then_inc(pe_done, 1), "im", l)
            ps = pe.open("co", l)
            for b in range(DB):
                last = nc.tensor.matmul(ps[:, 16 * b:16 * b + 16], VC[:, b, :], PRT[:, 16 * b:16 * b + 16], start=True, stop=True)
            pe.full(last.then_inc(pe_done, 1), "co", l)
            pe.wait_ge(dve_done, at("BI", l))
            ps = pe.open("bt", l)
            pe.full(nc.tensor.transpose(ps[0:NSLC, 0:128], BI, idn).then_inc(pe_done, 1), "bt", l)
            pe.wait_ge(dve_done, at("BT", l))
            ps = pe.open("sb", l)
            pe.full(nc.tensor.matmul(ps[:, 0:128], C("expand", NSLC), BT[0:NSLC, :], start=True, stop=True).then_inc(pe_done, 1), "sb", l)

        def pe_decode_row(pe, l, b):
            pe.wait_ge(dve_done, at("QBD", l))
            pe.wait_ge(sem_of_slot("slc", l, b), at("here", "slc", l, b))
            pe.wait_ge(sem_of_slot("wm", l, b), at("here", "wm", l, b))
            sl, wm = slot("slc", l, b), slot("wm", l, b)
            K = sl[:, 0:2048].rearrange("p (n h j) -> p n h j", h=2, j=8)
            Vs = sl[:, 2048:4096].rearrange("p (s c) -> p s c", s=16)
            wK = wm[:, 0:512].rearrange("p (h j n) -> p h j n", h=2, j=2)
            wV = wm[:, 512:1024].rearrange("p (s c) -> p s c", s=4)
            mK = wm[:, 1024:1536].rearrange("p (h n) -> p h n", h=4)
            mV = wm[:, 1536:2048].rearrange("p (s c) -> p s c", s=2)
            ps = pe.open("ds", l, b)
            S = ps[:, 0:384].rearrange("p (s c) -> p s c", s=24)
            for h in range(2):
                q = QBD.rearrange("p (b h c) -> p b h c", b=DB, h=2)[:, b, h, :]
                for j in range(8):
                    nc.tensor.matmul(S[:, 2 * j:2 * j + 2, 8 * h:8 * h + 8], K[:, :, h, j], q, start=True, stop=True)
                for j in range(2):
                    nc.tensor.matmul(S[:, 17 + 2 * j:19 + 2 * j, 8 * h:8 * h + 8], wK[:, h, j, :], q, start=True, stop=True)
            for h in range(NH):
                nc.tensor.matmul(S[:, 22:24, 4 * h:4 * h + 4], mK[:, h, :], QBDM.rearrange("p (b h c) -> p b h c", b=DB, h=4)[:, b, h, :],
                                 start=True, stop=True)
            nc.tensor.matmul(S[0:32, 16, :], FT[:, FKS, DT], QN2[:, 16 * b:16 * b + 16], start=True, stop=True)
            last = nc.tensor.matmul(S[0:32, 21, :], FT[:, FKW, DT], QN2[:, 16 * b:16 * b + 16], start=True, stop=True)
            pe.full(last.then_inc(pe_done, 1), "ds", l, b)
            pe.wait_ge(dve_done, at("MX", l, b))
            ps = pe.open("mxt", l, b)
            pe.full(nc.tensor.transpose(ps[0:48, 0:128], MX, idn).then_inc(pe_done, 1), "mxt", l, b)
            pe.wait_ge(dve_done, at("DG", l, b))
            ps = pe.open("mxb", l, b)
            pe.full(nc.tensor.matmul(ps[:, 0:48], C("ones", 48), DG[0:48, :], start=True, stop=True).then_inc(pe_done, 1), "mxb", l, b)
            pe.wait_ge(act_done, at("EB", l, b))
            ps = pe.open("dp", l, b)
            for s in range(16):
                nc.tensor.matmul(ps[:, 0:16], Vs[:, s, :], EB[:, s, :], start=(s == 0), stop=False)
            nc.tensor.matmul(ps[:, 0:16], PN[0:32, 4, 768:896], EB[0:32, 16, :], start=False, stop=True)
            for s in range(4):
                nc.tensor.matmul(ps[:, 16:32], wV[:, s, :], EB[:, 17 + s, :], start=(s == 0), stop=False)
            nc.tensor.matmul(ps[:, 16:32], PN[0:32, 4, 896:1024], EB[0:32, 21, :], start=False, stop=True)
            for hp in range(2):
                for s in range(2):
                    last = nc.tensor.matmul(ps[:, 32 + 16 * hp:48 + 16 * hp], mV[:, s, 128 * hp:128 * hp + 128], EB[:, 22 + s, :],
                                            start=(s == 0), stop=(s == 1))
            pe(last.then_inc(pe_done, 1))
            pe.name("used", "slc", l, b)
            pe.name("used", "wm", l, b)
            pe.wait_ge(dve_done, at("ES", l, b))
            pe.full(nc.tensor.matmul(ps[:, 64:112], C("ones"), ES, start=True, stop=True).then_inc(pe_done, 1), "dp", l, b)

        UNITS = [(br, i, h) for i in range(4) for br in ("s", "w", "m") for h in range(2)]

        def ukeys(br, i):
            return 128 * (i + 1) if br != "m" else NMEM

        def pe_prompt(pe, l):
            ps = pe.open("pcs", l)
            for h in range(2):
                for i in range(4):
                    for g in range(2):
                        o = 128 * i + 64 * g + 32 * h
                        last = nc.tensor.matmul(ps[:, o:o + 32], FT[half(h), FQN + g, tok(i)], KC[half(h), 1024:1056], start=True, stop=True)
                if h == 0:
                    pe.fence(last.then_inc(pe_done, 1))
            pe.full(last.then_inc(pe_done, 1), "pcs", l)
            pe_unit_s(pe, l, 0)
            pe.wait_ge(dve_done, at("PC", l))
            ps = pe.open("pct", l)
            for i in range(4):
                last = nc.tensor.transpose(ps[:, tok(i)], PP[1][:, tok(i)], idn)
            pe.full(last.then_inc(pe_done, 1), "pct", l)
            pe.wait_ge(dve_done, at("PCT", l))
            for hf in range(2):
                ps = pe.open("pco", l, hf)
                for i in range(2):
                    last = nc.tensor.matmul(ps[:, 256 * i:256 * i + 256], PT[1][:, tok(2 * hf + i)], VBD, start=True, stop=True)
                pe.full(last.then_inc(pe_done, 1), "pco", l, hf)
            for u in range(len(UNITS)):
                if u + 1 < len(UNITS):
                    pe_unit_s(pe, l, u + 1)
                pe_unit_t(pe, l, u)
                pe_unit_v(pe, l, u)

        def pe_unit_s(pe, l, u):
            br, i, h = UNITS[u]
            n = ukeys(br, i)
            if br == "m":
                ps = pe.open("us", l, u, 0)
                for hp in range(2):
                    last = nc.tensor.matmul(ps[:, 256 * hp:256 * hp + 256], FT[half(h), FMQ + hp, tok(i)], MKT[half(h), hp, :], start=True, stop=True)
                pe.full(last.then_inc(pe_done, 1), "us", l, u, 0)
                return
            kt = FKS if br == "s" else FKW
            bk = [pe.open("us", l, u, g) for g in range(2)]
            for g, ps in enumerate(bk):
                last = nc.tensor.matmul(ps[:, 0:n], FT[half(h), FQR + g, tok(i)], FT[half(h), kt, 0:n], start=True, stop=False)
            pe.fence(last.then_inc(pe_done, 1))
            for g, ps in enumerate(bk):
                last = nc.tensor.matmul(ps[:, n - 128:n], idn, C("caus"), start=False, stop=True)
                pe.full(last.then_inc(pe_done, 1), "us", l, u, g)

        def pe_unit_t(pe, l, u):
            br, i, h = UNITS[u]
            n = ukeys(br, i)
            for g in range(2):
                pe.wait_ge(act_done, at("UE", l, u, g))
                ps = pe.open("ut", l, u, g)
                for j in range(n // 128):
                    last = nc.tensor.transpose(ps[:, 128 * j:128 * j + 128], PP[g][:, 128 * j:128 * j + 128], idn)
                pe.full(last.then_inc(pe_done, 1), "ut", l, u, g)

        def pe_unit_v(pe, l, u):
            br, i, h = UNITS[u]
            nk = ukeys(br, i) // 128
            ps = pe.open("uv", l, u)
            for g in range(2):
                pe.wait_ge((dve_done, act_done)[g], at("UT", l, u, g))
                for j in range(nk):
                    v = MKV[:, j, 256 + 64 * (2 * g + h):320 + 64 * (2 * g + h)] if br == "m" else \
                        PN[:, j, (768 if br == "s" else 896) + 64 * h:(832 if br == "s" else 960) + 64 * h]
                    last = nc.tensor.matmul(ps[:, 64 * g:64 * g + 64], PT[g][:, 128 * j:128 * j + 128], v, start=(j == 0), stop=(j == nk - 1))
            pe.full(last.then_inc(pe_done, 1), "uv", l, u)

        def act_n(act, l):
            barrier(act, ("R", l))
            act.wait_ge(stored["R"][l], at("stR", l))
            act.wait_ge(dve_done, at("ntails", l))
            take_project_tm(act, l, "T3", PN[:, :, 0:512], nc.scalar.copy)
            take_project_tm(act, l, "T4", PN[:, :, 512:1024], nc.scalar.copy)
            act.wait_ge(dve_done, at("nss", l))
            act(nc.scalar.activation(nss, nss, ACT.Ln, bias=eps, scale=1.0 / HD).then_inc(act_done, 1))
            act(nc.scalar.activation(nss, nss, ACT.Exp, scale=-0.5).then_inc(act_done, 1), "nrs", l)
            for k in range(len(CJ)):
                n = 32 if k == 0 else 128
                act.wait_ge(dve_done, at("HID", l, k))
                if k >= 2:
                    act.wait_ge(pe_done, at("full", "kv", l, k - 2))
                for c in range(2):
                    act(nc.scalar.activation(Gb[k % 2][0:64, 2 * n * c:2 * n * c + 2 * n], HID[0:64, 2 * n * c:2 * n * c + 2 * n],
                                           ACT.Gelu_apprx_tanh, bias=peb[0:64, c:c + 1]).then_inc(act_done, 1), "G", l, k)
            for k, (o, n) in enumerate(((0, 512), (512, 512), (1024, 32))):
                act.wait_ge(pe_done, at("full", "kn", l, k))
                ps = bank("kn", l, k)
                act(nc.scalar.activation(KQ[:, o:o + n], ps[:, 0:n], ACT.Ln, bias=eps, scale=1.0 / HD).then_inc(act_done, 1))
                act.free("kn", l, k)
            act(nc.scalar.activation(KQ, KQ, ACT.Exp, scale=-0.5).then_inc(act_done, 1), "KR", l)
            take_project_tm(act, l, "T5", PN[:, :, 1024:1292], nc.scalar.copy)
            take_project_tm(act, l, "T6", PN[:, :, 1292:1804], nc.scalar.copy)
            act.wait_ge(dve_done, at("mss", l))
            act(nc.scalar.activation(mss, mss, ACT.Ln, bias=eps, scale=1.0 / HD).then_inc(act_done, 1))
            act(nc.scalar.activation(mss, mss, ACT.Exp, scale=-0.5).then_inc(act_done, 1), "mrs", l)
            act(nc.scalar.activation(PN[:, :, 1024:1280], PN[:, :, 1024:1280], ACT.Silu).then_inc(act_done, 1))
            act(nc.scalar.activation(PN[:, :, 1548:1804], PN[:, :, 1548:1804], ACT.Silu).then_inc(act_done, 1))
            act(nc.scalar.activation(GS, PN[:, :, 1280:1292], ACT.Tanh, scale=0.5).then_inc(act_done, 1), "GS", l)
            for i in range(TILES):
                n = rows(i)
                act.wait_ge(pe_done, at("full", "fa", l, i))
                ps = bank("fa", l, i)
                act(nc.scalar.mul(FT[:, 0:4, tok(i)], ps[:, 0:4 * n].rearrange("p (a t) -> p a t", a=4), SCALE).then_inc(act_done, 1), "FA", l)
                act.free("fa", l, i)
            act.wait_ge(dve_done, at("cmn", l))
            act.wait_ge(pe_done, at("full", "cs", l))
            ps = bank("cs", l)
            act(nc.scalar.activation(PR[:, 0:NCMP], ps[:, 0:NCMP], ACT.Exp, bias=cmn, accum_out=csm).then_inc(act_done, 1), "csm", l)
            act.free("cs", l)
            for b in range(DB):
                act.wait_ge(dve_done, at("EX", l, b))
                act(nc.scalar.activation(EB, EB, ACT.Exp).then_inc(act_done, 1), "EB", l, b)
            act.wait_ge(dve_done, at("PCx", l))
            act(nc.scalar.activation(PP[1], PP[1], ACT.Exp).then_inc(act_done, 1), "PCe", l)
            for u, (br, i, h) in enumerate(UNITS):
                n = ukeys(br, i)
                if u == 0:
                    act.wait_ge(pe_done, at("full", "pct", l))
                else:
                    act.wait_ge(pe_done, at("full", "ut", l, u - 1, 1))
                act.wait_ge(dve_done, at("UM", l, u))
                for g in range(2):
                    act.wait_ge(pe_done, at("full", "us", l, u, 0 if br == "m" else g))
                    ps = bank("us", l, u, 0 if br == "m" else g)
                    s = ps[:, 256 * g:256 * g + 256] if br == "m" else ps[:, 0:n]
                    act(nc.scalar.activation(PP[g][:, 0:n], s, ACT.Exp, bias=pm2[u % 2][:, g:g + 1], accum_out=ps2[u % 2][:, g:g + 1]).then_inc(act_done, 1),
                      "UE", l, u, g)
                    if br != "m" or g:
                        act.free("us", l, u, 0 if br == "m" else g)
                g = 1
                act.wait_ge(pe_done, at("full", "ut", l, u, g))
                ps = bank("ut", l, u, g)
                if u == 0:
                    act.wait_ge(pe_done, at("full", "pco", l, 1))
                else:
                    act.wait_ge(pe_done, at("full", "uv", l, u - 1))
                act(nc.scalar.copy(PT[g][:, 0:n], ps[:, 0:n]).then_inc(act_done, 1), "UT", l, u, g)
                act.free("ut", l, u, g)
            act.wait_ge(stored["N"][l], at("stN", l))
            phase_end(act, "N", l)

        def dve_n(dve, l):
            barrier(dve, ("R", l))
            dve.wait_ge(stored["R"][l], at("stR", l))
            dve(nc.vector.memset(PN[:, 4, :], 0.0).then_inc(dve_done, 1), "ntails", l)
            dve(nc.vector.memset(VBD, 0.0).then_inc(dve_done, 1))
            dve(nc.vector.memset(HID, 0.0).then_inc(dve_done, 1))
            dve.wait_ge(act_done, at("PT3", l))
            for i in range(TILES):
                dve(nc.vector.tensor_tensor(PP[0], PN[:, i, 0:512], PN[:, i, 0:512], ALU.mult).then_inc(dve_done, 1))
                dve(nc.vector.reduce_sum(nss[:, 8 * i:8 * i + 8], PP[0].rearrange("p (h d) -> p h d", d=HD), axis=AX.X).then_inc(dve_done, 1))
            dve.name("nss", l)
            dve.wait_ge(pe_done, at("full", "ph", l))
            ps = bank("ph", l)
            ph = ps[:, 0:4].rearrange("p (c r) -> p c r", c=2)
            dve(nc.vector.tensor_copy(PEH[0:64], ph[64:128, :, 1]).then_inc(dve_done, 1))
            dve(nc.vector.tensor_tensor(peb[0:64], ph[0:64, :, 0], PEH[0:64], ALU.add).then_inc(dve_done, 1))
            dve.free("ph", l)
            for c in range(2):
                dve.wait_ge(pe_done, at("full", "kvt", l, c))
                ps = bank("kvt", l, c)
                dve(nc.vector.tensor_copy(KVT[:, c, :], ps[:, :]).then_inc(dve_done, 1), "KVT", l)
                dve.free("kvt", l, c)
            for k, b in enumerate(CJ):
                n = 32 if k == 0 else 128
                if k:
                    dve.wait_ge(act_done, at("G", l, k - 1))
                hid = HID[0:64, 0:4 * n].rearrange("p (c h n) -> p c h n", c=2, h=2)
                tmp = TMP[0:64, 0:4 * n].rearrange("p (c h n) -> p c h n", c=2, h=2)
                if b == "p":
                    for h in range(2):
                        dve.wait_ge(pe_done, at("full", "ab", l, b, h))
                        ps = bank("ab", l, b, h)
                        pv = ps[:, 0:64].rearrange("p (c n) -> p c n", c=2)
                        dve(nc.vector.tensor_copy(tmp[:, :, h, :], pv[64:128]).then_inc(dve_done, 1))
                        dve(nc.vector.tensor_tensor(hid[:, :, h, 0:n - 1], pv[0:64, :, 0:n - 1], tmp[:, :, h, 1:n], ALU.add).then_inc(dve_done, 1), "HID", l, k)
                        dve.free("ab", l, b, h)
                else:
                    if k == 1:
                        dve(nc.vector.memset(HID, 0.0).then_inc(dve_done, 1))
                    dve.wait_ge(pe_done, at("full", "ab", l, b))
                    ps = bank("ab", l, b)
                    pv = ps[:, :].rearrange("p (a n) -> p a n", a=4)
                    t4, h4 = (a[0:64].rearrange("p (a n) -> p a n", a=4) for a in (TMP, HID))
                    dve(nc.vector.tensor_copy(t4, pv[64:128]).then_inc(dve_done, 1))
                    dve(nc.vector.tensor_tensor(h4[:, :, 0:n - 1], pv[0:64, :, 0:n - 1], t4[:, :, 1:n], ALU.add).then_inc(dve_done, 1), "HID", l, k)
                    dve.free("ab", l, b)
                if k:
                    dve_cmp_kv(dve, l, k - 1)
                if 1 <= k <= TILES:
                    dve_head_norm(dve, l, k - 1)
            dve_cmp_kv(dve, l, DB)
            dve(nc.vector.tensor_tensor(KQ, KC, KC, ALU.mult).then_inc(dve_done, 1), "KQ", l)
            dve.wait_ge(act_done, at("KR", l))
            dve(nc.vector.scalar_tensor_tensor(KC, KC, Q("kcg"), KQ, ALU.mult, ALU.mult).then_inc(dve_done, 1), "KC", l)
            dve.wait_ge(act_done, at("PT6", l))
            mq = PN[:, :, 1292:1548]
            for i in range(TILES):
                dve(nc.vector.tensor_tensor(PP[i % 2][:, 0:256], mq[:, i, :], mq[:, i, :], ALU.mult).then_inc(dve_done, 1))
                dve(nc.vector.reduce_sum(mss[:, 4 * i:4 * i + 4], PP[i % 2][:, 0:256].rearrange("p (h d) -> p h d", d=HD), axis=AX.X).then_inc(dve_done, 1))
            dve.name("mss", l)
            dve.wait_ge(act_done, at("mrs", l))
            m4 = mq.rearrange("p i (h d) -> p i h d", d=HD)
            dve(nc.vector.tensor_tensor(m4, m4, bc(mss.rearrange("p (i h) -> p i h", i=TILES), 3, HD), ALU.mult).then_inc(dve_done, 1))
            dve(nc.vector.tensor_tensor(m4, m4, bc(bc(Q("mqg"), 1, NH), 1, TILES), ALU.mult).then_inc(dve_done, 1), "mqn", l)
            dve.wait_ge(act_done, at("GS", l))
            dve(nc.vector.tensor_scalar(GS, GS, 0.5, 0.5, ALU.mult, ALU.add).then_inc(dve_done, 1))
            for i in range(TILES):
                n = rows(i)
                dve.wait_ge(pe_done, at("full", "fb", l, i))
                ps = bank("fb", l, i)
                dve.wait_ge(pe_done, at("used", "w", l, "T6"))
                dve(nc.vector.tensor_scalar(FT[:, 4:6, tok(i)], ps[:, 0:2 * n].rearrange("p (a t) -> p a t", a=2), SCALE, None, ALU.mult).then_inc(dve_done, 1))
                dve(nc.vector.tensor_copy(FT[:, 6:8, tok(i)], ps[:, 2 * n:4 * n].rearrange("p (a t) -> p a t", a=2)).then_inc(dve_done, 1))
                dve.free("fb", l, i)
            dve_decode_cmp(dve, l)
            for b in range(DB):
                dve_decode_row(dve, l, b)
            dve_decode_out(dve, l)
            dve_prompt(dve, l)
            dve(nc.vector.tensor_tensor(PN[:, :, 0:256], PN[:, :, 0:256], PN[:, :, 1024:1280], ALU.mult).then_inc(dve_done, 1), "y", l, 2)
            dve(nc.vector.tensor_tensor(PN[:, :, 1292:1548], PN[:, :, 1292:1548], PN[:, :, 1548:1804], ALU.mult).then_inc(dve_done, 1), "y", l, 6)
            dve_yT(dve, l, 2)
            dve_yT(dve, l, 6)
            dve.wait_ge(stored["N"][l], at("stN", l))
            phase_end(dve, "N", l)

        def dve_cmp_kv(dve, l, k):
            dve.wait_ge(pe_done, at("full", "kv", l, k))
            ps = bank("kv", l, k)
            if k == 0:
                dve(nc.vector.tensor_copy(KC[:, 1024:1056], ps[:, 0:32]).then_inc(dve_done, 1))
                for hd in range(NH):
                    dve(nc.vector.tensor_copy(VBD[32 * hd:32 * hd + 32, 64 * hd:64 * hd + 64], ps[0:32, 128 + 64 * (hd % 2):192 + 64 * (hd % 2)]).then_inc(dve_done, 1))
            else:
                dve(nc.vector.tensor_copy(KC[:, 128 * (k - 1):128 * k], ps[:, 0:128]).then_inc(dve_done, 1))
                dve(nc.vector.tensor_copy(VC[:, k - 1, :], ps[:, 128:256]).then_inc(dve_done, 1))
            dve.free("kv", l, k)

        def dve_head_norm(dve, l, i):
            if i == 0:
                dve.wait_ge(act_done, at("nrs", l))
            x = PN[:, i, 0:512].rearrange("p (h d) -> p h d", h=8)
            dve(nc.vector.tensor_tensor(x, x, bc(nss[:, 8 * i:8 * i + 8], 2, HD), ALU.mult).then_inc(dve_done, 1))
            dve(nc.vector.tensor_tensor(PN[:, i, 0:512], PN[:, i, 0:512], Q("qkg"), ALU.mult).then_inc(dve_done, 1))
            cs, sn = (bc(C(n)[:, 32 * i:32 * i + 32], 1, 8) for n in ("cos", "sin"))
            R4 = [r.rearrange("p (h d) -> p h d", h=8) for r in RT]
            for r, (a, b) in zip(R4, ((0, cs), (32, sn), (0, sn), (32, cs))):
                dve(nc.vector.tensor_tensor(r, x[:, :, a:a + 32], b, ALU.mult).then_inc(dve_done, 1))
            q = QR[:, i, :].rearrange("p (h d) -> p h d", h=4)
            for dst, s in ((q, slice(0, 4)), (x[:, 4:8], slice(4, 8))):
                dve(nc.vector.tensor_tensor(dst[:, :, 0:32], R4[0][:, s], R4[1][:, s], ALU.subtract).then_inc(dve_done, 1))
                dve(nc.vector.tensor_tensor(dst[:, :, 32:64], R4[2][:, s], R4[3][:, s], ALU.add).then_inc(dve_done, 1), "rope", l, i)

        def dve_decode_cmp(dve, l):
            for a in (QNZ, QBD, QBDM, QN2):
                dve(nc.vector.memset(a, 0.0).then_inc(dve_done, 1))
            dve(nc.vector.memset(PR[:, NCMP:128], 0.0).then_inc(dve_done, 1))
            dve(nc.vector.memset(SB[:, 16:22, :], NEG).then_inc(dve_done, 1))
            dve.wait_ge(act_done, at("FA", l))
            z = QNZ.rearrange("p (b a c) -> p b a c", b=4, a=2)
            for h in range(2):
                for a in range(2):
                    dve(nc.vector.tensor_copy(z[half(h), :, a, 16 * a + 8 * h:16 * a + 8 * h + 8].rearrange("p b (g t) -> p b g t", g=2),
                                            FT[half(h), FQN:FQN + 2, DT].rearrange("p g (b a t) -> p a b g t", b=4, a=2)[:, a]).then_inc(dve_done, 1))
            dve.name("QZ", l)
            qb = QBD.rearrange("p (b h s g t) -> p h s b g t", b=DB, h=2, s=2, g=2)
            qm = QBDM.rearrange("p (b q h s t) -> p h s b q t", b=DB, q=2, h=2, s=2)
            q2 = QN2.rearrange("p (b h g t) -> p h b g t", b=DB, h=2, g=2)
            for h in range(2):
                src = FT[half(h), FQR:FQR + 2, DT].rearrange("p g (b t) -> p b g t", b=DB)
                srm = FT[half(h), FMQ:FMQ + 2, DT].rearrange("p q (b t) -> p b q t", b=DB)
                dve(nc.vector.tensor_copy(q2[half(h), h], src).then_inc(dve_done, 1))
                for s in range(2):
                    dve(nc.vector.tensor_copy(qb[half(s), h, s], src).then_inc(dve_done, 1))
                    dve(nc.vector.tensor_copy(qm[half(s), h, s], srm).then_inc(dve_done, 1), "QBD", l)
            dve.wait_ge(pe_done, at("full", "cs", l))
            ps = bank("cs", l)
            dve(nc.vector.reduce_max(cmn, ps[:, 0:NCMP], axis=AX.X, negate=True).then_inc(dve_done, 1), "cmn", l)
            dve.wait_ge(act_done, at("csm", l))
            dve(nc.vector.reciprocal(csm, csm).then_inc(dve_done, 1))
            dve(nc.vector.tensor_scalar(PR[:, 0:NCMP], PR[:, 0:NCMP], csm, None, ALU.mult).then_inc(dve_done, 1), "PR", l)
            dve.wait_ge(pe_done, at("full", "ct", l))
            ps = bank("ct", l)
            dve(nc.vector.tensor_copy(PRT, ps[:, 0:128]).then_inc(dve_done, 1))
            dve.free("ct", l)
            p4, g4 = (a.rearrange("p (r g t) -> p r g t", g=2, t=4) for a in (PRT, PG))
            for g in range(2):
                dve(nc.vector.tensor_tensor(g4[:, :, g, :], p4[:, :, 0, :], p4[:, :, 1, :], ALU.add).then_inc(dve_done, 1), "PG", l)
            dve.wait_ge(pe_done, at("full", "im", l))
            ps = bank("im", l)
            dve(nc.vector.tensor_tensor(IM, ps[:, 0:NSLC], C("forced"), ALU.add).then_inc(dve_done, 1))
            dve.free("im", l)
            dve(nc.vector.max(mx8[:, 0:8], IM).then_inc(dve_done, 1))
            dve(nc.vector.match_replace(BI, mx8[:, 0:8], IM, -1.0).then_inc(dve_done, 1))
            dve(nc.vector.max(mx8[:, 8:16], BI).then_inc(dve_done, 1))
            dve(nc.vector.match_replace(IM, mx8[:, 8:16], BI, -1.0).then_inc(dve_done, 1))
            dve(nc.vector.tensor_scalar(BI, IM, 0.0, None, ALU.is_ge).then_inc(dve_done, 1), "BI", l)
            dve.wait_ge(pe_done, at("full", "co", l))
            ps = bank("co", l)
            for h in range(2):
                dve(nc.vector.tensor_copy(OTA[half(h), 0].rearrange("p g (b t) -> p b g t", b=DB),
                                        ps[half(h), 0:128].rearrange("p (b h g t) -> p h b g t", b=DB, h=2, g=2)[:, h]).then_inc(dve_done, 1))
            dve.free("co", l)
            dve.wait_ge(pe_done, at("full", "bt", l))
            ps = bank("bt", l)
            dve(nc.vector.tensor_copy(BT[0:NSLC], ps[0:NSLC, 0:128]).then_inc(dve_done, 1), "BT", l)
            dve.free("bt", l)
            dve.wait_ge(pe_done, at("full", "sb", l))
            ps = bank("sb", l)
            dve(nc.vector.tensor_scalar(SELB, ps[:, 0:128], NEG, None, ALU.mult).then_inc(dve_done, 1))
            dve.free("sb", l)

        def dve_decode_row(dve, l, b):
            dve.wait_ge(pe_done, at("full", "ds", l, b))
            ps = bank("ds", l, b)
            S = ps[:, 0:384].rearrange("p (s c) -> p s c", s=24)
            nb = C("newb", 32)[:, 16 * b:16 * b + 16]
            dve(nc.vector.tensor_tensor(SB[:, 0:16, :], S[:, 0:16, :], bc(SELB[:, 16 * b:16 * b + 16], 1, 16), ALU.add).then_inc(dve_done, 1))
            dve(nc.vector.tensor_tensor(SB[:, 17:21, :], S[:, 17:21, :], C("winb").rearrange("p (s c) -> p s c", s=4), ALU.add).then_inc(dve_done, 1))
            for s in (16, 21):
                dve(nc.vector.tensor_tensor(SB[0:32, s, :], S[0:32, s, :], nb, ALU.add).then_inc(dve_done, 1))
            dve(nc.vector.tensor_copy(SB[:, 22:24, :], S[:, 22:24, :]).then_inc(dve_done, 1))
            dve.free("ds", l, b)
            for k, (a, e) in enumerate(GR3):
                dve(nc.vector.reduce_max(MX[:, 16 * k:16 * k + 16], SB[:, a:e, :].rearrange("p s c -> p c s"), axis=AX.X).then_inc(dve_done, 1), "MX", l, b)
            dve.wait_ge(pe_done, at("full", "mxt", l, b))
            ps = bank("mxt", l, b)
            dve(nc.vector.reduce_max(m48[0:48], ps[0:48, 0:128], axis=AX.X).then_inc(dve_done, 1))
            dve.free("mxt", l, b)
            dve(nc.vector.tensor_scalar(DG[0:48], idn[0:48, 0:48], m48[0:48], None, ALU.mult).then_inc(dve_done, 1), "DG", l, b)
            dve.wait_ge(pe_done, at("full", "mxb", l, b))
            ps = bank("mxb", l, b)
            for k, (a, e) in enumerate(GR3):
                dve(nc.vector.tensor_tensor(EB[:, a:e, :], SB[:, a:e, :], bc(ps[:, 16 * k:16 * k + 16], 1, e - a), ALU.subtract).then_inc(dve_done, 1), "EX", l, b)
            dve.free("mxb", l, b)
            dve.wait_ge(act_done, at("EB", l, b))
            for k, (a, e) in enumerate(GR3):
                dve(nc.vector.reduce_sum(ES[:, 16 * k:16 * k + 16], EB[:, a:e, :].rearrange("p s c -> p c s"), axis=AX.X).then_inc(dve_done, 1), "ES", l, b)
            dve.wait_ge(pe_done, at("full", "dp", l, b))
            ps = bank("dp", l, b)
            for h in range(2):
                dve(nc.vector.tensor_copy(OTA[half(h), 1:3, :, 4 * b:4 * b + 4],
                                        ps[half(h), 0:32].rearrange("p (r h g t) -> p h r g t", r=2, h=2, g=2)[:, h]).then_inc(dve_done, 1))
                dve(nc.vector.tensor_copy(OTM[half(h), :, 4 * b:4 * b + 4],
                                        ps[half(h), 32 + 4 * h:80 + 4 * h].rearrange("p (q c) -> p q c", q=2)[:, :, 0:4]).then_inc(dve_done, 1))
            dve(nc.vector.tensor_copy(DEN3[:, b, :], ps[:, 64:112]).then_inc(dve_done, 1))
            dve.free("dp", l, b)

        def dve_decode_out(dve, l):
            dve(nc.vector.reciprocal(DEN3, DEN3).then_inc(dve_done, 1))
            for h in range(2):
                for r in range(2):
                    o = OTA[half(h), 1 + r].rearrange("p g (b t) -> p b g t", b=DB)
                    dve(nc.vector.tensor_tensor(o, o, DEN3[half(h), :, 16 * r + 8 * h:16 * r + 8 * h + 8].rearrange("p b (g t) -> p b g t", g=2), ALU.mult).then_inc(dve_done, 1))
                o = OTM[half(h)].rearrange("p q (b t) -> p b q t", b=DB)
                dve(nc.vector.tensor_tensor(o, o, DEN3[half(h), :, 32:48].rearrange("p b (q h t) -> p h b q t", q=2, h=2)[:, h], ALU.mult).then_inc(dve_done, 1))
            dve.name("OTn", l)
            dve.wait_ge(pe_done, at("full", "oa", l))
            dve.wait_ge(pe_done, at("full", "ob", l))
            oa, ob = bank("oa", l), bank("ob", l)
            acc, mo = PN[0:32, 4, 0:256].rearrange("p (h d) -> p h d", h=4), PN[0:32, 4, 1292:1548]
            dve(nc.vector.tensor_copy(mo, ob[0:32, 256:512]).then_inc(dve_done, 1))
            tmp = PP[0][0:32, 0:256].rearrange("p (h d) -> p h d", h=4)
            for r, src in enumerate((oa[0:32, 0:256], oa[0:32, 256:512], ob[0:32, 0:256])):
                dve(nc.vector.tensor_tensor(acc if r == 0 else tmp, src.rearrange("p (h d) -> p h d", h=4),
                                          bc(GS[0:32, 4, 4 * r:4 * r + 4], 2, HD), ALU.mult).then_inc(dve_done, 1))
                if r:
                    dve(nc.vector.tensor_tensor(acc, acc, tmp, ALU.add).then_inc(dve_done, 1))
            dve.free("oa", l)
            dve.free("ob", l)

        def dve_prompt(dve, l):
            dve.wait_ge(pe_done, at("full", "pcs", l))
            ps = bank("pcs", l)
            s4 = PP[1].rearrange("p (i h e) -> p i h e", i=4, h=4)
            s16 = PP[1].rearrange("p (r e) -> p r e", r=16)
            dve(nc.vector.tensor_tensor(s4, ps[:, :].rearrange("p (i h e) -> p i h e", i=4, h=4),
                                      bc(C("cmpb").rearrange("p (i e) -> p i e", i=4), 2, 4), ALU.add).then_inc(dve_done, 1))
            dve.free("pcs", l)
            dve(nc.vector.reduce_max(nmx, s16, axis=AX.X).then_inc(dve_done, 1))
            dve(nc.vector.tensor_scalar(nmx, nmx, -1e29, None, ALU.max).then_inc(dve_done, 1))
            dve(nc.vector.tensor_tensor(s16, s16, bc(nmx, 2, 32), ALU.subtract).then_inc(dve_done, 1), "PCx", l)
            dve.wait_ge(act_done, at("PCe", l))
            dve(nc.vector.reduce_sum(ncs, s16, axis=AX.X).then_inc(dve_done, 1))
            dve(nc.vector.tensor_scalar(ncs, ncs, 1e-30, None, ALU.max).then_inc(dve_done, 1))
            dve(nc.vector.reciprocal(ncs, ncs).then_inc(dve_done, 1))
            n4 = ncs.rearrange("p (i h) -> p i h", i=4)
            dve(nc.vector.tensor_tensor(n4, n4, GS[:, 0:4, 0:4], ALU.mult).then_inc(dve_done, 1))
            dve(nc.vector.tensor_tensor(s16, s16, bc(ncs, 2, 32), ALU.mult).then_inc(dve_done, 1), "PC", l)
            dve.wait_ge(pe_done, at("full", "pct", l))
            ps = bank("pct", l)
            dve(nc.vector.tensor_copy(PT[1], ps[:, :]).then_inc(dve_done, 1), "PCT", l)
            dve.free("pct", l)
            for hf in range(2):
                dve.wait_ge(pe_done, at("full", "pco", l, hf))
                ps = bank("pco", l, hf)
                dve(nc.vector.tensor_copy(PN[:, 2 * hf:2 * hf + 2, 0:256], ps[:, :].rearrange("p (i c) -> p i c", i=2)).then_inc(dve_done, 1))
                dve.free("pco", l, hf)
            dve_unit_m(dve, l, 0)
            for u, (br, i, h) in enumerate(UNITS):
                if u + 1 < len(UNITS):
                    dve_unit_m(dve, l, u + 1)
                n = ukeys(br, i)
                dve.wait_ge(pe_done, at("full", "ut", l, u, 0))
                ps = bank("ut", l, u, 0)
                if u:
                    dve.wait_ge(pe_done, at("full", "uv", l, u - 1))
                dve(nc.vector.tensor_copy(PT[0][:, 0:n], ps[:, 0:n]).then_inc(dve_done, 1), "UT", l, u, 0)
                dve.free("ut", l, u, 0)
                dve.wait_ge(act_done, at("UE", l, u, 1))
                c2 = CO[:, 2 * (u % 8):2 * (u % 8) + 2]
                dve(nc.vector.reciprocal(c2, ps2[u % 2]).then_inc(dve_done, 1))
                if br != "m":
                    r = 4 if br == "s" else 8
                    dve(nc.vector.tensor_tensor(c2, c2, GS[:, i, r:r + 4].rearrange("p (g h) -> p h g", g=2)[:, h], ALU.mult).then_inc(dve_done, 1))
                dve.wait_ge(pe_done, at("full", "uv", l, u))
                ps = bank("uv", l, u)
                pv = ps[:, 0:128].rearrange("p (g d) -> p g d", g=2)
                base = 1292 if br == "m" else 0
                dst = PN[:, i, base:base + 256].rearrange("p (g h d) -> p h g d", g=2, h=2)[:, h]
                if br == "m":
                    dve(nc.vector.tensor_tensor(dst, pv, bc(c2, 2, HD), ALU.mult).then_inc(dve_done, 1))
                else:
                    t = CO2.rearrange("p (g d) -> p g d", g=2)
                    dve(nc.vector.tensor_tensor(t, pv, bc(c2, 2, HD), ALU.mult).then_inc(dve_done, 1))
                    dve(nc.vector.tensor_tensor(dst, dst, t, ALU.add).then_inc(dve_done, 1))
                dve.free("uv", l, u)

        CO2 = cv(128)

        def dve_unit_m(dve, l, u):
            br, i, h = UNITS[u]
            n = ukeys(br, i)
            if br == "m":
                dve.wait_ge(pe_done, at("full", "us", l, u, 0))
                ps = bank("us", l, u, 0)
                dve(nc.vector.reduce_max(pm2[u % 2], ps[:, :].rearrange("p (g n) -> p g n", g=2), axis=AX.X, negate=True).then_inc(dve_done, 1), "UM", l, u)
            else:
                for g in range(2):
                    dve.wait_ge(pe_done, at("full", "us", l, u, g))
                    ps = bank("us", l, u, g)
                    dve(nc.vector.reduce_max(pm2[u % 2][:, g:g + 1], ps[:, 0:n], axis=AX.X, negate=True).then_inc(dve_done, 1), "UM", l, u)

        PE_STAGES = (pe_m, pe_r, pe_n,)
        ACT_STAGES = (act_m, act_r, act_n,)
        DVE_STAGES = (dve_m, dve_r, dve_n,)
        POOL_STAGES = (pool_m, pool_r, pool_n,)

        def pe_out(pe, l):
            for t0 in (0, 2, 4, 6):
                pe.wait_ge(dve_done, at("YT", l, t0))
            for hf in range(2):
                pe.wait_ge(sem_of_slot("wout", l, hf), at("here", "wout", l, hf))
                w = slot("wout", l, hf).rearrange("p (k c) -> p k c", k=KT)
                for i in range(TILES):
                    ps = pe.open("out", l, hf, i)
                    for k in range(KT):
                        last = nc.tensor.matmul(ps[0:rows(i), :], YT[:, k, tok(i)], w[:, k, :], start=(k == 0), stop=(k == KT - 1))
                    pe.full(last.then_inc(pe_done, 1), "out", l, hf, i)
                pe.name("used", "wout", l, hf)

        def dve_out(dve, l):
            for hf in range(2):
                for i in range(TILES):
                    dve.wait_ge(pe_done, at("full", "out", l, hf, i))
                    ps = bank("out", l, hf, i)
                    xs = X[0:rows(i), i, 512 * hf:512 * hf + 512]
                    dve(nc.vector.tensor_tensor(xs, ps[0:rows(i), :], xs, ALU.add).then_inc(dve_done, 1))
                    dve.free("out", l, hf, i)
            dve.name("x", l + 1)

        block = ctx.enter_context(nc.Block())

        @block.sync
        def _(eng):
            sp = Line(plan, eng, "sp")
            sp.dma("const", sp.eng.dma_start(cst[:, :], io["const"]).then_inc(const_in, 16), "const")
            sp.dma("prm0", sp.eng.dma_start(prm[:, :], io["prm"][0]).then_inc(prm_in[0], 16), "prm", 0)
            sp.dma("ptab", sp.eng.dma_start(ptab[:, :], io["ptab"]).then_inc(ptab_in, 16), "ptab")
            sp.wait_ge(ptab_in, at("ptab"))
            sp.wait_ge(dve_done, at("X0"))
            sp.dma("x", sp.eng.dma_start(X[:, 0:4, :], io["x"][:, 0:4, :]).then_inc(x_in, 16))
            sp.dma("x", sp.eng.dma_start(X[0:DTOK, 4, :], io["x"][0:DTOK, 4, :]).then_inc(x_in, 16), "x", 0)
            sp.dma("memx0", sp.eng.dma_start(E["memx"], io["memx"]).then_inc(memx_in[0], 16), "memx", 0)
            sync_stream(sp)

        @block.gpsimd
        def _(eng):
            pool = Line(plan, eng, "pool")
            for l in range(DEPTH):
                if l:
                    for who in ("pe", "dve", "act"):
                        pool.wait_ge(done[who], at(who, "N", l - 1))
                    pool.dma(f"prm{l}", pool.eng.dma_start(prm[:, :], io["prm"][l]).then_inc(prm_in[l], 16), "prm", l)
                    pool.wait_ge(stored["N"][l - 1], at("stN", l - 1))
                    pool.dma(f"memx{l}", pool.eng.dma_start(E["memx"], io["memx"]).then_inc(memx_in[l], 16), "memx", l)
                for st in POOL_STAGES:
                    st(pool, l)
            pool.wait_ge(dve_done, at("x", DEPTH))
            pool.dma("st_end", pool.eng.dma_start(io["y"], X).then_inc(y_stored, 16), "end")
            pool.wait_ge(y_stored, at("end"))
            for l in range(DEPTH):
                for ph in "EMRN":
                    pool.wait_ge(stored[ph][l], at("st" + ph, l))

        @block.tensor
        def _(eng):
            pe = Line(plan, eng, "pe", chained=False)
            for l in range(DEPTH):
                pe_norm(pe, l)
                pe_memkv(pe, l)
                for st in PE_STAGES:
                    st(pe, l)
                pe_out(pe, l)

        @block.scalar
        def _(eng):
            act = Line(plan, eng, "act")
            for l in range(DEPTH):
                act_norm(act, l)
                act_memkv(act, l)
                phase_end(act, "E", l)
                for st in ACT_STAGES:
                    st(act, l)

        @block.vector
        def _(eng):
            dve = Line(plan, eng, "dve")
            dve(nc.vector.memset(X[:, 4, :], 0.0).then_inc(dve_done, 1), "X0")
            for l in range(DEPTH):
                dve_norm(dve, l)
                dve_memkv(dve, l)
                phase_end(dve, "E", l)
                for st in DVE_STAGES:
                    st(dve, l)
                dve_out(dve, l)


def layout(inp):
    f = np.float32
    I = {k: np.asarray(v) for k, v in inp.items()}
    o = {"const": CONST}

    def rep(a):
        return np.broadcast_to(a, (128,) + a.shape)

    w = I["w_in"]
    A0 = 0
    B0 = 1288
    C0_ = B0 + 1292
    D0 = C0_ + 1152
    ar = np.arange
    gk = np.concatenate([ar(64) + 64 * (2 * kv + g) for g in range(2) for kv in range(2)])
    gh = np.array([2 * kv + g for g in range(2) for kv in range(2)])
    cols = {
        "F0": A0 + ar(512), "T0": np.concatenate([A0 + 512 + ar(256), A0 + 776 + ar(256)]),
        "T1": np.concatenate([A0 + 1032 + ar(256), A0 + 768 + ar(8)]),
        "F1": C0_ + ar(512), "F2": C0_ + 512 + ar(384), "T2": C0_ + 896 + ar(256),
        "T3": np.concatenate([B0 + gk, B0 + 512 + ar(128), B0 + 768 + ar(128)]),
        "T4": np.concatenate([B0 + 256 + ar(256), B0 + 640 + ar(128), B0 + 896 + ar(128)]),
        "T5": np.concatenate([B0 + 1036 + gk] + [B0 + 1024 + 4 * br + gh for br in range(3)]),
        "T6": D0 + ar(512)}
    parts = []
    for n, wd in CHUNKS:
        ww = w[:, :, cols[n]].reshape(DEPTH, KT, 128, wd).transpose(0, 2, 1, 3).reshape(DEPTH, 128, KT * wd)
        parts.append(ww)
    o["win_"] = np.ascontiguousarray(np.concatenate(parts, 2))
    rowsel = np.concatenate([ar(256), 256 + gk, 512 + ar(256), 768 + ar(256)])
    wo = I["w_out"][:, rowsel]
    o["wout"] = np.ascontiguousarray(wo.reshape(DEPTH, KT, 128, 2, 512).transpose(0, 3, 2, 1, 4).reshape(DEPTH, 2, 128, 4096))
    o["wmem"] = np.ascontiguousarray(I["w_mem_kv"].reshape(DEPTH, KT, 128, 512).transpose(0, 2, 1, 3).reshape(DEPTH, 128, 4096))
    w1 = I["nsa_cmp_w1"]
    r = w1.reshape(DEPTH, 2, 2, 16, 64, 64)
    w1p = r.reshape(DEPTH, 2, 2, 8, 2, 64, 64).transpose(0, 4, 5, 1, 3, 2, 6)
    w1p = w1p.reshape(DEPTH, 128, 2048)
    w1f = r.transpose(0, 4, 1, 3, 2, 5).reshape(DEPTH, 64, 4096)
    o["w1f"] = np.ascontiguousarray(np.concatenate([w1f, w1f], 1))
    pe = I["nsa_pe"].reshape(DEPTH, 2, 2, 8, 2, 64).transpose(0, 4, 5, 1, 2, 3).reshape(DEPTH, 128, 32)
    w2 = I["nsa_cmp_w2"].transpose(0, 2, 1, 3).reshape(DEPTH, 64, 128)
    fm = lambda a, n: a.reshape(n, 128).T
    prm = []
    for l in range(DEPTH):
        qk = I["nsa_qk_g"][l]
        P = {
            "g": fm(I["norm_g"][l], 8), "mg": fm(I["mem_norm_g"][l], 8),
            "cw": I["mlstm_conv_w"][l].reshape(4, 4, 128).transpose(2, 1, 0).reshape(128, 16), "cb": fm(I["mlstm_conv_b"][l], 4),
            "gb": rep(I["mlstm_gate_b"][l].reshape(8)), "mlg": rep(I["mlstm_norm_g"][l]),
            "qkg": rep(np.concatenate([qk[0]] * 4 + [qk[2]] * 2 + [qk[3]] * 2)), "kcg": np.concatenate([qk[1], qk[1]])[:, None],
            "mqg": rep(I["mem_qk_g"][l, 0]), "mkg": rep(I["mem_qk_g"][l, 1]), "mu": fm(I["rwkv_mu"][l], 7),
            "w0": fm(I["rwkv_w0"][l], 2), "a0": fm(I["rwkv_a0"][l], 2),
            "kk": fm(I["rwkv_kk"][l, 0], 2), "ka": fm(I["rwkv_kk"][l, 1], 2), "rk": fm(I["rwkv_kk"][l, 2], 2),
            "ln0": rep(I["rwkv_ln"][l, 0]), "ln1": rep(I["rwkv_ln"][l, 1]),
            "lora": np.concatenate([I["rwkv_w2"][l], I["rwkv_a2"][l]], 0), "w2": np.concatenate([w2[l], w2[l]], 0),
            "pe": pe[l], "w1p": w1p[l]}
        prm.append(np.concatenate([P[n].astype(f, copy=False) for n, _ in PARAMS], 1))
    o["prm"] = np.ascontiguousarray(np.stack(prm))
    x = np.zeros((128, TILES, D), f)
    x[:, 0:4] = I["x_prompt"].reshape(4, 128, D).transpose(1, 0, 2)
    x[0:DTOK, 4] = I["x_sample"].reshape(DTOK, D)
    o["x"] = x
    o["memx"] = np.ascontiguousarray(I["mem_prompt"].reshape(2, 128, D).transpose(1, 0, 2))
    o["ptab"] = np.ascontiguousarray(I["page_table"].reshape(1, DB * NPAGE))
    cc = I["cache_cmp_kv"].reshape(DEPTH, NPOOL, 8, 8, 2, 2, 2, 64)
    o["cmpL"] = np.ascontiguousarray(cc.transpose(0, 1, 4, 7, 3, 6, 5, 2).reshape(DEPTH, NPOOL, 128, 256))
    sc = I["cache_slc_kv"].reshape(DEPTH, NPOOL, 8, 8, 2, 2, 2, 64)
    o["slcK"] = np.ascontiguousarray(sc[..., 0, :].transpose(0, 1, 4, 6, 2, 5, 3).reshape(DEPTH, NPOOL, 128, 128))
    o["slcV"] = np.ascontiguousarray(sc[..., 1, :].reshape(DEPTH, NPOOL, 8, 2048))
    wc = I["cache_win_kv"].reshape(DEPTH, DB, 128, 2, 2, 2, 2, 64)
    wK = wc[..., 0, :].transpose(0, 1, 4, 6, 5, 3, 2).reshape(DEPTH, DB, 128, 512)
    wV = wc[..., 1, :].reshape(DEPTH, DB, 128, 512)
    mc = I["cache_mem_kv"].reshape(DEPTH, DB, 128, 2, 4, 2, 64)
    mK = mc[..., 0, :].transpose(0, 1, 3, 5, 4, 2).reshape(DEPTH, DB, 128, 512)
    mV = mc[..., 1, :].reshape(DEPTH, DB, 128, 512)
    o["wmL"] = np.ascontiguousarray(np.concatenate([wK, wV, mK, mV], 3))
    o["winraw"] = np.ascontiguousarray(I["cache_win_kv"].reshape(DEPTH, DB, WIN, 256))
    mC = I["state_mlstm_C"].reshape(DEPTH, DB, 2, 2, 64, 64)
    o["mC0"] = np.ascontiguousarray(mC.transpose(0, 3, 4, 2, 1, 5).reshape(DEPTH, 128, 2, 8, 64))
    mn = I["state_mlstm_n"].reshape(DEPTH, DB, 2, 2, 64)
    o["mn0"] = np.ascontiguousarray(mn.transpose(0, 3, 4, 2, 1).reshape(DEPTH, 128, 2, 8))
    o["mm0"] = np.ascontiguousarray(I["state_mlstm_m"].transpose(0, 2, 1))
    o["mconv0"] = np.ascontiguousarray(I["state_mlstm_conv"].reshape(DEPTH, DB, 3, 4, 128).transpose(0, 4, 3, 1, 2))
    rS = I["state_rwkv_S"].reshape(DEPTH, DB, 2, 2, 64, 64)
    o["rS0"] = np.ascontiguousarray(rS.transpose(0, 3, 5, 1, 2, 4).reshape(DEPTH, 128, 8, 128))
    o["rsh0"] = np.ascontiguousarray(I["state_rwkv_shift"].reshape(DEPTH, DB, NRT, 128).transpose(0, 3, 2, 1))
    return o


def unlayout(r):
    A = np.ascontiguousarray

    def rows_of(a, n):
        return a[:, 0:4].transpose(1, 0, 2).reshape(SEQ, n), a[0:DTOK, 4]

    yp, ys = rows_of(r["y"], D)
    outs = [yp.reshape(1, SEQ, D), ys.reshape(DB, DS, D)]

    def kv(name):
        p, s = zip(*[rows_of(r[name][l], 256) for l in range(DEPTH)])
        p = np.stack(p).reshape(DEPTH, 1, SEQ, 2, 2, 64).transpose(0, 1, 2, 4, 3, 5)
        s = np.stack(s).reshape(DEPTH, DB, DS, 2, 2, 64).transpose(0, 1, 2, 4, 3, 5)
        return p, s

    outs += [*kv("cmp"), *kv("slc")]
    p, s = kv("win")
    past = r["winpast"].reshape(DEPTH, DB, WIN - DS, 2, 2, 64)
    outs += [p, np.concatenate([past, s], 2)]
    outs.append(r["mem"].transpose(0, 2, 1, 3).reshape(DEPTH, 1, NMEM, 2, NH, 64).transpose(0, 1, 2, 4, 3, 5))
    C = r["mC"].reshape(DEPTH, 2, 64, 2, 65).transpose(0, 3, 1, 2, 4).reshape(DEPTH, 1, NH, 64, 65)
    outs.append(C[..., 0:64])
    outs.append(r["mCd"].reshape(DEPTH, 2, 64, 2, 8, 64).transpose(0, 4, 3, 1, 2, 5).reshape(DEPTH, DB, NH, 64, 64))
    outs.append(C[..., 64])
    outs.append(r["mnd"].reshape(DEPTH, 2, 64, 2, 8).transpose(0, 4, 3, 1, 2).reshape(DEPTH, DB, NH, 64))
    outs.append(r["mm"][:, 127:128, 3, :])
    outs.append(r["mm"][:, 3:32:4, 4, :])
    cv = r["mconv"].transpose(0, 3, 4, 2, 1).reshape(DEPTH, 9, 3, 512)
    outs += [cv[:, 0:1], cv[:, 1:]]
    S = r["rS"].reshape(DEPTH, 2, 64, 9, 2, 64).transpose(0, 3, 4, 1, 5, 2).reshape(DEPTH, 9, NH, 64, 64)
    outs += [S[:, 8:9], S[:, 0:8]]
    sh = r["rsh"].transpose(0, 3, 2, 1).reshape(DEPTH, 9, 1, 896)
    outs += [sh[:, 8:9], sh[:, 0:8]]
    return tuple(A(o) for o in outs)


def kernel(**inputs):
    from concourse import bacc
    from concourse.bass_utils import run_bass_kernel_spmd

    arrays = layout(inputs)
    plan = Plan()
    for counting in (True, False):
        plan.counting = counting
        nc = bacc.Bacc("TRN2", target_bir_lowering=False, num_devices=1)
        io = {n: nc.dram_tensor("in_" + n, arrays[n].shape, mybir.dt.from_np(arrays[n].dtype), kind="ExternalInput").ap() for n in INS}
        for n, shape in OUTS.items():
            io[n] = nc.dram_tensor("out_" + n, shape, F32, kind="ExternalOutput").ap()
        build(nc, io, plan)
    r = run_bass_kernel_spmd(nc, [{"in_" + n: arrays[n] for n in INS}], core_ids=[0])
    return unlayout({n: r.results[0]["out_" + n] for n in OUTS})
```

```python
from contextlib import ExitStack

import numpy as np

import concourse.bass as bass
from concourse import mybir

ALU = mybir.AluOpType
ACT = mybir.ActivationFunctionType
F32 = mybir.dt.float32
I32 = mybir.dt.int32
AX = mybir.AxisListType

D = 1024
SEQ = 512
DEPTH = 2
DB, DS = 8, 4
PAST = 2048
PAGE = 128
HD = 64
GW = 256
NH = 4
WIN = 512
NMEM = 256
NPAGE = PAST // PAGE
NPOOL = 5 * DB * NPAGE // 4
CMP_STRIDE, CMP_BLOCK, SLC_BLOCK = 16, 32, 64
NCMP = (PAST - CMP_BLOCK) // CMP_STRIDE + 1
NSUB = PAST // CMP_STRIDE
NSLC = PAST // SLC_BLOCK + 1
PSUBS = SEQ // CMP_STRIDE
PCMP = PSUBS - 1
SCALE = HD ** -0.5
EPS = 1e-6
RW_EPS = HD * 1e-5
DECAY = float(np.exp(-0.5))
NEG = -1e30
DTOK = DB * DS
NT = SEQ + DTOK
TILES = 5
KT = D // 128
CH = 32
NRT = 7
SLOT = 2048
NSLOT = 6

CHUNKS = [("F0", 512), ("T0", 512), ("T1", 264), ("F1", 512), ("F2", 384), ("T2", 256),
          ("T3", 512), ("T4", 512), ("T5", 268), ("T6", 512)]


def rows(i):
    return 128 if i < 4 else DTOK


def tok(i):
    return slice(128 * i, 128 * i + rows(i))


def constants():
    p = np.arange(128)
    t = np.arange(128)
    f = np.float32
    c = {}
    c["idn"] = np.eye(128)
    c["onesbd"] = (p[:, None] // 64 == t[None] // 64)
    c["ones"] = np.ones((128, 128))
    c["caus"] = np.where(t[None] > p[:, None], NEG, 0.0)
    c["tri"] = t[None] >= p[:, None]
    same = p[:, None] // CH == t[None] // CH
    c["nSL"] = -1.0 * (same & (t[None] < p[:, None]))
    c["nSU"] = -1.0 * (same & (t[None] > p[:, None]))
    c["SU"] = same & (t[None] > p[:, None])
    c["IU"] = same & (t[None] >= p[:, None])
    q = np.arange(32)
    samed = (p[:, None] // DS == q[None] // DS) & (p[:, None] < 32)
    c["nSLd"] = -1.0 * (samed & (q[None] < p[:, None]))
    c["nSUd"] = -1.0 * (samed & (q[None] > p[:, None]))
    c["SUd"] = samed & (q[None] > p[:, None])
    c["IUd"] = samed & (q[None] >= p[:, None])
    c["endsel"] = samed & (q[None] % DS == DS - 1)
    c["chD"] = (p[:, None] // DS == np.arange(8)[None]) & (p[:, None] < 32)
    c["IDN2"] = (p[:, None] % 64 == np.arange(64)[None])
    half = HD // 2
    inv = (10000.0 ** (-np.arange(half) / half)).astype(np.float32)
    pos = np.zeros((128, TILES), np.float32)
    for i in range(4):
        pos[:, i] = 128 * i + p
    pos[:32, 4] = PAST + p[:32] % DS
    ang = (pos[:, :, None] * inv.astype(np.float32)).astype(np.float32)
    c["cos"] = np.cos(ang).reshape(128, -1)
    c["sin"] = np.sin(ang).reshape(128, -1)
    n = p[:, None] * CMP_STRIDE
    blk = np.arange(NSLC)[None]
    c["cover"] = (n < (blk + 1) * SLC_BLOCK) & (n + CMP_BLOCK > blk * SLC_BLOCK) & (p[:, None] < NCMP)
    c["expand"] = (p[:, None] == t[None] // 4) & (p[:, None] < NSLC)
    col = np.arange(16)
    tq = col % DS
    s = np.arange(4)
    j = p[:, None] * 4 + s[None]
    c["winb"] = np.where(j[:, :, None] > tq[None, None], 0.0, NEG).reshape(128, -1)
    q = np.arange(128)
    c["newb"] = np.where((p[:, None] // DS == q[None] // 16) & (p[:, None] % DS <= q[None] % DS), 0.0, NEG)
    e = np.arange(32)
    cb = np.zeros((128, 4, 32))
    for i in range(4):
        cb[:, i] = np.where((e[None] < PCMP) & (e[None] * CMP_STRIDE + CMP_BLOCK - 1 <= 128 * i + p[:, None]), 0.0, NEG)
    c["cmpb"] = cb.reshape(128, -1)
    fo = np.zeros((128, NSLC))
    fo[:, 0], fo[:, NSLC - 1], fo[:, NSLC - 2] = 3e30, 2e30, 1e30
    c["forced"] = fo
    m = np.zeros((128, 8))
    m[:, 0], m[:, 1], m[:, 2], m[:, 3] = EPS, 1.0, RW_EPS, 10 * np.log(2.0)
    c["misc"] = m
    offs, parts, o = {}, [], 0
    for k, v in c.items():
        v = np.asarray(v, f)
        offs[k] = (o, v.shape[1])
        parts.append(v)
        o += v.shape[1]
    return np.ascontiguousarray(np.concatenate(parts, 1)), offs


CONST, COFF = constants()

PARAMS = [("g", 8), ("mg", 8), ("cw", 16), ("cb", 4), ("gb", 8), ("mlg", 256), ("qkg", 512), ("kcg", 1),
          ("mqg", 64), ("mkg", 64), ("mu", 7), ("w0", 2), ("a0", 2), ("kk", 2), ("ka", 2), ("rk", 2),
          ("ln0", 256), ("ln1", 256), ("lora", 256), ("w2", 128), ("pe", 32), ("w1p", 2048)]
POFF = {}
_o = 0
for _n, _w in PARAMS:
    POFF[_n] = (_o, _w)
    _o += _w
NPRM = _o

OUTS = {
    "y": (128, TILES, D), "cmp": (DEPTH, 128, TILES, 256), "slc": (DEPTH, 128, TILES, 256),
    "win": (DEPTH, 128, TILES, 256), "winpast": (DEPTH, DB, WIN - DS, 256), "mem": (DEPTH, 128, 2, 512),
    "mC": (DEPTH, 128, 2, 65), "mCd": (DEPTH, 128, 2, 8, 64), "mnd": (DEPTH, 128, 2, 8), "mm": (DEPTH, 128, TILES, NH),
    "mconv": (DEPTH, 128, 4, 9, 3), "rS": (DEPTH, 128, 9, 128), "rsh": (DEPTH, 128, NRT, 9),
}
INS = ["const", "prm", "x", "memx", "wmem", "win_", "wout", "w1f", "ptab", "cmpL", "slcK", "slcV", "wmL", "winraw",
       "mC0", "mn0", "mm0", "mconv0", "rS0", "rsh0"]


class Line:

    def __init__(self, plan, eng, key, chained=True):
        self.plan, self.eng, self.key, self.chained = plan, eng, key, chained
        self.n = 0
        self.seen = {}
        self.done = plan.sems.get(key)

    def wait_ge(self, sem, value):
        if not self.plan.counting and self.seen.get(id(sem), 0) < value:
            self.seen[id(sem)] = value
            self.eng.wait_ge(sem, value)

    def __call__(self, ins, *name):
        self.n += 1
        if self.chained:
            self.wait_ge(self.done, self.n)
        if name:
            self.plan.at[name] = (self.key, self.n)
        return ins

    def name(self, *name):
        self.plan.at[name] = (self.key, self.n)

    def dma(self, sem, ins, *name):
        self.plan.dmas[sem] = self.plan.dmas.get(sem, 0) + 16
        if name:
            self.plan.at[name] = (sem, self.plan.dmas[sem])

    def fence(self, ins):
        self(ins)
        self.wait_ge(self.done, self.n)

    def open(self, *key):
        p = self.plan
        k = len(p.opened)
        p.opened.append(key)
        if k >= 8 and not p.counting:
            key8, value = p.at[("free", *p.opened[k - 8])]
            self.wait_ge(p.sems[key8], value)
        p.bank[key] = k % 8
        return p.banks[k % 8]

    def full(self, ins, *key):
        self(ins, "full", *key)

    def free(self, *key):
        self.name("free", *key)


class Plan:
    def __init__(self):
        self.at, self.bank = {}, {}
        self.counting = True
        self.reset()

    def reset(self):
        self.opened, self.dmas, self.sems, self.banks = [], {}, {}, []


def build(nc, io, plan, debug=None):
    ctx = ExitStack()
    with ctx:
        def sb(name, n, dt=F32):
            return ctx.enter_context(nc.sbuf_tensor(name, [128, n], dt))

        cst = sb("cst", CONST.shape[1])
        prm = sb("prm", NPRM)
        Xf = sb("X", TILES * D)[:, :]
        X = Xf.rearrange("p (i c) -> p i c", i=TILES)
        hT = sb("hT", KT * NT)[:, :].rearrange("p (k t) -> p k t", k=KT)
        YTf = sb("YT", KT * NT)[:, :]
        YT = YTf.rearrange("p (k t) -> p k t", k=KT)
        stream = sb("stream", NSLOT * SLOT)
        MKV = sb("MKV", 2 * 512)[:, :].rearrange("p (i c) -> p i c", i=2)
        MKT = sb("MKT", 2 * 256)[:, :].rearrange("p (i c) -> p i c", i=2)
        ptab = ctx.enter_context(nc.sbuf_tensor("ptab", [1, DB * NPAGE], I32))
        AREA = 19264
        area = sb("area", AREA)
        plan.reset()
        plan.banks = [ctx.enter_context(nc.psum_tensor(f"bank{i}", [128, 512], F32)) for i in range(8)]
        names = ["pe", "dve", "act", "pool", "const", "x", "prm0", "prm1", "memx0", "memx1", "ptab",
                 "st_end"] + [f"slot{i}" for i in range(NSLOT)]
        names += [f"{a}{l}" for a in ("xr", "ys") for l in range(DEPTH)]
        names += [f"{a}{g}{l}" for a in ("st", "ld") for g in "EMRN" for l in range(DEPTH)]
        for n in names:
            plan.sems[n] = ctx.enter_context(nc.semaphore("s_" + n))

        pe_done, dve_done, act_done, pool_done = (plan.sems[n] for n in ("pe", "dve", "act", "pool"))
        done = {n: plan.sems[n] for n in ("pe", "dve", "act", "pool")}
        const_in, ptab_in, x_in, y_stored = (plan.sems[n] for n in ("const", "ptab", "x", "st_end"))
        prm_in, memx_in = ([plan.sems[f"{n}{l}"] for l in range(DEPTH)] for n in ("prm", "memx"))
        x_reloaded, y_kept = ([plan.sems[f"{n}{l}"] for l in range(DEPTH)] for n in ("xr", "ys"))
        slot_in = [plan.sems[f"slot{i}"] for i in range(NSLOT)]
        stored, loaded = ({g: [plan.sems[f"{n}{g}{l}"] for l in range(DEPTH)] for g in "EMRN"} for n in ("st", "ld"))

        def at(*name):
            return 0 if plan.counting else plan.at[name][1]

        def bank(*key):
            return plan.banks[plan.bank.get(key, 0)]

        def sem_of_slot(*item):
            return slot_in[slot_of[item]]

        def C(name, r=128):
            o, w = COFF[name]
            return cst[0:r, o:o + w]

        def Q(name):
            o, w = POFF[name]
            return prm[:, o:o + w]

        def bc(ap, axis, n):
            ap = ap.unsqueeze(axis)
            shape = list(ap.shape)
            shape[axis] = n
            return ap.broadcast_to(shape)

        class Carve:

            def __init__(self):
                self.o = 0

            def __call__(self, n):
                a = area[:, self.o:self.o + n]
                self.o += n
                assert self.o <= AREA, self.o
                return a

        eps, one_c, rweps, ln2_10 = (C("misc")[:, i:i + 1] for i in range(4))
        idn = C("idn")

        def selh(h, n):
            return idn[0:4, h:h + 1].broadcast_to([4, n])

        items = []
        for l in range(DEPTH):
            items += [("wmem", l)] + [("w", l, n) for n, _ in CHUNKS[:5]] + [("cmp", l, b) for b in range(DB)]
            items += [("w", l, n) for n, _ in CHUNKS[5:8]] + [("w1f", l)]
            items += [("w", l, "T6"), ("w", l, "T5")]
            for b in range(DB):
                items += [("slcK", l, b), ("wm", l, b), ("slcV", l, b)]
            items += [("wout", l, 0), ("wout", l, 1)]
        slot_of, before, last_user, at_slot = {}, {}, {}, 0
        for it in items:
            n = 1 if it[0] in ("slcK", "wm", "slcV") else 2
            at_slot += (at_slot % NSLOT) % n
            mine = [(at_slot + i) % NSLOT for i in range(n)]
            slot_of[it] = mine[0]
            before[it] = [last_user[s] for s in mine if s in last_user]
            last_user.update({s: it for s in mine})
            at_slot += n
        coff = {}
        o = 0
        for n, w in CHUNKS:
            coff[n] = (o, w)
            o += w

        def slot(*item):
            s = slot_of[item]
            return stream[:, s * SLOT:(s + (1 if item[0] in ("slcK", "wm", "slcV") else 2)) * SLOT]

        def sync_stream(sp):
            for it in items:
                l = it[1]
                pages = it[0] in ("cmp", "slcK", "slcV")
                if pages and it[0] != "slcV":
                    if it == ("cmp", 0, 0):
                        sp.wait_ge(ptab_in, at("ptab"))
                    page = [sp.eng.value_load(ptab[0:1, it[2] * NPAGE + g:it[2] * NPAGE + g + 1], min_val=0, max_val=NPOOL - 1)
                            for g in range(NPAGE)]
                for old in before[it]:
                    sp.wait_ge(pe_done, at("used", *old))
                s, sem, nm = slot(*it), f"slot{slot_of[it]}", ("here",) + it
                if it[0] == "wmem":
                    sp.dma(sem, sp.eng.dma_start(s, io["wmem"][l]).then_inc(slot_in[slot_of[it]], 16), *nm)
                elif it[0] == "w":
                    o, w = coff[it[2]]
                    sp.dma(sem, sp.eng.dma_start(s[:, 0:KT * w], io["win_"][l, :, KT * o:KT * (o + w)]).then_inc(slot_in[slot_of[it]], 16), *nm)
                elif it[0] == "w1f":
                    sp.dma(sem, sp.eng.dma_start(s, io["w1f"][l]).then_inc(slot_in[slot_of[it]], 16), *nm)
                elif it[0] == "wout":
                    sp.dma(sem, sp.eng.dma_start(s, io["wout"][l, it[2]]).then_inc(slot_in[slot_of[it]], 16), *nm)
                elif it[0] == "wm":
                    sp.dma(sem, sp.eng.dma_start(s, io["wmL"][l, it[2]]).then_inc(slot_in[slot_of[it]], 16), *nm)
                for g in range(NPAGE if pages else 0):
                    pg = bass.DynSlice(page[g], 1)
                    if it[0] == "cmp":
                        sp.dma(sem, sp.eng.dma_start(s[:, g * 256:(g + 1) * 256], io["cmpL"][l, pg].rearrange("a p c -> (a p) c")).then_inc(slot_in[slot_of[it]], 16), *nm)
                    elif it[0] == "slcK":
                        sp.dma(sem, sp.eng.dma_start(s[:, g * 128:(g + 1) * 128], io["slcK"][l, pg].rearrange("a p c -> (a p) c")).then_inc(slot_in[slot_of[it]], 16), *nm)
                    else:
                        sp.dma(sem, sp.eng.dma_start(s[8 * g:8 * g + 8, :], io["slcV"][l, pg].rearrange("a p c -> (a p) c")).then_inc(slot_in[slot_of[it]], 16), *nm)

        cv = Carve()
        E = {"junk": cv(1024), "xn": [cv(1024), cv(1024)], "memx": cv(2048).rearrange("p (i c) -> p i c", i=2),
             "hm": cv(2048).rearrange("p (k t) -> p k t", k=KT), "ss": cv(8), "rs": cv(8), "kj": cv(512), "ks": cv(8), "kr": cv(8)}

        def src_tile(l, i):
            return X[:, i, :] if i < TILES else E["memx"][:, i - TILES, :]

        def act_norm(act, l):
            act.wait_ge(const_in, at("const"))
            for i in range(7):
                if i == 0:
                    act.wait_ge(dve_done if l else x_in, at("x", l))
                if i == TILES:
                    act.wait_ge(memx_in[l], at("memx", l))
                act(nc.scalar.activation(E["junk"], src_tile(l, i), ACT.Square, accum_out=E["ss"][:, i:i + 1]).then_inc(act_done, 1))
            act(nc.scalar.activation(E["rs"][:, 0:7], E["ss"][:, 0:7], ACT.Ln, bias=eps, scale=1.0 / D).then_inc(act_done, 1))
            act(nc.scalar.activation(E["rs"][:, 0:7], E["rs"][:, 0:7], ACT.Exp, scale=-0.5).then_inc(act_done, 1))
            for i in range(7):
                if i >= 2:
                    act.wait_ge(pe_done, at("xnT", l, i - 2))
                act(nc.scalar.mul(E["xn"][i % 2], src_tile(l, i), E["rs"][:, i:i + 1]).then_inc(act_done, 1), "xn", l, i)

        def dve_norm(dve, l):
            dve.wait_ge(prm_in[l], at("prm", l))
            for i in range(7):
                n = rows(i) if i < TILES else 128
                for hf in range(2):
                    dve.wait_ge(pe_done, at("full", "xt", l, i, hf))
                    ps = bank("xt", l, i, hf)
                    g = Q("g" if i < TILES else "mg")[:, 4 * hf:4 * hf + 4]
                    dst = hT[:, 4 * hf:4 * hf + 4, tok(i)] if i < TILES else \
                        E["hm"][:, 4 * hf:4 * hf + 4, 128 * (i - TILES):128 * (i - TILES) + 128]
                    dve(nc.vector.tensor_tensor(dst, ps[:, 0:4 * n].rearrange("p (k t) -> p k t", k=4), bc(g, 2, n), ALU.mult).then_inc(dve_done, 1),
                      "hT", l, i, hf)
                    dve.free("xt", l, i, hf)

        def pe_norm(pe, l):
            pe.wait_ge(const_in, at("const"))
            for i in range(7):
                n = rows(i) if i < TILES else 128
                pe.wait_ge(act_done, at("xn", l, i))
                for hf in range(2):
                    ps = pe.open("xt", l, i, hf)
                    for k in range(4):
                        kk = 4 * hf + k
                        last = nc.tensor.transpose(ps[:, k * n:(k + 1) * n], E["xn"][i % 2][0:n, 128 * kk:128 * kk + 128], idn[0:n, 0:n])
                    pe.full(last.then_inc(pe_done, 1), "xt", l, i, hf)
                pe.name("xnT", l, i)

        def pe_memkv(pe, l):
            pe.wait_ge(dve_done, at("hT", l, 6, 1))
            pe.wait_ge(sem_of_slot("wmem", l), at("here", "wmem", l))
            w = slot("wmem", l).rearrange("p (k c) -> p k c", k=KT)
            for i in range(2):
                ps = pe.open("mk", l, i)
                for k in range(KT):
                    last = nc.tensor.matmul(ps[:, :], E["hm"][:, k, 128 * i:128 * i + 128], w[:, k, :], start=(k == 0), stop=(k == KT - 1))
                pe.full(last.then_inc(pe_done, 1), "mk", l, i)
            pe.name("used", "wmem", l)
            pe.wait_ge(dve_done, at("mkn", l))
            ps = pe.open("mkt", l)
            for i in range(2):
                for pr in range(2):
                    last = nc.tensor.transpose(ps[:, pr * 256 + 128 * i:pr * 256 + 128 * i + 128], MKV[:, i, 128 * pr:128 * pr + 128], idn)
            pe.full(last.then_inc(pe_done, 1), "mkt", l)
            phase_end(pe, "E", l)

        def dve_memkv(dve, l):
            for i in range(2):
                dve.wait_ge(pe_done, at("full", "mk", l, i))
                ps = bank("mk", l, i)
                dve(nc.vector.tensor_copy(MKV[:, i, :], ps[:, :]).then_inc(dve_done, 1))
                dve.free("mk", l, i)
            k = MKV[:, :, 0:256].rearrange("p i (h d) -> p i h d", d=HD)
            kj = E["kj"].rearrange("p (i h d) -> p i h d", i=2, d=HD)
            dve(nc.vector.tensor_tensor(kj, k, k, ALU.mult).then_inc(dve_done, 1))
            dve(nc.vector.reduce_sum(E["ks"], E["kj"].rearrange("p (j d) -> p j d", d=HD), axis=AX.X).then_inc(dve_done, 1), "mks", l)
            dve.wait_ge(act_done, at("mkr", l))
            dve(nc.vector.tensor_tensor(k, k, bc(E["kr"].rearrange("p (i h) -> p i h", i=2), 3, HD), ALU.mult).then_inc(dve_done, 1))
            dve(nc.vector.tensor_tensor(k, k, bc(bc(Q("mkg"), 1, NH), 1, 2), ALU.mult).then_inc(dve_done, 1), "mkn", l)
            dve.wait_ge(pe_done, at("full", "mkt", l))
            ps = bank("mkt", l)
            dve(nc.vector.tensor_copy(MKT, ps[:, :].rearrange("p (i c) -> p i c", i=2)).then_inc(dve_done, 1), "MKT", l)
            dve.free("mkt", l)

        def act_memkv(act, l):
            act.wait_ge(dve_done, at("mks", l))
            act(nc.scalar.activation(E["kr"], E["ks"], ACT.Ln, bias=eps, scale=1.0 / HD).then_inc(act_done, 1))
            act(nc.scalar.activation(E["kr"], E["kr"], ACT.Exp, scale=-0.5).then_inc(act_done, 1), "mkr", l)

        KC = Xf[:, 0:1056]
        VC = Xf[:, 1056:2080].rearrange("p (b c) -> p b c", b=DB)
        HIDD = Xf[:, 2080:4128].rearrange("p (q c m) -> p q c m", q=4, c=2)
        TMP = Xf[:, 4128:4640]

        def pe_project_tm(pe, l, name):
            pe.wait_ge(dve_done, at("hT", l, 4, 1))
            pe.wait_ge(sem_of_slot("w", l, name), at("here", "w", l, name))
            w = coff[name][1]
            ws = slot("w", l, name)[:, 0:KT * w].rearrange("p (k c) -> p k c", k=KT)
            for i in range(TILES):
                ps = pe.open(name, l, i)
                for k in range(KT):
                    last = nc.tensor.matmul(ps[0:rows(i), 0:w], hT[:, k, tok(i)], ws[:, k, :], start=(k == 0), stop=(k == KT - 1))
                pe.full(last.then_inc(pe_done, 1), name, l, i)
            pe.name("used", "w", l, name)

        def take_project_tm(L, l, name, dst, copy):
            w = coff[name][1]
            for i in range(TILES):
                L.wait_ge(pe_done, at("full", name, l, i))
                ps = bank(name, l, i)
                L(copy(dst[0:rows(i), i, 0:w], ps[0:rows(i), 0:w]).then_inc(L.done, 1))
                L.free(name, l, i)
            L.name("P" + name, l)

        def pe_project_fm(pe, l, name):
            pe.wait_ge(dve_done, at("hT", l, 4, 1))
            pe.wait_ge(sem_of_slot("w", l, name), at("here", "w", l, name))
            w = coff[name][1]
            ws = slot("w", l, name)[:, 0:KT * w].rearrange("p (k c) -> p k c", k=KT)
            nf = w // 128
            for f in range(nf):
                ps = pe.open(name, l, f)
                for k in range(KT):
                    last = nc.tensor.matmul(ps[:, :], ws[:, k, 128 * f:128 * f + 128], hT[:, k, 0:SEQ], start=(k == 0), stop=(k == KT - 1))
                pe.full(last.then_inc(pe_done, 1), name, l, f)
            ps = pe.open(name, l, "d")
            for f in range(nf):
                for k in range(KT):
                    last = nc.tensor.matmul(ps[:, DTOK * f:DTOK * f + DTOK], ws[:, k, 128 * f:128 * f + 128], hT[:, k, SEQ:NT],
                                            start=(k == 0), stop=(k == KT - 1))
            pe.full(last.then_inc(pe_done, 1), name, l, "d")
            pe.name("used", "w", l, name)

        def pe_yT(pe, l, src, t0):
            pe.wait_ge(dve_done, at("y", l, t0))
            for f in range(2):
                ps = pe.open("yt", l, t0 + f, 0)
                for i in range(4):
                    last = nc.tensor.transpose(ps[:, tok(i)], src[:, i, 128 * f:128 * f + 128], idn)
                pe.full(last.then_inc(pe_done, 1), "yt", l, t0 + f, 0)
            ps = pe.open("yt", l, t0, 1)
            for f in range(2):
                last = nc.tensor.transpose(ps[:, DTOK * f:DTOK * f + DTOK], src[0:DTOK, 4, 128 * f:128 * f + 128], idn[0:DTOK, 0:DTOK])
            pe.full(last.then_inc(pe_done, 1), "yt", l, t0, 1)

        def dve_yT(dve, l, t0):
            for f in range(2):
                dve.wait_ge(pe_done, at("full", "yt", l, t0 + f, 0))
                ps = bank("yt", l, t0 + f, 0)
                dve(nc.vector.tensor_copy(YT[:, t0 + f, 0:SEQ], ps[:, :]).then_inc(dve_done, 1))
                dve.free("yt", l, t0 + f, 0)
            dve.wait_ge(pe_done, at("full", "yt", l, t0, 1))
            ps = bank("yt", l, t0, 1)
            dve(nc.vector.tensor_copy(YT[:, t0:t0 + 2, SEQ:NT], ps[:, 0:2 * DTOK].rearrange("p (f t) -> p f t", f=2)).then_inc(dve_done, 1), "YT", l, t0)
            dve.free("yt", l, t0, 1)

        def barrier(L, prev):
            for who in ("pe", "dve", "act", "pool"):
                if (who, *prev) in plan.at:
                    L.wait_ge(done[who], at(who, *prev))

        def phase_end(L, *ph):
            L.name(L.key, *ph)

        cv = Carve()
        XE = cv(4 * 515).rearrange("p (f t) -> p f t", f=4)
        XD = cv(4 * 56).rearrange("p (f b t) -> p f b t", f=4, b=DB)
        QK = cv(4 * NT).rearrange("p (f t) -> p f t", f=4)
        PM = cv(TILES * 776).rearrange("p (i c) -> p i c", i=TILES)
        Ktok = cv(TILES * 256).rearrange("p (i c) -> p i c", i=TILES)
        VX = cv(TILES * 260).rearrange("p (i h e) -> p i h e", i=TILES, h=NH)
        EJ = [cv(1280), cv(1280)]
        EOFF = [0, 512, 896, 1152]
        KW = cv(1024).rearrange("p (j c) -> p j c", j=4)
        HH = cv(TILES * 256).rearrange("p (i c) -> p i c", i=TILES)
        HSQ = EJ[0]
        gx, gax, LF, LI, Bt, AA, Mt, EM, DEN, hss, hrs = (cv(20).rearrange("p (i h) -> p i h", i=TILES) for _ in range(11))
        R = [cv(768), cv(768)]
        RD = cv(40).rearrange("p (b t) -> p b t", b=8)
        MDc, WIr, = (cv(32).rearrange("p (b t) -> p b t", b=8) for _ in range(2))
        WIt, WKD, dtmp = cv(4), cv(4), cv(4)
        ED, EDt = (EJ[1][:, o:o + 128].rearrange("p (h t) -> p h t", h=4) for o in (768, 896))
        KWD = EJ[1][:, 512:768].rearrange("p (h d) -> p h d", h=4)
        QCs = cv(64)
        QNp = cv(64).rearrange("p (f b t) -> p f b t", f=2, b=8)
        VXe = EJ[1][:, 0:512].rearrange("p (b e) -> p b e", b=8)
        C0 = cv(1024).rearrange("p (f b e) -> p f b e", f=2, b=8)
        n0, Nn, DCs = (cv(16).rearrange("p (f b) -> p f b", f=2) for _ in range(3))
        CP = cv(130).rearrange("p (f e) -> p f e", f=2)
        m0 = cv(8)
        CI = cv(96).rearrange("p (f b t) -> p f b t", f=4, b=8)
        CS = cv(108).rearrange("p (f b t) -> p f b t", f=4, b=9)

        def pool_m(pool, l):
            barrier(pool, ("E", l))
            pool.dma(f"stE{l}", pool.eng.dma_start(io["mem"][l], MKV).then_inc(stored["E"][l], 16), "stE", l)
            pool.dma(f"ldM{l}", pool.eng.dma_start(CI, io["mconv0"][l]).then_inc(loaded["M"][l], 16))
            pool.dma(f"ldM{l}", pool.eng.dma_start(C0, io["mC0"][l]).then_inc(loaded["M"][l], 16))
            pool.dma(f"ldM{l}", pool.eng.dma_start(n0, io["mn0"][l]).then_inc(loaded["M"][l], 16))
            pool.dma(f"ldM{l}", pool.eng.dma_start(m0[0:4], io["mm0"][l]).then_inc(loaded["M"][l], 16), "ldM", l)
            pool.wait_ge(dve_done, at("CS", l))
            pool.dma(f"stM{l}", pool.eng.dma_start(io["mconv"][l], CS).then_inc(stored["M"][l], 16))
            pool.wait_ge(dve_done, at("CP", l))
            pool.dma(f"stM{l}", pool.eng.dma_start(io["mC"][l], CP).then_inc(stored["M"][l], 16))
            pool.dma(f"stM{l}", pool.eng.dma_start(io["mm"][l], Mt).then_inc(stored["M"][l], 16))
            pool.wait_ge(dve_done, at("Cn", l))
            pool.dma(f"stM{l}", pool.eng.dma_start(io["mCd"][l], C0).then_inc(stored["M"][l], 16))
            pool.dma(f"stM{l}", pool.eng.dma_start(io["mnd"][l], Nn).then_inc(stored["M"][l], 16), "stM", l)

        def pe_m(pe, l):
            pe_project_fm(pe, l, "F0")
            pe_project_tm(pe, l, "T0")
            pe_project_tm(pe, l, "T1")
            pe.wait_ge(dve_done, at("LF", l))
            ps = pe.open("cb", l)
            nc.tensor.matmul(ps[0:32, 16:20], C("IUd", 32), LF[0:32, 4, :], start=True, stop=True)
            nc.tensor.matmul(ps[:, 0:16], C("tri"), LF[:, 0:4, :], start=True, stop=False)
            for j in range(3):
                last = nc.tensor.matmul(ps[:, 4 * (j + 1):16], C("ones"), bc(LF[:, j, :], 1, 3 - j), start=False, stop=(j == 2))
            pe.full(last.then_inc(pe_done, 1), "cb", l)
            pe.wait_ge(dve_done, at("AA", l))
            ps = pe.open("at", l)
            for i in range(4):
                last = nc.tensor.transpose(ps[0:4, tok(i)], AA[:, i, :], idn)
            pe.full(last.then_inc(pe_done, 1), "at", l)
            ps = pe.open("ad", l)
            pe.full(nc.tensor.transpose(ps[0:4, 0:32], AA[0:32, 4, :], idn[0:32, 0:32]).then_inc(pe_done, 1), "ad", l)
            pe.wait_ge(dve_done, at("qk", l))
            for f in range(2):
                ps = pe.open("kt", l, f)
                for i in range(4):
                    last = nc.tensor.transpose(ps[:, tok(i)], QK[:, 2 + f, tok(i)], idn)
                pe.full(last.then_inc(pe_done, 1), "kt", l, f)
            ps = pe.open("kt", l, 2)
            for f in range(2):
                last = nc.tensor.transpose(ps[0:32, 128 * f:128 * f + 128], QK[:, 2 + f, SEQ:NT], idn)
            pe.full(last.then_inc(pe_done, 1), "kt", l, 2)
            pe.wait_ge(loaded["M"][l], at("ldM", l))
            pe.wait_ge(dve_done, at("QNp", l))
            ps = pe.open("qc", l)
            for h in range(NH):
                hh, hp = h % 2, h // 2
                for b in range(DB):
                    o = 32 * hp + 4 * b
                    last = nc.tensor.matmul(ps[64 * hh:64 * hh + 64, o:o + 4], C0[64 * hh:64 * hh + 64, hp, b, :],
                                            QK[64 * hh:64 * hh + 64, hp, SEQ + 4 * b:SEQ + 4 * b + 4], start=True, stop=True)
            pe.full(last.then_inc(pe_done, 1), "qc", l)
            ps = pe.open("qn", l)
            for hp in range(2):
                last = nc.tensor.matmul(ps[0:32, 2 * hp:2 * hp + 2], QNp[:, hp, :, :], C("onesbd")[:, 0:128:64], start=True, stop=True)
            pe.full(last.then_inc(pe_done, 1), "qn", l)
            pe.wait_ge(dve_done, at("QCs", l))
            ps = pe.open("qct", l)
            for hp in range(2):
                last = nc.tensor.transpose(ps[0:32, 128 * hp:128 * hp + 128], QCs[:, 32 * hp:32 * hp + 32], idn)
            pe.full(last.then_inc(pe_done, 1), "qct", l)
            pe.wait_ge(dve_done, at("Mrow", l))
            pe.wait_ge(act_done, at("WIr", l))
            ps = pe.open("mt", l)
            for i in range(4):
                nc.tensor.transpose(ps[:, 4 * i:4 * i + 4], R[1][0:4, 256 + 128 * i:384 + 128 * i], idn[0:4, 0:4])
            nc.tensor.transpose(ps[0:32, 16:20], MDc[0:4], idn[0:4, 0:4])
            pe.full(nc.tensor.transpose(ps[0:32, 20:24], WIr[0:4], idn[0:4, 0:4]).then_inc(pe_done, 1), "mt", l)
            ps = pe.open("md", l)
            for h in range(NH):
                last = nc.tensor.matmul(ps[0:32, 32 * h:32 * h + 32], selh(h, 32), MDc[0:4], start=True, stop=True)
            pe.full(last.then_inc(pe_done, 1), "md", l)
            ps = pe.open("sd", l)
            for h in (0, 2, 1, 3):
                hs = slice(64 * (h % 2), 64 * (h % 2) + 64)
                if h == 1:
                    pe.fence(last.then_inc(pe_done, 1))
                last = nc.tensor.matmul(ps[0:32, 32 * h:32 * h + 32], QK[hs, 2 + h // 2, SEQ:NT], QK[hs, h // 2, SEQ:NT], start=True, stop=True)
            pe.full(last.then_inc(pe_done, 1), "sd", l)
            ps = pe.open("dc", l)
            for h in range(NH):
                hs = slice(64 * (h % 2), 64 * (h % 2) + 64)
                last = nc.tensor.matmul(ps[hs, 8 * (h // 2):8 * (h // 2) + 8], selh(h, 64), WIr[0:4, :, 3], start=True, stop=True)
            pe.full(last.then_inc(pe_done, 1), "dc", l)
            pe.wait_ge(dve_done, at("ED", l))
            ps = pe.open("pd", l)
            for h in range(NH):
                last = nc.tensor.matmul(ps[0:32, 65 * h:65 * h + 65], ED[0:32, h, :], VX[0:32, 4, h, :], start=True, stop=True)
            pe.full(last.then_inc(pe_done, 1), "pd", l)
            ps = pe.open("nu", l)
            for h in range(NH):
                hs = slice(64 * (h % 2), 64 * (h % 2) + 64)
                last = nc.tensor.matmul(ps[hs, 8 * (h // 2):8 * (h // 2) + 8], KWD[0:32, h, :], C("chD", 32), start=True, stop=True)
            pe.full(last.then_inc(pe_done, 1), "nu", l)
            for h in range(NH):
                hs = slice(64 * (h % 2), 64 * (h % 2) + 64)
                pe.wait_ge(dve_done, at("VXe", l, h))
                if h % 2 == 0:
                    ps = pe.open("cu", l, h // 2)
                last = nc.tensor.matmul(ps[hs, :], KWD[0:32, h, :], VXe[0:32], start=True, stop=True)
                pe(last.then_inc(pe_done, 1), "cuh", l, h)
                if h % 2:
                    pe.name("full", "cu", l, h // 2)
            cf = None
            for h in range(NH):
                hs = slice(64 * (h % 2), 64 * (h % 2) + 64)
                for hn in ((0, 1) if h == 0 else (h + 1,)):
                    if hn < NH:
                        ps = pe.open("mb", l, hn)
                        pe.full(nc.tensor.matmul(ps[:, :], selh(hn, 128), R[1][0:4, 256:768], start=True, stop=True).then_inc(pe_done, 1), "mb", l, hn)
                for j in range(4):
                    ps = pe.open("st", l, h, j)
                    pe.full(nc.tensor.matmul(ps[:, 0:512 - 128 * j], QK[hs, 2 + h // 2, tok(j)], QK[hs, h // 2, 128 * j:SEQ], start=True, stop=True).then_inc(pe_done, 1),
                           "st", l, h, j)
                pe.wait_ge(dve_done, at("PJ", l, h))
                ps = pe.open("pv", l, h)
                for i in range(4):
                    for j in range(i + 1):
                        o = EOFF[j] + 128 * (i - j)
                        last = nc.tensor.matmul(ps[:, 65 * i:65 * i + 65], EJ[h % 2][:, o:o + 128], VX[:, j, h, :], start=(j == 0), stop=(j == i))
                pe.full(last.then_inc(pe_done, 1), "pv", l, h)
            ps = pe.open("cf", l)
            for h in range(NH):
                hs = slice(64 * (h % 2), 64 * (h % 2) + 64)
                for j in range(4):
                    last = nc.tensor.matmul(ps[hs, 65 * (h // 2):65 * (h // 2) + 65], KW[:, j, 64 * h:64 * h + 64], VX[:, j, h, :],
                                            start=(j == 0), stop=(j == 3))
            pe.full(last.then_inc(pe_done, 1), "cf", l)

        def pe_m_end(pe, l):
            pe_yT(pe, l, PM[:, :, 512:768], 0)
            phase_end(pe, "M", l)

        def act_m(act, l):
            barrier(act, ("E", l))
            take_project_tm(act, l, "T0", PM[:, :, 0:512], nc.scalar.copy)
            take_project_tm(act, l, "T1", PM[:, :, 512:776], nc.scalar.copy)
            act.wait_ge(dve_done, at("gax", l))
            act(nc.scalar.activation(gax, gax, ACT.Exp, scale=-1.0).then_inc(act_done, 1))
            act(nc.scalar.activation(gax, gax, ACT.Ln, bias=one_c).then_inc(act_done, 1), "gln", l)
            act.wait_ge(dve_done, at("mtails", l))
            act.wait_ge(dve_done, at("conv", l))
            act(nc.scalar.activation(QK[:, :, :], QK[:, :, :], ACT.Silu).then_inc(act_done, 1), "silu", l)
            act(nc.scalar.activation(PM[:, :, 512:768], PM[:, :, 512:768], ACT.Silu).then_inc(act_done, 1))
            act(nc.scalar.activation(PM[:, :, 256:512], PM[:, :, 256:512], ACT.Tanh, scale=0.5).then_inc(act_done, 1), "ogz", l)
            act.wait_ge(dve_done, at("WIx", l))
            act(nc.scalar.activation(WIr[0:4], WIr[0:4], ACT.Exp).then_inc(act_done, 1), "WIr", l)
            act.wait_ge(dve_done, at("Mt", l))
            act(nc.scalar.activation(EM, Mt, ACT.Exp, scale=-1.0).then_inc(act_done, 1), "EM", l)
            act.wait_ge(dve_done, at("EDx", l))
            act(nc.scalar.activation(ED[0:32], ED[0:32], ACT.Exp, scale=-1.0).then_inc(act_done, 1), "EDe", l)
            for h in range(NH):
                act.wait_ge(dve_done, at("EJx", l, h))
                act(nc.scalar.activation(EJ[h % 2], EJ[h % 2], ACT.Exp, scale=-1.0).then_inc(act_done, 1), "EJe", l, h)
            act.wait_ge(dve_done, at("hss", l))
            act(nc.scalar.activation(hrs, hss, ACT.Ln, bias=eps, scale=1.0 / HD).then_inc(act_done, 1))
            act(nc.scalar.activation(hrs, hrs, ACT.Exp, scale=-0.5).then_inc(act_done, 1), "hrs", l)
            phase_end(act, "M", l)

        def dve_m(dve, l):
            barrier(dve, ("E", l))
            dve(nc.vector.memset(XE[:, :, 0:3], 0.0).then_inc(dve_done, 1))
            dve(nc.vector.memset(VX[:, :, :, 64:65], 1.0).then_inc(dve_done, 1))
            dve(nc.vector.memset(HH[:, 4, :], 0.0).then_inc(dve_done, 1))
            dve(nc.vector.memset(DEN[:, 4, :], 1.0).then_inc(dve_done, 1))
            dve(nc.vector.memset(Mt[:, 4, :], 0.0).then_inc(dve_done, 1))
            dve(nc.vector.memset(R[0][0:4, 0:256], NEG).then_inc(dve_done, 1))
            dve(nc.vector.memset(R[1][0:4, 0:256], NEG).then_inc(dve_done, 1))
            dve(nc.vector.memset(PM[:, 4, :], 0.0).then_inc(dve_done, 1), "mtails", l)
            dve.wait_ge(loaded["M"][l], at("ldM", l))
            dve(nc.vector.tensor_copy(XD[:, :, :, 0:3], CI).then_inc(dve_done, 1))
            dve(nc.vector.tensor_copy(RD[0:4, :, 0], m0[0:4]).then_inc(dve_done, 1))
            for f in range(4):
                dve.wait_ge(pe_done, at("full", "F0", l, f))
                ps = bank("F0", l, f)
                dve(nc.vector.tensor_copy(XE[:, f, 3:515], ps[:, :]).then_inc(dve_done, 1))
                dve.free("F0", l, f)
            dve.wait_ge(pe_done, at("full", "F0", l, "d"))
            ps = bank("F0", l, "d")
            dve(nc.vector.tensor_copy(XD[:, :, :, 3:7], ps[:, 0:128].rearrange("p (f b t) -> p f b t", f=4, b=DB)).then_inc(dve_done, 1))
            dve.free("F0", l, "d")
            cw = Q("cw").rearrange("p (f j) -> p f j", f=4)
            for f in range(4):
                for src, dst in ((lambda j: XE[:, f, j:j + SEQ], QK[:, f, 0:SEQ]),
                                 (lambda j: XD[:, f, :, j:j + DS], QK[:, f, SEQ:NT].rearrange("p (b t) -> p b t", b=DB))):
                    dve(nc.vector.tensor_scalar(dst, src(0), cw[:, f, 0:1], Q("cb")[:, f:f + 1], ALU.mult, ALU.add).then_inc(dve_done, 1))
                    for j in range(1, 4):
                        dve(nc.vector.scalar_tensor_tensor(dst, src(j), cw[:, f, j:j + 1], dst, ALU.mult, ALU.add).then_inc(dve_done, 1))
            dve.name("conv", l)
            dve(nc.vector.tensor_copy(CS[:, :, 0, :], XE[:, :, 512:515]).then_inc(dve_done, 1))
            dve(nc.vector.tensor_copy(CS[:, :, 1:9, :], XD[:, :, :, 4:7]).then_inc(dve_done, 1), "CS", l)
            dve.wait_ge(act_done, at("PT1", l))
            dve.wait_ge(act_done, at("PT0", l))
            dve(nc.vector.tensor_tensor(gx, PM[:, :, 772:776], bc(Q("gb")[:, 4:8], 1, TILES), ALU.add).then_inc(dve_done, 1))
            dve(nc.vector.scalar_tensor_tensor(gax, gx, -1.0, gx, ALU.mult, ALU.max).then_inc(dve_done, 1), "gax", l)
            dve(nc.vector.tensor_tensor(LI, PM[:, :, 768:772], bc(Q("gb")[:, 0:4], 1, TILES), ALU.add).then_inc(dve_done, 1))
            dve.wait_ge(act_done, at("gln", l))
            dve(nc.vector.scalar_tensor_tensor(LF, gx, 0.0, gax, ALU.min, ALU.subtract).then_inc(dve_done, 1), "LF", l)
            dve.wait_ge(pe_done, at("full", "cb", l))
            ps = bank("cb", l)
            dve(nc.vector.tensor_copy(Bt[:, 0:4, :], ps[:, 0:16].rearrange("p (i h) -> p i h", i=4)).then_inc(dve_done, 1))
            dve(nc.vector.memset(Bt[:, 4, :], 0.0).then_inc(dve_done, 1))
            dve(nc.vector.tensor_copy(Bt[0:32, 4, :], ps[0:32, 16:20]).then_inc(dve_done, 1))
            dve.free("cb", l)
            dve(nc.vector.tensor_tensor(AA, LI, Bt, ALU.subtract).then_inc(dve_done, 1), "AA", l)
            dve.wait_ge(pe_done, at("full", "at", l))
            ps = bank("at", l)
            dve(nc.vector.tensor_copy(R[0][0:4, 256:768], ps[0:4, :]).then_inc(dve_done, 1))
            dve.free("at", l)
            for n in range(9):
                k = 1 << n
                dve(nc.vector.tensor_tensor(R[(n + 1) % 2][0:4, 256:768], R[n % 2][0:4, 256:768], R[n % 2][0:4, 256 - k:768 - k], ALU.max).then_inc(dve_done, 1))
            dve.name("Mrow", l)
            dve.wait_ge(pe_done, at("full", "ad", l))
            ps = bank("ad", l)
            dve(nc.vector.tensor_copy(RD[0:4, :, 1:5], ps[0:4, 0:32].rearrange("p (b t) -> p b t", b=DB)).then_inc(dve_done, 1))
            dve.free("ad", l)
            for t in range(1, 5):
                dve(nc.vector.tensor_tensor(RD[0:4, :, t], RD[0:4, :, t - 1], RD[0:4, :, t], ALU.max).then_inc(dve_done, 1))
            dve(nc.vector.tensor_copy(MDc[0:4], RD[0:4, :, 1:5]).then_inc(dve_done, 1))
            dve(nc.vector.tensor_tensor(WIr[0:4], RD[0:4, :, 0:1].broadcast_to([4, 8, 4]), MDc[0:4], ALU.subtract).then_inc(dve_done, 1), "WIx", l)
            dve.wait_ge(act_done, at("silu", l))
            dve(nc.vector.tensor_scalar(QK[:, 0:2, :], QK[:, 0:2, :], SCALE, None, ALU.mult).then_inc(dve_done, 1), "qk", l)
            dve(nc.vector.tensor_tensor(QNp, QK[:, 0:2, SEQ:NT].rearrange("p f (b t) -> p f b t", b=DB), bc(n0, 3, DS), ALU.mult).then_inc(dve_done, 1), "QNp", l)
            dve(nc.vector.tensor_copy(VX[:, 0:4, :, 0:64], PM[:, 0:4, 0:256].rearrange("p i (h e) -> p i h e", h=NH)).then_inc(dve_done, 1))
            dve(nc.vector.tensor_copy(VX[0:32, 4, :, 0:64], PM[0:32, 4, 0:256].rearrange("p (h e) -> p h e", h=NH)).then_inc(dve_done, 1))
            for f in range(2):
                dve.wait_ge(pe_done, at("full", "kt", l, f))
                ps = bank("kt", l, f)
                dve(nc.vector.tensor_copy(Ktok[:, 0:4, 128 * f:128 * f + 128], ps[:, :].rearrange("p (i c) -> p i c", i=4)).then_inc(dve_done, 1))
                dve.free("kt", l, f)
            dve.wait_ge(pe_done, at("full", "kt", l, 2))
            ps = bank("kt", l, 2)
            dve(nc.vector.tensor_copy(Ktok[0:32, 4, :], ps[0:32, 0:256]).then_inc(dve_done, 1))
            dve.free("kt", l, 2)
            dve.wait_ge(pe_done, at("full", "qc", l))
            ps = bank("qc", l)
            dve(nc.vector.tensor_copy(QCs, ps[:, 0:64]).then_inc(dve_done, 1), "QCs", l)
            dve.free("qc", l)
            dve.wait_ge(pe_done, at("full", "mt", l))
            ps = bank("mt", l)
            dve(nc.vector.tensor_tensor(Mt[:, 0:4, :], Bt[:, 0:4, :], ps[:, 0:16].rearrange("p (i h) -> p i h", i=4), ALU.add).then_inc(dve_done, 1))
            dve(nc.vector.tensor_tensor(Mt[0:32, 4, :], Bt[0:32, 4, :], ps[0:32, 16:20], ALU.add).then_inc(dve_done, 1), "Mt", l)
            dve(nc.vector.tensor_copy(WIt[0:32], ps[0:32, 20:24]).then_inc(dve_done, 1))
            dve.free("mt", l)
            dve.wait_ge(pe_done, at("full", "md", l))
            ps = bank("md", l)
            dve(nc.vector.tensor_tensor(ED[0:32], ps[0:32, 0:128].rearrange("p (h t) -> p h t", h=NH), bc(AA[0:32, 4, :], 2, 32), ALU.subtract).then_inc(dve_done, 1))
            dve.free("md", l)
            dve(nc.vector.tensor_scalar(ED[0:32], ED[0:32], 0.0, None, ALU.max).then_inc(dve_done, 1), "EDx", l)
            dve.wait_ge(act_done, at("EDe", l))
            dve(nc.vector.tensor_tensor(ED[0:32], ED[0:32], bc(C("IUd", 32), 1, NH), ALU.mult).then_inc(dve_done, 1))
            dve(nc.vector.tensor_tensor(EDt[0:32], ED[0:32], bc(C("endsel", 32), 1, NH), ALU.mult).then_inc(dve_done, 1))
            dve(nc.vector.reduce_sum(WKD[0:32], EDt[0:32], axis=AX.X).then_inc(dve_done, 1))
            dve(nc.vector.tensor_tensor(KWD[0:32], Ktok[0:32, 4, :].rearrange("p (h d) -> p h d", h=NH), bc(WKD[0:32], 2, HD), ALU.mult).then_inc(dve_done, 1))
            dve.wait_ge(pe_done, at("full", "sd", l))
            ps = bank("sd", l)
            dve(nc.vector.tensor_tensor(ED[0:32], ED[0:32], ps[0:32, 0:128].rearrange("p (h t) -> p h t", h=NH), ALU.mult).then_inc(dve_done, 1), "ED", l)
            dve.free("sd", l)
            dve.wait_ge(pe_done, at("full", "dc", l))
            ps = bank("dc", l)
            dve(nc.vector.tensor_copy(DCs, ps[:, 0:16].rearrange("p (f b) -> p f b", f=2)).then_inc(dve_done, 1))
            dve.free("dc", l)
            dve.wait_ge(pe_done, at("full", "pd", l))
            pd = bank("pd", l)
            pdv = pd[0:32, 0:260].rearrange("p (h e) -> p h e", h=NH)
            hd = HH[0:32, 4, :].rearrange("p (h e) -> p h e", h=NH)
            dve.wait_ge(pe_done, at("full", "qct", l))
            qct = bank("qct", l)
            dve(nc.vector.tensor_tensor(hd, bc(WIt[0:32], 2, HD), qct[0:32, 0:256].rearrange("p (h e) -> p h e", h=NH), ALU.mult).then_inc(dve_done, 1))
            dve.free("qct", l)
            dve(nc.vector.tensor_tensor(hd, hd, pdv[:, :, 0:64], ALU.add).then_inc(dve_done, 1))
            dve.wait_ge(pe_done, at("full", "qn", l))
            qn = bank("qn", l)
            dve(nc.vector.tensor_tensor(dtmp[0:32], WIt[0:32], qn[0:32, 0:4], ALU.mult).then_inc(dve_done, 1))
            dve.free("qn", l)
            dve(nc.vector.tensor_tensor(DEN[0:32, 4, :], dtmp[0:32], pdv[:, :, 64], ALU.add).then_inc(dve_done, 1))
            dve.free("pd", l)
            dve.wait_ge(pe_done, at("full", "nu", l))
            ps = bank("nu", l)
            dve(nc.vector.tensor_tensor(Nn, n0, DCs, ALU.mult).then_inc(dve_done, 1))
            dve(nc.vector.tensor_tensor(Nn, Nn, ps[:, 0:16].rearrange("p (f b) -> p f b", f=2), ALU.add).then_inc(dve_done, 1))
            dve.free("nu", l)
            for h in range(NH):
                if h:
                    dve.wait_ge(pe_done, at("cuh", l, h - 1))
                dve(nc.vector.tensor_tensor(VXe[0:32], bc(VX[0:32, 4, h, 0:64], 1, DB), bc(C("chD", 32), 2, HD), ALU.mult).then_inc(dve_done, 1), "VXe", l, h)
            for hp in range(2):
                dve.wait_ge(pe_done, at("full", "cu", l, hp))
                ps = bank("cu", l, hp)
                dve(nc.vector.tensor_tensor(C0[:, hp], C0[:, hp], bc(DCs[:, hp, :], 2, HD), ALU.mult).then_inc(dve_done, 1))
                dve(nc.vector.tensor_tensor(C0[:, hp], C0[:, hp], ps[:, :].rearrange("p (b e) -> p b e", b=DB), ALU.add).then_inc(dve_done, 1), "Cn", l)
                dve.free("cu", l, hp)
            for h in range(NH):
                EE = EJ[h % 2]
                for hn in ((0, 1) if h == 0 else (h + 1,)):
                    if hn < NH:
                        dve.wait_ge(pe_done, at("full", "mb", l, hn))
                        ps = bank("mb", l, hn)
                        for j in range(4):
                            dve(nc.vector.tensor_scalar(EJ[hn % 2][:, EOFF[j]:EOFF[j] + 512 - 128 * j], ps[:, 128 * j:512], AA[:, j, hn:hn + 1],
                                                      0.0, ALU.subtract, ALU.max).then_inc(dve_done, 1))
                        dve.name("EJx", l, hn)
                        dve.free("mb", l, hn)
                dve.wait_ge(act_done, at("EJe", l, h))
                for j in range(4):
                    e = EE[:, EOFF[j]:EOFF[j] + 512 - 128 * j]
                    dve(nc.vector.tensor_scalar(KW[:, j, 64 * h:64 * h + 64], Ktok[:, j, 64 * h:64 * h + 64], e[:, 511 - 128 * j:512 - 128 * j],
                                              None, ALU.mult).then_inc(dve_done, 1))
                    dve.wait_ge(pe_done, at("full", "st", l, h, j))
                    ps = bank("st", l, h, j)
                    dve(nc.vector.tensor_tensor(e, e, ps[:, 0:512 - 128 * j], ALU.mult).then_inc(dve_done, 1))
                    dve.free("st", l, h, j)
                    dve(nc.vector.tensor_tensor(e[:, 0:128], e[:, 0:128], C("tri"), ALU.mult).then_inc(dve_done, 1))
                dve.name("PJ", l, h)
                dve.wait_ge(pe_done, at("full", "pv", l, h))
                pv = bank("pv", l, h)
                pvv = pv[:, 0:260].rearrange("p (i e) -> p i e", i=4)
                dve(nc.vector.tensor_copy(HH[:, 0:4, 64 * h:64 * h + 64], pvv[:, :, 0:64]).then_inc(dve_done, 1))
                dve(nc.vector.tensor_copy(DEN[:, 0:4, h:h + 1], pvv[:, :, 64:65]).then_inc(dve_done, 1))
                dve.free("pv", l, h)
            dve.wait_ge(pe_done, at("full", "cf", l))
            ps = bank("cf", l)
            dve(nc.vector.tensor_copy(CP, ps[:, 0:130].rearrange("p (f e) -> p f e", f=2)).then_inc(dve_done, 1), "CP", l)
            dve.free("cf", l)
            dve.wait_ge(act_done, at("EM", l))
            dve(nc.vector.scalar_tensor_tensor(DEN, DEN, -1.0, DEN, ALU.mult, ALU.max).then_inc(dve_done, 1))
            dve(nc.vector.tensor_tensor(DEN, DEN, EM, ALU.max).then_inc(dve_done, 1))
            dve(nc.vector.reciprocal(DEN, DEN).then_inc(dve_done, 1))
            H20 = HH.rearrange("p i (h e) -> p (i h) e", h=NH)
            dve(nc.vector.tensor_tensor(H20, H20, bc(DEN.rearrange("p i h -> p (i h)"), 2, HD), ALU.mult).then_inc(dve_done, 1))
            dve(nc.vector.tensor_tensor(HSQ.rearrange("p (i c) -> p i c", i=TILES), HH, HH, ALU.mult).then_inc(dve_done, 1))
            dve(nc.vector.reduce_sum(hss, HSQ.rearrange("p (i h e) -> p i h e", i=TILES, h=NH), axis=AX.X).then_inc(dve_done, 1), "hss", l)
            dve.wait_ge(act_done, at("hrs", l))
            dve(nc.vector.tensor_tensor(H20, H20, bc(hrs.rearrange("p i h -> p (i h)"), 2, HD), ALU.mult).then_inc(dve_done, 1))
            dve(nc.vector.tensor_tensor(HH, HH, bc(Q("mlg"), 1, TILES), ALU.mult).then_inc(dve_done, 1))
            dve.wait_ge(act_done, at("ogz", l))
            dve(nc.vector.scalar_tensor_tensor(HH, PM[:, :, 256:512], 1.0, HH, ALU.add, ALU.mult).then_inc(dve_done, 1))
            dve(nc.vector.scalar_tensor_tensor(PM[:, :, 512:768], HH, 0.5, PM[:, :, 512:768], ALU.mult, ALU.mult).then_inc(dve_done, 1), "y", l, 0)
            dve_yT(dve, l, 0)
            phase_end(dve, "M", l)

        cv = Carve()
        UX = cv(NRT * 513).rearrange("p (f t) -> p f t", f=NRT)
        UD = cv(NRT * 40).rearrange("p (f b t) -> p f b t", f=NRT, b=DB)
        UC = cv(NRT * 32).rearrange("p (f t) -> p f t", f=NRT)
        SHI = cv(NRT * 8).rearrange("p (f b) -> p f b", f=NRT)
        SHO = cv(NRT * 9).rearrange("p (f b) -> p f b", f=NRT)
        LW, AG = (cv(2 * NT).rearrange("p (f t) -> p f t", f=2) for _ in range(2))
        DTm = cv(512)
        YR = cv(TILES * 256).rearrange("p (i c) -> p i c", i=TILES)
        BN, s20, v20 = cv(4), cv(20), cv(20)
        HWA = cv(4)
        G14 = cv(14 * 256)
        Cc, E1, E2, E3, E4, KK, KE, Bv, RT_, KH, TQ, RX, YY, YF = (G14[:, 256 * i:256 * i + 256].rearrange("p (f t) -> p f t", f=2) for i in range(14))
        SQ5 = G14[:, 0:1280]
        NRM = YT[:, 6:8, :]
        BNV = YTf[:, 2 * NT:2 * NT + 1280].rearrange("p (i c) -> p i c", i=TILES)
        LWT = cv(256)
        TOK = cv(768).rearrange("p (a c) -> p a c", a=3)
        NNb = cv(2048)
        Nb = [NNb[:, 512 * i:512 * i + 512].rearrange("p (h t) -> p h t", h=NH) for i in range(2)]
        Tb = [NNb[:, 1024 + 512 * i:1536 + 512 * i].rearrange("p (h t) -> p h t", h=NH) for i in range(2)]
        GT, HT_, Zb = (cv(512).rearrange("p (h t) -> p h t", h=NH) for _ in range(3))
        MT = cv(512)
        MTc = MT.rearrange("p (c f k) -> p c f k", c=4, f=2)
        MTd = MT.rearrange("p (c k) -> p c k", c=8)
        WTb = MT.rearrange("p (h t) -> p h t", h=NH)
        ZS = cv(512)
        ZSc = ZS.rearrange("p (c k) -> p c k", c=4)
        ZSd = ZS.rearrange("p (c k) -> p c k", c=8)
        STt = cv(5 * 128).rearrange("p (c k) -> p c k", c=5)
        SD = cv(8 * 128).rearrange("p (b k) -> p b k", b=DB)
        BhE, VE, YE = (NNb[:, 512 * i:512 * i + 512].rearrange("p (c k) -> p c k", c=8) for i in range(3))
        RZ = NNb[:, 0:1280].rearrange("p (i c) -> p i c", i=TILES)

        def um(m, f, ps=slice(0, 128)):
            return UX[ps, f, 1 + 128 * m:129 + 128 * m] if m < 4 else UC[ps, f, :]

        def levels(m):
            return 5 if m < 4 else 2

        def hsl(h):
            return slice(64 * (h % 2), 64 * (h % 2) + 64)

        def pool_r(pool, l):
            barrier(pool, ("M", l))
            pool.wait_ge(stored["M"][l], at("stM", l))
            pool.dma(f"ldR{l}", pool.eng.dma_start(SHI, io["rsh0"][l]).then_inc(loaded["R"][l], 16))
            pool.dma(f"ldR{l}", pool.eng.dma_start(SD, io["rS0"][l]).then_inc(loaded["R"][l], 16), "ldR", l)
            pool.wait_ge(dve_done, at("SHO", l))
            pool.dma(f"stR{l}", pool.eng.dma_start(io["rsh"][l], SHO).then_inc(stored["R"][l], 16))
            pool.wait_ge(dve_done, at("SDn", l))
            pool.dma(f"stR{l}", pool.eng.dma_start(io["rS"][l, :, 8, :], STt[:, 4, :]).then_inc(stored["R"][l], 16))
            pool.dma(f"stR{l}", pool.eng.dma_start(io["rS"][l, :, 0:8, :], SD).then_inc(stored["R"][l], 16), "stR", l)

        def pe_r(pe, l):
            pe_project_fm(pe, l, "F1")
            pe_m_end(pe, l)
            pe_project_fm(pe, l, "F2")
            pe.wait_ge(dve_done, at("kk2", l))
            for f in range(3):
                ps = pe.open("ns", l, f)
                src, w = (NRM[:, f, 0:SEQ], SEQ) if f < 2 else (NRM[:, :, SEQ:NT], 2 * DTOK)
                pe.full(nc.tensor.matmul(ps[:, 0:w], C("onesbd"), src, start=True, stop=True).then_inc(pe_done, 1), "ns", l, f)
            pe.wait_ge(act_done, at("tanhw", l))
            lora = Q("lora")
            for key, ps_, in (("lw", slice(0, 64)), ("la", slice(64, 128))):
                for f in range(2):
                    ps = pe.open(key, l, f)
                    pe.full(nc.tensor.matmul(ps[:, :], lora[ps_, 128 * f:128 * f + 128], UX[ps_, 6, 1:513], start=True, stop=True).then_inc(pe_done, 1), key, l, f)
                ps = pe.open(key, l, "d")
                for f in range(2):
                    last = nc.tensor.matmul(ps[:, 32 * f:32 * f + 32], lora[ps_, 128 * f:128 * f + 128], UC[ps_, 6, :], start=True, stop=True)
                pe.full(last.then_inc(pe_done, 1), key, l, "d")
            for m in range(TILES):
                pe_r_block(pe, l, m)
            pe_project_tm(pe, l, "T2")

        def pe_r_end(pe, l):
            pe_yT(pe, l, YR, 4)
            phase_end(pe, "R", l)

        def pe_compress(pe, l, b):
            w1p = Q("w1p").rearrange("p (c j e) -> p c j e", c=2, j=8)
            pe.wait_ge(sem_of_slot("cmp", l, b), at("here", "cmp", l, b))
            cs = slot("cmp", l, b).rearrange("p (g j c m) -> p g j c m", g=NPAGE, j=8, c=2)
            ps = pe.open("ab", l, b)
            for c in range(2):
                for j in range(8):
                    last = nc.tensor.matmul(ps[:, 256 * c:256 * c + 256], w1p[:, c, j, :], cs[:, :, j, c, :], start=(j == 0), stop=(j == 7))
            pe.full(last.then_inc(pe_done, 1), "ab", l, b)
            pe.name("used", "cmp", l, b)

        def dve_compress(dve, l, b):
            dve.wait_ge(pe_done, at("full", "ab", l, b))
            ps = bank("ab", l, b)
            pv = ps[:, :].rearrange("p (c m) -> p c m", c=2)
            t = TMP.rearrange("p (c m) -> p c m", c=2)
            if b % 2 == 0:
                lo = slice(0, 64)
                dve(nc.vector.tensor_copy(t[lo], pv[64:128]).then_inc(dve_done, 1))
                dve(nc.vector.tensor_tensor(HIDD[lo, b // 2, :, 0:254], pv[lo, :, 0:254], t[lo, :, 2:256], ALU.add).then_inc(dve_done, 1), "HID", l, b)
            else:
                hi = slice(64, 128)
                dve(nc.vector.tensor_copy(t[hi], pv[0:64]).then_inc(dve_done, 1))
                dve(nc.vector.tensor_tensor(HIDD[hi, b // 2, :, 0:254], pv[hi, :, 2:256], t[hi, :, 0:254], ALU.add).then_inc(dve_done, 1), "HID", l, b)
            dve.free("ab", l, b)

        def pe_r_block(pe, l, m):
            n = rows(m)
            pe.wait_ge(dve_done, at("LW", l))
            ps = pe.open("lt", l, m)
            for f in range(2):
                last = nc.tensor.transpose(ps[0:n, 128 * f:128 * f + 128], LW[:, f, tok(m)], idn)
            pe.full(last.then_inc(pe_done, 1), "lt", l, m)
            pe.wait_ge(dve_done, at("LWT", l, m))
            ps = pe.open("cc", l, m)
            for f in range(2):
                last = nc.tensor.matmul(ps[:, n * f:n * f + n], LWT[0:n, 128 * f:128 * f + 128], C("IU") if m < 4 else C("IUd", 32), start=True, stop=True)
            pe.full(last.then_inc(pe_done, 1), "cc", l, m)
            if m < 4:
                pe_compress(pe, l, 2 * m)
            pe.wait_ge(dve_done, at("fm", l, m))
            for key, srcs in (("t1", (E4, KH)), ("t2", (None, E1))):
                ps = pe.open(key, l, m)
                for a, s in enumerate(srcs):
                    for f in range(2):
                        o = 256 * a + 128 * f
                        src = s[:, f, 0:n] if s is not None else um(m, 4 + f)
                        last = nc.tensor.transpose(ps[0:n, o:o + 128], src, idn)
                pe.full(last.then_inc(pe_done, 1), key, l, m)
            ps = pe.open("bn", l, m)
            for f in range(2):
                last = nc.tensor.matmul(ps[0:n, 2 * f:2 * f + 2], TQ[:, f, 0:n], C("onesbd")[:, 0:128:64], start=True, stop=True)
            pe.full(last.then_inc(pe_done, 1), "bn", l, m)
            pairs = (("pN", E1, E2), ("pT", E2, E1), ("pW", Cc, E1), ("pG", E2, RT_), ("pH", Cc, RT_))
            bank = [pe.open(key, l, m) for key, _, _ in pairs]
            for odd in range(2):
                for (key, a, b), ps in zip(pairs, bank):
                    for hp in range(2):
                        o = n * (2 * hp + odd)
                        last = nc.tensor.matmul(ps[0:n, o:o + n], a[hsl(odd), hp, 0:n], b[hsl(odd), hp, 0:n], start=True, stop=True)
                    if odd:
                        pe.full(last.then_inc(pe_done, 1), key, l, m)
                if not odd:
                    pe.fence(last.then_inc(pe_done, 1))
            pe.wait_ge(dve_done, at("WT", l, m))
            ps = pe.open("wv", l, m)
            for h in range(NH):
                last = nc.tensor.matmul(ps[0:n, 64 * h:64 * h + 64], WTb[0:n, h, 0:n], TOK[0:n, 2, 64 * h:64 * h + 64], start=True, stop=True)
            pe.full(last.then_inc(pe_done, 1), "wv", l, m)
            for lev in range(levels(m)):
                Nl, Tl = Nb[lev % 2], Tb[lev % 2]
                pe.wait_ge(dve_done, at("Nlev", l, m, lev))
                if 0 < lev < levels(m) - 1:
                    pe.wait_ge(act_done, at("Nsq", l, m, lev))
                if lev < levels(m) - 1:
                    if lev < levels(m) - 2:
                        ps = pe.open("sq", l, m, lev)
                        for h in range(NH):
                            last = nc.tensor.matmul(ps[0:n, n * h:n * h + n], Tl[0:n, h, 0:n], Nl[0:n, h, 0:n], start=True, stop=True)
                        pe.full(last.then_inc(pe_done, 1), "sq", l, m, lev)
                    ps = pe.open("sqt", l, m, lev)
                    for h in range(NH):
                        last = nc.tensor.matmul(ps[0:n, n * h:n * h + n], Nl[0:n, h, 0:n], Tl[0:n, h, 0:n], start=True, stop=True)
                    pe.full(last.then_inc(pe_done, 1), "sqt", l, m, lev)
                pe.wait_ge(dve_done, at("Z", l, m, lev))
                ps = pe.open("za", l, m, lev)
                for h in range(NH):
                    last = nc.tensor.matmul(ps[0:n, 128 * h:128 * h + 128], Tl[0:n, h, 0:n], Zb[0:n, h, :], start=True, stop=True)
                pe.full(last.then_inc(pe_done, 1), "za", l, m, lev)
            pe.wait_ge(dve_done, at("Z", l, m, levels(m)))
            ps = pe.open("rx", l, m)
            for h in range(NH):
                last = nc.tensor.matmul(ps[hsl(h), n * (h // 2):n * (h // 2) + n], Zb[0:n, h, 0:64], GT[0:n, h, 0:n], start=True, stop=True)
            pe.full(last.then_inc(pe_done, 1), "rx", l, m)
            ps = pe.open("yy", l, m)
            for h in range(NH):
                o = ps[hsl(h), n * (h // 2):n * (h // 2) + n]
                nc.tensor.matmul(o, TOK[0:n, 2, 64 * h:64 * h + 64], HT_[0:n, h, 0:n], start=True, stop=False)
                last = nc.tensor.matmul(o, Zb[0:n, h, 64:128], GT[0:n, h, 0:n], start=False, stop=True)
            pe.full(last.then_inc(pe_done, 1), "yy", l, m)
            if m < 4:
                pe.wait_ge(act_done, at("TOKa", l, m))
                for c in range(4):
                    r = slice(32 * c, 32 * c + 32)
                    ps = pe.open("mc", l, m, c)
                    for h in range(NH):
                        o = 64 * (h // 2)
                        nc.tensor.matmul(ps[hsl(h), o:o + 64], Zb[r, h, 0:64], TOK[r, 0, 64 * h:64 * h + 64], start=True, stop=True)
                        o += 128
                        nc.tensor.matmul(ps[hsl(h), o:o + 64], TOK[r, 1, 64 * h:64 * h + 64], TOK[r, 2, 64 * h:64 * h + 64], start=True, stop=False)
                        last = nc.tensor.matmul(ps[hsl(h), o:o + 64], TOK[r, 0, 64 * h:64 * h + 64], Zb[r, h, 64:128], start=False, stop=True)
                    pe.full(last.then_inc(pe_done, 1), "mc", l, m, c)
                pe_compress(pe, l, 2 * m + 1)
                for c in range(4):
                    pe.wait_ge(dve_done, at("S", l, m, c))
                    ps = pe.open("sc", l, m, c)
                    for h in range(NH):
                        last = nc.tensor.matmul(ps[hsl(h), 64 * (h // 2):64 * (h // 2) + 64], MTc[hsl(h), c, h // 2, :],
                                                STt[hsl(h), c, 64 * (h // 2):64 * (h // 2) + 64], start=True, stop=True)
                    pe.full(last.then_inc(pe_done, 1), "sc", l, m, c)
            pe.wait_ge(dve_done, at("RX", l, m))
            pe.wait_ge(loaded["R"][l], at("ldR", l))
            ps = pe.open("yr", l, m)
            nch, cl = (4, 32) if m < 4 else (8, DS)
            Ssrc = STt if m < 4 else SD
            for h in range(NH):
                for c in range(nch):
                    o = n * (h // 2) + cl * c
                    last = nc.tensor.matmul(ps[hsl(h), o:o + cl], Ssrc[hsl(h), c, 64 * (h // 2):64 * (h // 2) + 64],
                                            RX[hsl(h), h // 2, cl * c:cl * c + cl], start=True, stop=True)
            pe.full(last.then_inc(pe_done, 1), "yr", l, m)
            if m == 4:
                pe.wait_ge(act_done, at("TOKa", l, m))
                for hp in range(2):
                    pm, pz = pe.open("md4", l, hp), pe.open("zd4", l, hp)
                    for hh in range(2):
                        h = 2 * hp + hh
                        pe.wait_ge(dve_done, at("exp", l, h))
                        nc.tensor.matmul(pm[hsl(h), :], Zb[0:32, h, 0:64], BhE[0:32], start=True, stop=True)
                        nc.tensor.matmul(pz[hsl(h), :], TOK[0:32, 1, 64 * h:64 * h + 64], VE[0:32], start=True, stop=False)
                        pe(nc.tensor.matmul(pz[hsl(h), :], TOK[0:32, 0, 64 * h:64 * h + 64], YE[0:32], start=False, stop=True).then_inc(pe_done, 1), "expu", l, h)
                    pe.name("full", "md4", l, hp)
                    pe.name("full", "zd4", l, hp)
                    pe.wait_ge(dve_done, at("MTd", l, hp))
                    ps = pe.open("sd4", l, hp)
                    for b in range(DB):
                        for hh in range(2):
                            last = nc.tensor.matmul(ps[hsl(hh), 64 * b:64 * b + 64], MTd[hsl(hh), b, :], SD[hsl(hh), b, 64 * hp:64 * hp + 64],
                                                    start=True, stop=True)
                    pe.full(last.then_inc(pe_done, 1), "sd4", l, hp)
            pe.wait_ge(dve_done, at("YF", l, m))
            ps = pe.open("yt2", l, m)
            for f in range(2):
                last = nc.tensor.transpose(ps[0:n, 128 * f:128 * f + 128], YF[:, f, 0:n], idn)
            pe.full(last.then_inc(pe_done, 1), "yt2", l, m)

        def act_r(act, l):
            barrier(act, ("M", l))
            act.wait_ge(dve_done, at("um6", l))
            act(nc.scalar.activation(UX[0:64, 6, 1:513], UX[0:64, 6, 1:513], ACT.Tanh).then_inc(act_done, 1))
            act(nc.scalar.activation(UC[0:64, 6, :], UC[0:64, 6, :], ACT.Tanh).then_inc(act_done, 1), "tanhw", l)
            for key, dst, o in (("lw", LW, 0), ("la", AG, 2)):
                for f in range(2):
                    act.wait_ge(pe_done, at("full", key, l, f))
                    ps = bank(key, l, f)
                    act(nc.scalar.activation(dst[:, f, 0:SEQ], ps[:, :], ACT.Tanh, bias=HWA[:, o + f:o + f + 1], scale=0.5).then_inc(act_done, 1))
                    act.free(key, l, f)
                act.wait_ge(pe_done, at("full", key, l, "d"))
                ps = bank(key, l, "d")
                for f in range(2):
                    act(nc.scalar.activation(dst[:, f, SEQ:NT], ps[:, 32 * f:32 * f + 32], ACT.Tanh, bias=HWA[:, o + f:o + f + 1], scale=0.5).then_inc(act_done, 1))
                act.free(key, l, "d")
                act.name("th" + key, l)
            act.wait_ge(dve_done, at("ss", l))
            act(nc.scalar.activation(NRM, NRM, ACT.Ln, scale=float(2 ** 20)).then_inc(act_done, 1))
            act(nc.scalar.activation(NRM, NRM, ACT.Exp, bias=ln2_10, scale=-0.5).then_inc(act_done, 1), "ri", l)
            for m in range(TILES):
                n = rows(m)
                act.wait_ge(dve_done, at("Ex", l, m))
                act(nc.scalar.activation(E1[:, :, 0:n], E1[:, :, 0:n], ACT.Exp).then_inc(act_done, 1), "E1", l, m)
                act(nc.scalar.activation(E2[:, :, 0:n], Cc[:, :, 0:n], ACT.Exp, scale=-1.0).then_inc(act_done, 1))
                act(nc.scalar.activation(E3[:, :, 0:n], Cc[:, :, 0:n], ACT.Exp).then_inc(act_done, 1))
                act(nc.scalar.activation(E4[:, :, 0:n], E4[:, :, 0:n], ACT.Exp).then_inc(act_done, 1), "E", l, m)
                act.wait_ge(pe_done, at("full", "t1", l, m))
                ps = bank("t1", l, m)
                act(nc.scalar.copy(TOK[0:n, 0:2, :], ps[0:n, :].rearrange("p (a c) -> p a c", a=2)).then_inc(act_done, 1), "TOKa", l, m)
                act.free("t1", l, m)
                for lev in range(levels(m) - 2):
                    act.wait_ge(pe_done, at("full", "sq", l, m, lev))
                    ps = bank("sq", l, m, lev)
                    act(nc.scalar.copy(Nb[(lev + 1) % 2][0:n, :, 0:n], ps[0:n, 0:4 * n].rearrange("p (h t) -> p h t", h=NH)).then_inc(act_done, 1), "Nsq", l, m, lev + 1)
                    act.free("sq", l, m, lev)
            act.wait_ge(dve_done, at("v20", l))
            act(nc.scalar.activation(v20, v20, ACT.Ln, bias=rweps, scale=1.0 / HD).then_inc(act_done, 1))
            act(nc.scalar.activation(v20, v20, ACT.Exp, scale=-0.5).then_inc(act_done, 1), "lnr", l)
            for i in range(TILES):
                act.wait_ge(pe_done, at("full", "T2", l, i))
                ps = bank("T2", l, i)
                if i == 0:
                    act.wait_ge(dve_done, at("rblocks", l))
                act(nc.scalar.activation(RZ[0:rows(i), i, :], ps[0:rows(i), 0:256], ACT.Silu).then_inc(act_done, 1))
                act.free("T2", l, i)
            act.name("RZ", l)
            phase_end(act, "R", l)

        def dve_r(dve, l):
            barrier(dve, ("M", l))
            dve.wait_ge(stored["M"][l], at("stM", l))
            dve(nc.vector.memset(UX[:, :, 0:1], 0.0).then_inc(dve_done, 1))
            if l:
                dve.wait_ge(y_kept[l], at("ys", l))
            dve(nc.vector.memset(HIDD, 0.0).then_inc(dve_done, 1))
            dve(nc.vector.memset(STt[:, 4, :], 0.0).then_inc(dve_done, 1))
            dve(nc.vector.tensor_scalar(HWA[:, 0:2], Q("w0"), 0.5, None, ALU.mult).then_inc(dve_done, 1))
            dve(nc.vector.tensor_scalar(HWA[:, 2:4], Q("a0"), 0.5, None, ALU.mult).then_inc(dve_done, 1))
            dve.wait_ge(loaded["R"][l], at("ldR", l))
            dve(nc.vector.tensor_copy(UD[:, :, :, 0], SHI).then_inc(dve_done, 1))
            dve(nc.vector.memset(YR[:, 4, :], 0.0).then_inc(dve_done, 1))
            dve(nc.vector.memset(BNV[:, 4, :], 0.0).then_inc(dve_done, 1))
            mu = Q("mu")
            for name, f0, nf in (("F1", 0, 4), ("F2", 4, 3)):
                for f in range(nf):
                    dve.wait_ge(pe_done, at("full", name, l, f))
                    ps = bank(name, l, f)
                    dve(nc.vector.tensor_copy(UX[:, f0 + f, 1:513], ps[:, :]).then_inc(dve_done, 1))
                    dve.free(name, l, f)
                dve.wait_ge(pe_done, at("full", name, l, "d"))
                ps = bank(name, l, "d")
                dve(nc.vector.tensor_copy(UD[:, f0:f0 + nf, :, 1:5], ps[:, 0:32 * nf].rearrange("p (f b t) -> p f b t", f=nf, b=DB)).then_inc(dve_done, 1))
                dve.free(name, l, "d")
                dve(nc.vector.tensor_copy(SHO[:, f0:f0 + nf, 8:9], UX[:, f0:f0 + nf, 512:513]).then_inc(dve_done, 1))
                dve(nc.vector.tensor_copy(SHO[:, f0:f0 + nf, 0:8], UD[:, f0:f0 + nf, :, 4]).then_inc(dve_done, 1), "SHO", l)
                for f in ((2, 3, 0, 1) if f0 == 0 else (6, 4, 5)):
                    dve(nc.vector.tensor_tensor(DTm, UX[:, f, 0:512], UX[:, f, 1:513], ALU.subtract).then_inc(dve_done, 1))
                    dve(nc.vector.scalar_tensor_tensor(UX[:, f, 1:513], DTm, mu[:, f:f + 1], UX[:, f, 1:513], ALU.mult, ALU.add).then_inc(dve_done, 1))
                    dd = DTm[:, 0:32].rearrange("p (b t) -> p b t", b=DB)
                    dve(nc.vector.tensor_tensor(dd, UD[:, f, :, 0:4], UD[:, f, :, 1:5], ALU.subtract).then_inc(dve_done, 1))
                    dve(nc.vector.scalar_tensor_tensor(UC[:, f, :].rearrange("p (b t) -> p b t", b=DB), dd, mu[:, f:f + 1], UD[:, f, :, 1:5],
                                                     ALU.mult, ALU.add).then_inc(dve_done, 1))
                    if f == 6:
                        dve.name("um6", l)
                if f0 == 0:
                    kk = Q("kk")
                    for dst, src, w in ((NRM[:, :, 0:SEQ], UX[:, 2:4, 1:513], SEQ), (NRM[:, :, SEQ:NT], UC[:, 2:4, :], DTOK)):
                        dve(nc.vector.tensor_tensor(dst, src, bc(kk, 2, w), ALU.mult).then_inc(dve_done, 1))
                    dve(nc.vector.tensor_tensor(NRM, NRM, NRM, ALU.mult).then_inc(dve_done, 1), "kk2", l)
            for f in range(3):
                dve.wait_ge(pe_done, at("full", "ns", l, f))
                ps = bank("ns", l, f)
                dst, src = (NRM[:, f, 0:SEQ], ps[:, :]) if f < 2 else (NRM[:, :, SEQ:NT], ps[:, 0:2 * DTOK].rearrange("p (f t) -> p f t", f=2))
                dve(nc.vector.tensor_scalar(dst, src, 1e-24, None, ALU.max).then_inc(dve_done, 1), "ss", l)
                dve.free("ns", l, f)
            dve.wait_ge(act_done, at("thlw", l))
            dve(nc.vector.tensor_scalar(LW, LW, -0.5 * DECAY, -0.5 * DECAY, ALU.mult, ALU.add).then_inc(dve_done, 1), "LW", l)
            dve.wait_ge(act_done, at("thla", l))
            dve(nc.vector.tensor_scalar(AG, AG, 0.5, 0.5, ALU.mult, ALU.add).then_inc(dve_done, 1))
            for m in range(TILES):
                dve_r_block(dve, l, m)
            dve.name("rblocks", l)
            dve_r_norm(dve, l)
            dve.wait_ge(act_done, at("RZ", l))
            dve(nc.vector.tensor_tensor(YR[:, 0:4, :], YR[:, 0:4, :], RZ[:, 0:4, :], ALU.mult).then_inc(dve_done, 1))
            dve(nc.vector.tensor_tensor(YR[0:32, 4, :], YR[0:32, 4, :], RZ[0:32, 4, :], ALU.mult).then_inc(dve_done, 1), "y", l, 4)
            dve_yT(dve, l, 4)
            phase_end(dve, "R", l)

        def dve_r_block(dve, l, m):
            n = rows(m)
            nch, cl = (4, 32) if m < 4 else (8, DS)
            mk = (lambda s: C(s)) if m < 4 else (lambda s: C(s + "d", 32))
            c2 = lambda b: b[:, :, 0:n]
            r, k = (um_pair(m, f) for f in (0, 2))
            lw, ag = LW[:, :, tok(m)], AG[:, :, tok(m)]
            dve.wait_ge(pe_done, at("full", "lt", l, m))
            ps = bank("lt", l, m)
            dve(nc.vector.tensor_copy(LWT[0:n], ps[0:n, 0:256]).then_inc(dve_done, 1), "LWT", l, m)
            dve.free("lt", l, m)
            dve.wait_ge(pe_done, at("full", "cc", l, m))
            ps = bank("cc", l, m)
            dve(nc.vector.tensor_copy(c2(Cc), ps[:, 0:2 * n].rearrange("p (f t) -> p f t", f=2)).then_inc(dve_done, 1))
            dve.free("cc", l, m)
            dve(nc.vector.tensor_tensor(c2(E1), c2(Cc), lw, ALU.subtract).then_inc(dve_done, 1))
            cend = c2(Cc).rearrange("p f (c t) -> p f c t", t=cl)
            for f in range(2):
                dve(nc.vector.tensor_tensor(c2(E4).rearrange("p f (c t) -> p f c t", t=cl)[:, f], cend[:, f, :, cl - 1:cl].broadcast_to([128, nch, cl]),
                                          cend[:, f], ALU.subtract).then_inc(dve_done, 1))
            dve.name("Ex", l, m)
            dve(nc.vector.tensor_tensor(c2(KK), k, bc(Q("kk"), 2, n), ALU.mult).then_inc(dve_done, 1))
            dve(nc.vector.scalar_tensor_tensor(c2(KE), ag, -1.0, bc(Q("ka"), 2, n), ALU.add, ALU.mult).then_inc(dve_done, 1))
            dve(nc.vector.scalar_tensor_tensor(c2(KE), c2(KE), 1.0, k, ALU.add, ALU.mult).then_inc(dve_done, 1))
            dve.wait_ge(act_done, at("ri", l))
            dve(nc.vector.tensor_tensor(c2(KK), c2(KK), NRM[:, :, tok(m)], ALU.mult).then_inc(dve_done, 1))
            dve(nc.vector.tensor_tensor(c2(Bv), c2(KK), ag, ALU.mult).then_inc(dve_done, 1))
            dve.wait_ge(act_done, at("E1", l, m))
            dve(nc.vector.tensor_tensor(c2(E1), c2(E1), c2(KK), ALU.mult).then_inc(dve_done, 1))
            dve.wait_ge(act_done, at("E", l, m))
            dve(nc.vector.tensor_tensor(c2(Cc), c2(KE), c2(E2), ALU.mult).then_inc(dve_done, 1))
            dve(nc.vector.tensor_tensor(c2(E2), c2(E2), c2(Bv), ALU.mult).then_inc(dve_done, 1))
            dve(nc.vector.tensor_tensor(c2(KH), c2(KE), c2(E4), ALU.mult).then_inc(dve_done, 1))
            dve(nc.vector.tensor_tensor(c2(E4), c2(E4), c2(Bv), ALU.mult).then_inc(dve_done, 1))
            dve(nc.vector.tensor_tensor(c2(RT_), r, c2(E3), ALU.mult).then_inc(dve_done, 1))
            dve(nc.vector.tensor_tensor(c2(TQ), r, c2(KE), ALU.mult).then_inc(dve_done, 1))
            dve(nc.vector.tensor_tensor(c2(TQ), c2(TQ), bc(Q("rk"), 2, n), ALU.mult).then_inc(dve_done, 1), "fm", l, m)
            if m < 4:
                dve_compress(dve, l, 2 * m)
            dve.wait_ge(pe_done, at("full", "t2", l, m))
            ps = bank("t2", l, m)
            dve(nc.vector.tensor_copy(TOK[0:n, 2, :], ps[0:n, 0:256]).then_inc(dve_done, 1))
            dve(nc.vector.tensor_scalar(Zb[0:n, :, 0:64], ps[0:n, 256:512].rearrange("p (h d) -> p h d", h=NH), -1.0, None, ALU.mult).then_inc(dve_done, 1))
            dve.free("t2", l, m)
            dve.wait_ge(pe_done, at("full", "bn", l, m))
            ps = bank("bn", l, m)
            dve(nc.vector.tensor_copy(BN[0:n], ps[0:n, 0:4]).then_inc(dve_done, 1))
            dve.free("bn", l, m)
            v4n = lambda p: p[0:n, 0:4 * n].rearrange("p (h t) -> p h t", h=NH)
            for key, dst, mask in (("pN", Nb[0], "nSL"), ("pT", Tb[0], "nSU"), ("pW", WTb, "SU"), ("pG", GT, "IU"), ("pH", HT_, "IU")):
                dve.wait_ge(pe_done, at("full", key, l, m))
                ps = bank(key, l, m)
                dve(nc.vector.tensor_tensor(dst[0:n, :, 0:n], v4n(ps), bc(mk(mask), 1, NH), ALU.mult).then_inc(dve_done, 1))
                dve.free(key, l, m)
                if key == "pT":
                    dve.name("Nlev", l, m, 0)
                if key == "pW":
                    dve.name("WT", l, m)
            dve.wait_ge(pe_done, at("full", "wv", l, m))
            ps = bank("wv", l, m)
            dve(nc.vector.tensor_scalar(Zb[0:n, :, 64:128], ps[0:n, 0:256].rearrange("p (h d) -> p h d", h=NH), -1.0, None, ALU.mult).then_inc(dve_done, 1), "Z", l, m, 0)
            dve.free("wv", l, m)
            for lev in range(levels(m)):
                if lev < levels(m) - 1:
                    dve.wait_ge(pe_done, at("full", "sqt", l, m, lev))
                    ps = bank("sqt", l, m, lev)
                    dve(nc.vector.tensor_copy(Tb[(lev + 1) % 2][0:n, :, 0:n], v4n(ps)).then_inc(dve_done, 1), "Nlev", l, m, lev + 1)
                    dve.free("sqt", l, m, lev)
                dve.wait_ge(pe_done, at("full", "za", l, m, lev))
                ps = bank("za", l, m, lev)
                dve(nc.vector.tensor_tensor(Zb[0:n], ps[0:n, :].rearrange("p (h d) -> p h d", h=NH), Zb[0:n], ALU.add).then_inc(dve_done, 1), "Z", l, m, lev + 1)
                dve.free("za", l, m, lev)
            dve.wait_ge(pe_done, at("full", "rx", l, m))
            ps = bank("rx", l, m)
            dve(nc.vector.tensor_tensor(c2(RX), ps[:, 0:2 * n].rearrange("p (f t) -> p f t", f=2), c2(RT_), ALU.add).then_inc(dve_done, 1), "RX", l, m)
            dve.free("rx", l, m)
            dve.wait_ge(pe_done, at("full", "yy", l, m))
            ps = bank("yy", l, m)
            dve(nc.vector.tensor_copy(c2(YY), ps[:, 0:2 * n].rearrange("p (f t) -> p f t", f=2)).then_inc(dve_done, 1))
            dve.free("yy", l, m)
            if m < 4:
                dve(nc.vector.tensor_copy(STt[:, 0, :], STt[:, 4, :]).then_inc(dve_done, 1), "S", l, m, 0)
                for c in range(4):
                    dve(nc.vector.tensor_tensor(MTc[:, c], bc(C("IDN2"), 1, 2), E3[:, :, 32 * c + 31:32 * c + 32].broadcast_to([128, 2, 64]), ALU.mult).then_inc(dve_done, 1))
                    dve.wait_ge(pe_done, at("full", "mc", l, m, c))
                    ps = bank("mc", l, m, c)
                    dve(nc.vector.tensor_tensor(MTc[:, c], MTc[:, c], ps[:, 0:128].rearrange("p (f k) -> p f k", f=2), ALU.add).then_inc(dve_done, 1))
                    dve(nc.vector.tensor_copy(ZSc[:, c], ps[:, 128:256]).then_inc(dve_done, 1), "S", l, m, 0)
                    dve.free("mc", l, m, c)
                for c in range(4):
                    dve.wait_ge(pe_done, at("full", "sc", l, m, c))
                    ps = bank("sc", l, m, c)
                    dve(nc.vector.tensor_tensor(STt[:, c + 1, :], ps[:, 0:128], ZSc[:, c], ALU.add).then_inc(dve_done, 1), "S", l, m, c + 1)
                    dve.free("sc", l, m, c)
                dve_compress(dve, l, 2 * m + 1)
            dve.wait_ge(pe_done, at("full", "yr", l, m))
            ps = bank("yr", l, m)
            dve(nc.vector.tensor_tensor(c2(YF), ps[:, 0:2 * n].rearrange("p (f t) -> p f t", f=2), c2(YY), ALU.add).then_inc(dve_done, 1), "YF", l, m)
            dve.free("yr", l, m)
            if m == 4:
                dve.wait_ge(act_done, at("TOKa", l, m))
                for hp in range(2):
                    for hh in range(2):
                        h = 2 * hp + hh
                        if h:
                            dve.wait_ge(pe_done, at("expu", l, h - 1))
                        for dst, src in ((BhE, TOK[0:32, 0, 64 * h:64 * h + 64]), (VE, TOK[0:32, 2, 64 * h:64 * h + 64]), (YE, Zb[0:32, h, 64:128])):
                            dve(nc.vector.tensor_tensor(dst[0:32], bc(src, 1, DB), bc(C("chD", 32), 2, HD), ALU.mult).then_inc(dve_done, 1))
                        dve.name("exp", l, h)
                    dve.wait_ge(pe_done, at("full", "md4", l, hp))
                    dve.wait_ge(pe_done, at("full", "zd4", l, hp))
                    pm, pz = bank("md4", l, hp), bank("zd4", l, hp)
                    e3 = E3[:, hp, 0:32].rearrange("p (b t) -> p b t", t=DS)[:, :, DS - 1:DS].broadcast_to([128, DB, 64])
                    dve(nc.vector.tensor_tensor(MTd, bc(C("IDN2"), 1, DB), e3, ALU.mult).then_inc(dve_done, 1))
                    dve(nc.vector.tensor_tensor(MTd, MTd, pm[:, :].rearrange("p (c k) -> p c k", c=8), ALU.add).then_inc(dve_done, 1))
                    dve(nc.vector.tensor_copy(ZSd, pz[:, :].rearrange("p (c k) -> p c k", c=8)).then_inc(dve_done, 1), "MTd", l, hp)
                    dve.free("md4", l, hp)
                    dve.free("zd4", l, hp)
                    dve.wait_ge(pe_done, at("full", "sd4", l, hp))
                    ps = bank("sd4", l, hp)
                    dve(nc.vector.tensor_tensor(SD[:, :, 64 * hp:64 * hp + 64], ps[:, :].rearrange("p (c k) -> p c k", c=8), ZSd, ALU.add).then_inc(dve_done, 1), "SDn", l)
                    dve.free("sd4", l, hp)
            dve.wait_ge(pe_done, at("full", "yt2", l, m))
            ps = bank("yt2", l, m)
            dve(nc.vector.tensor_copy(YR[0:n, m, :], ps[0:n, 0:256]).then_inc(dve_done, 1))
            dve.free("yt2", l, m)
            dve(nc.vector.tensor_tensor(BNV[0:n, m, :].rearrange("p (h d) -> p h d", h=NH), TOK[0:n, 2, :].rearrange("p (h d) -> p h d", h=NH),
                                      bc(BN[0:n], 2, HD), ALU.mult).then_inc(dve_done, 1))

        def dve_r_norm(dve, l):
            y20 = YR.rearrange("p i (h d) -> p (i h) d", h=NH)
            sq = SQ5.rearrange("p (j d) -> p j d", d=HD)
            dve(nc.vector.reduce_sum(s20, y20, axis=AX.X).then_inc(dve_done, 1))
            dve(nc.vector.tensor_scalar(s20, s20, -1.0 / HD, None, ALU.mult).then_inc(dve_done, 1))
            dve(nc.vector.tensor_tensor(y20, y20, bc(s20, 2, HD), ALU.add).then_inc(dve_done, 1))
            dve(nc.vector.tensor_tensor(sq, y20, y20, ALU.mult).then_inc(dve_done, 1))
            dve(nc.vector.reduce_sum(v20, sq, axis=AX.X).then_inc(dve_done, 1), "v20", l)
            dve.wait_ge(act_done, at("lnr", l))
            dve(nc.vector.tensor_tensor(y20, y20, bc(v20, 2, HD), ALU.mult).then_inc(dve_done, 1))
            dve(nc.vector.tensor_tensor(YR, YR, bc(Q("ln0"), 1, TILES), ALU.mult).then_inc(dve_done, 1))
            dve(nc.vector.tensor_tensor(YR, YR, bc(Q("ln1"), 1, TILES), ALU.add).then_inc(dve_done, 1))
            dve(nc.vector.tensor_tensor(YR, YR, BNV, ALU.add).then_inc(dve_done, 1))

        def um_pair(m, f):
            return UX[:, f:f + 2, 1 + 128 * m:129 + 128 * m] if m < 4 else UC[:, f:f + 2, :]

        cv = Carve()
        PN = cv(TILES * 1804).rearrange("p (i c) -> p i c", i=TILES)
        QR = cv(TILES * 256).rearrange("p (i c) -> p i c", i=TILES)
        VBD = cv(256)
        nss, mss, ncs, nmx = cv(40), cv(20), cv(16), cv(16)
        GS = cv(60).rearrange("p (i c) -> p i c", i=TILES)
        PP = [cv(512), cv(512)]
        PT = [cv(512), cv(512)]
        pm2, ps2 = [cv(2), cv(2)], [cv(2), cv(2)]
        CO = cv(128)
        PEH, peb = cv(2), cv(2)
        OR = cv(1024).rearrange("p (k c) -> p k c", k=2)
        SHB = cv(4128)
        TMPP, HIDP = SHB[:, 0:128], SHB[:, 128:256]
        KVT = SHB[:, 1024:3072].rearrange("p (c h t) -> p c h t", c=2, h=2)
        KQ = SHB[:, 3072:4128]
        RT = [PT[0][:, 0:256], PT[0][:, 256:512], PT[1][:, 0:256], PT[1][:, 256:512]]
        sh_o = [0]

        def shc(n):
            sh_o[0] += n
            assert sh_o[0] <= 4128
            return SHB[:, sh_o[0] - n:sh_o[0]]

        QNZ, QBD, QBDM = (shc(256) for _ in range(3))
        QN2, PR, PRT, PG, BT, SELB = (shc(128) for _ in range(6))
        IM, BI = shc(NSLC), shc(NSLC)
        mx8 = shc(16)
        SB, EB = (shc(384).rearrange("p (s c) -> p s c", s=24) for _ in range(2))
        DEN3 = shc(384).rearrange("p (b c) -> p b c", b=DB)
        OTA = shc(192).rearrange("p (r g t) -> p r g t", r=3, g=2)
        OTM = shc(64).rearrange("p (g t) -> p g t", g=2)
        MX, DG, ES = (shc(48) for _ in range(3))
        m48, cmn, csm = (shc(1) for _ in range(3))
        FT = hT
        FQN, FQR, FMQ, FKS, FKW = 0, 2, 4, 6, 7
        GR3 = ((0, 17), (17, 22), (22, 24))
        DT = slice(SEQ, NT)

        def half(h):
            return slice(64 * h, 64 * h + 64)

        def pool_n(pool, l):
            pool.dma(f"stN{l}", pool.eng.dma_start(io["winpast"][l], io["winraw"][l, :, DS:WIN, :]).then_inc(stored["N"][l], 16))
            pool.wait_ge(act_done, at("PT4", l))
            pool.dma(f"stN{l}", pool.eng.dma_start(io["cmp"][l], PN[:, :, 512:768]).then_inc(stored["N"][l], 16))
            pool.wait_ge(dve_done, at("rope", l, 4))
            pool.dma(f"stN{l}", pool.eng.dma_start(io["slc"][l, :, :, 0:128], PN[:, :, 256:384]).then_inc(stored["N"][l], 16))
            pool.dma(f"stN{l}", pool.eng.dma_start(io["slc"][l, :, :, 128:256], PN[:, :, 768:896]).then_inc(stored["N"][l], 16))
            pool.dma(f"stN{l}", pool.eng.dma_start(io["win"][l, :, :, 0:128], PN[:, :, 384:512]).then_inc(stored["N"][l], 16))
            pool.dma(f"stN{l}", pool.eng.dma_start(io["win"][l, :, :, 128:256], PN[:, :, 896:1024]).then_inc(stored["N"][l], 16), "stN", l)
            pool.wait_ge(pe_done, at("full", "pcs", l))
            pool.dma(f"xr{l}", pool.eng.dma_start(X, io["x"] if l == 0 else io["y"]).then_inc(x_reloaded[l], 16), "xr", l)

        def pe_n(pe, l):
            pe_project_tm(pe, l, "T3")
            pe_r_end(pe, l)
            w1p = Q("w1p").rearrange("p (c j e) -> p c j e", c=2, j=8)
            ps = pe.open("ph", l)
            for c in range(2):
                for j in range(8):
                    last = nc.tensor.matmul(ps[:, 2 * c:2 * c + 2], w1p[:, c, j, :], Q("pe").rearrange("p (c r j) -> p c r j", c=2, r=2)[:, c, :, j],
                                            start=(j == 0), stop=(j == 7))
            pe.full(last.then_inc(pe_done, 1), "ph", l)
            for b in range(DB):
                pe_cmp_kv(pe, l, b)
            pe_project_tm(pe, l, "T4")
            pe.wait_ge(act_done, at("PT4", l))
            for c in range(2):
                ps = pe.open("kvt", l, c)
                for i in range(4):
                    last = nc.tensor.transpose(ps[:, tok(i)], PN[:, i, 512 + 128 * c:640 + 128 * c], idn)
                pe.full(last.then_inc(pe_done, 1), "kvt", l, c)
            pe.wait_ge(dve_done, at("KVT", l))
            pe.wait_ge(sem_of_slot("w1f", l), at("here", "w1f", l))
            wf = slot("w1f", l).rearrange("p (c s e) -> p c s e", c=2, s=16)
            kv = KVT.rearrange("p c h (n s) -> p c h n s", s=16)
            ps = pe.open("abp", l)
            for c in range(2):
                for s in range(16):
                    last = nc.tensor.matmul(ps[:, 64 * c:64 * c + 64], wf[:, c, s, :], kv[:, c, :, :, s], start=(s == 0), stop=(s == 15))
            pe.full(last.then_inc(pe_done, 1), "abp", l)
            pe.name("used", "w1f", l)
            pe_project_tm(pe, l, "T6")
            pe_cmp_kv(pe, l, "p")
            pe.wait_ge(dve_done, at("KQ", l))
            for k, (o, n) in enumerate(((0, 512), (512, 512), (1024, 32))):
                ps = pe.open("kn", l, k)
                pe.full(nc.tensor.matmul(ps[:, 0:n], C("onesbd"), KQ[:, o:o + n], start=True, stop=True).then_inc(pe_done, 1), "kn", l, k)
            pe_project_tm(pe, l, "T5")
            pe.wait_ge(dve_done, at("mqn", l))
            pe.wait_ge(dve_done, at("rope", l, 4))
            for i in range(TILES):
                n = rows(i)
                ps = pe.open("fa", l, i)
                for a in range(4):
                    src = PN[0:n, i, 128 * a:128 * a + 128] if a < 2 else QR[0:n, i, 128 * a - 256:128 * a - 128]
                    last = nc.tensor.transpose(ps[:, n * a:n * a + n], src, idn[0:n, 0:n])
                pe.full(last.then_inc(pe_done, 1), "fa", l, i)
                ps = pe.open("fb", l, i)
                for a, o in enumerate((1292, 1420, 256, 384)):
                    last = nc.tensor.transpose(ps[:, n * a:n * a + n], PN[0:n, i, o:o + 128], idn[0:n, 0:n])
                pe.full(last.then_inc(pe_done, 1), "fb", l, i)
            pe_decode_cmp(pe, l)
            pe_prompt(pe, l)
            pe.wait_ge(dve_done, at("OR", l))
            for k in range(2):
                ps = pe.open("ot", l, k)
                for a in range(4):
                    last = nc.tensor.transpose(ps[:, 128 * a:128 * a + 128], OR[:, k, 128 * a:128 * a + 128], idn)
                pe.full(last.then_inc(pe_done, 1), "ot", l, k)
            pe.wait_ge(dve_done, at("OTn", l))
            ps = pe.open("oa", l)
            for a in range(4):
                last = nc.tensor.transpose(ps[0:32, 128 * a:128 * a + 128], OTA[:, a // 2, a % 2, :], idn)
            pe.full(last.then_inc(pe_done, 1), "oa", l)
            ps = pe.open("ob", l)
            for a in range(4):
                last = nc.tensor.transpose(ps[0:32, 128 * a:128 * a + 128], OTA[:, 2, a, :] if a < 2 else OTM[:, a - 2, :], idn)
            pe.full(last.then_inc(pe_done, 1), "ob", l)
            pe_yT(pe, l, PN[:, :, 0:256], 2)
            pe_yT(pe, l, PN[:, :, 1292:1548], 6)
            phase_end(pe, "N", l)

        def pe_cmp_kv(pe, l, b):
            if b == "p":
                pe.wait_ge(act_done, at("GP", l))
                n, w2, g = 32, Q("w2")[0:64], HIDP[0:64].rearrange("p (c h n) -> p c h n", c=2, h=2)
            else:
                pe.wait_ge(act_done, at("G", l))
                n, w2, g = 128, Q("w2")[half(b % 2)], HIDD[half(b % 2), b // 2].rearrange("p c (n h) -> p c h n", h=2)
            ps = pe.open("kv", l, b)
            for h in range(2):
                nc.tensor.matmul(ps[half(h), 0:n], w2[:, 0:64], g[:, 0, h, :], start=True, stop=True)
            for h in range(2):
                last = nc.tensor.matmul(ps[0:n, 128 + 64 * h:192 + 64 * h], g[:, 1, h, :], w2[:, 64:128], start=True, stop=True)
            pe.full(last.then_inc(pe_done, 1), "kv", l, b)

        def pe_decode_cmp(pe, l):
            pe.wait_ge(dve_done, at("QZ", l))
            ps = pe.open("cs", l)
            for b in range(DB):
                last = nc.tensor.matmul(ps[32 * (b // 2):32 * (b // 2) + 32, 0:NCMP], QNZ[:, 32 * b:32 * b + 32], KC[:, 128 * b:128 * b + NCMP],
                                        start=(b % 2 == 0), stop=(b % 2 == 1))
            pe.full(last.then_inc(pe_done, 1), "cs", l)
            pe.wait_ge(dve_done, at("PR", l))
            ps = pe.open("ct", l)
            pe.full(nc.tensor.transpose(ps[:, 0:128], PR, idn).then_inc(pe_done, 1), "ct", l)
            pe.wait_ge(dve_done, at("PG", l))
            ps = pe.open("im", l)
            pe.full(nc.tensor.matmul(ps[:, 0:NSLC], PG, C("cover"), start=True, stop=True).then_inc(pe_done, 1), "im", l)
            ps = pe.open("co", l)
            for b in range(DB):
                last = nc.tensor.matmul(ps[:, 16 * b:16 * b + 16], VC[:, b, :], PRT[:, 16 * b:16 * b + 16], start=True, stop=True)
            pe.full(last.then_inc(pe_done, 1), "co", l)
            pe.wait_ge(dve_done, at("BI", l))
            ps = pe.open("bt", l)
            pe.full(nc.tensor.transpose(ps[0:NSLC, 0:128], BI, idn).then_inc(pe_done, 1), "bt", l)
            pe.wait_ge(dve_done, at("BT", l))
            ps = pe.open("sb", l)
            pe.full(nc.tensor.matmul(ps[:, 0:128], C("expand", NSLC), BT[0:NSLC, :], start=True, stop=True).then_inc(pe_done, 1), "sb", l)

        def pe_decode_row(pe, l, b, step):
            wm = slot("wm", l, b)
            if step == 0:
                pe_decode_scores(pe, l, b, wm)
            elif step == 1:
                pe.wait_ge(dve_done, at("MX", l, b))
                ps = pe.open("mxt", l, b)
                pe.full(nc.tensor.transpose(ps[0:48, 0:128], MX, idn).then_inc(pe_done, 1), "mxt", l, b)
            elif step == 2:
                pe.wait_ge(dve_done, at("DG", l, b))
                ps = pe.open("mxb", l, b)
                pe.full(nc.tensor.matmul(ps[:, 0:48], C("ones", 48), DG[0:48, :], start=True, stop=True).then_inc(pe_done, 1), "mxb", l, b)
            else:
                pe_decode_values(pe, l, b, wm)

        def pe_decode_scores(pe, l, b, wm):
            pe.wait_ge(dve_done, at("QBD", l))
            pe.wait_ge(sem_of_slot("slcK", l, b), at("here", "slcK", l, b))
            pe.wait_ge(sem_of_slot("wm", l, b), at("here", "wm", l, b))
            K = slot("slcK", l, b).rearrange("p (n h j) -> p n h j", h=2, j=8)
            wK = wm[:, 0:512].rearrange("p (h j n) -> p h j n", h=2, j=2)
            mK = wm[:, 1024:1536].rearrange("p (h n) -> p h n", h=4)
            ps = pe.open("ds", l, b)
            S = ps[:, 0:384].rearrange("p (s c) -> p s c", s=24)
            for h in range(2):
                q = QBD.rearrange("p (b h c) -> p b h c", b=DB, h=2)[:, b, h, :]
                for j in range(8):
                    nc.tensor.matmul(S[:, 2 * j:2 * j + 2, 8 * h:8 * h + 8], K[:, :, h, j], q, start=True, stop=True)
                for j in range(2):
                    nc.tensor.matmul(S[:, 17 + 2 * j:19 + 2 * j, 8 * h:8 * h + 8], wK[:, h, j, :], q, start=True, stop=True)
            for h in range(NH):
                nc.tensor.matmul(S[:, 22:24, 4 * h:4 * h + 4], mK[:, h, :], QBDM.rearrange("p (b h c) -> p b h c", b=DB, h=4)[:, b, h, :],
                                 start=True, stop=True)
            nc.tensor.matmul(S[0:32, 16, :], FT[:, FKS, DT], QN2[:, 16 * b:16 * b + 16], start=True, stop=True)
            last = nc.tensor.matmul(S[0:32, 21, :], FT[:, FKW, DT], QN2[:, 16 * b:16 * b + 16], start=True, stop=True)
            pe.full(last.then_inc(pe_done, 1), "ds", l, b)
            pe.name("used", "slcK", l, b)

        def pe_decode_values(pe, l, b, wm):
            Vs = slot("slcV", l, b).rearrange("p (s c) -> p s c", s=16)
            wV = wm[:, 512:1024].rearrange("p (s c) -> p s c", s=4)
            mV = wm[:, 1536:2048].rearrange("p (s c) -> p s c", s=2)
            pe.wait_ge(sem_of_slot("slcV", l, b), at("here", "slcV", l, b))
            pe.wait_ge(act_done, at("EB", l, b))
            ps = pe.open("dp", l, b)
            for s in range(16):
                nc.tensor.matmul(ps[0:16, 0:128], EB[:, s, :], Vs[:, s, :], start=(s == 0), stop=False)
            nc.tensor.matmul(ps[0:16, 0:128], EB[0:32, 16, :], PN[0:32, 4, 768:896], start=False, stop=True)
            for s in range(4):
                nc.tensor.matmul(ps[0:16, 128:256], EB[:, 17 + s, :], wV[:, s, :], start=(s == 0), stop=False)
            nc.tensor.matmul(ps[0:16, 128:256], EB[0:32, 21, :], PN[0:32, 4, 896:1024], start=False, stop=True)
            for s in range(2):
                last = nc.tensor.matmul(ps[0:16, 256:512], EB[:, 22 + s, :], mV[:, s, :], start=(s == 0), stop=(s == 1))
            pe.full(last.then_inc(pe_done, 1), "dp", l, b)
            pe.name("used", "slcV", l, b)
            pe.name("used", "wm", l, b)
            pe.wait_ge(dve_done, at("ES", l, b))
            ps = pe.open("dd", l, b)
            pe.full(nc.tensor.matmul(ps[:, 0:48], C("ones"), ES, start=True, stop=True).then_inc(pe_done, 1), "dd", l, b)

        UNITS = [(br, i, h) for i in range(4) for br in ("s", "w", "m") for h in range(2)]

        def ukeys(br, i):
            return 128 * (i + 1) if br != "m" else NMEM

        def pe_prompt(pe, l):
            ps = pe.open("pcs", l)
            for h in range(2):
                for i in range(4):
                    for g in range(2):
                        o = 128 * i + 64 * g + 32 * h
                        last = nc.tensor.matmul(ps[:, o:o + 32], FT[half(h), FQN + g, tok(i)], KC[half(h), 1024:1056], start=True, stop=True)
                if h == 0:
                    pe.fence(last.then_inc(pe_done, 1))
            pe.full(last.then_inc(pe_done, 1), "pcs", l)
            pe_unit_s(pe, l, 0)
            pe.wait_ge(dve_done, at("PC", l))
            ps = pe.open("pct", l)
            for i in range(4):
                last = nc.tensor.transpose(ps[:, tok(i)], PP[1][:, tok(i)], idn)
            pe.full(last.then_inc(pe_done, 1), "pct", l)
            pe.wait_ge(dve_done, at("PCT", l))
            for hf in range(2):
                ps = pe.open("pco", l, hf)
                for i in range(2):
                    last = nc.tensor.matmul(ps[:, 256 * i:256 * i + 256], PT[1][:, tok(2 * hf + i)], VBD, start=True, stop=True)
                pe.full(last.then_inc(pe_done, 1), "pco", l, hf)
            for u in range(len(UNITS)):
                pe_decode_row(pe, l, u // 3, u % 3)
                if u + 1 < len(UNITS):
                    pe_unit_s(pe, l, u + 1)
                pe_unit_t(pe, l, u)
                pe_unit_v(pe, l, u)
                if u % 3 == 2:
                    pe_decode_row(pe, l, u // 3, 3)

        def pe_unit_s(pe, l, u):
            br, i, h = UNITS[u]
            n = ukeys(br, i)
            if br == "m":
                ps = pe.open("us", l, u, 0)
                for hp in range(2):
                    last = nc.tensor.matmul(ps[:, 256 * hp:256 * hp + 256], FT[half(h), FMQ + hp, tok(i)], MKT[half(h), hp, :], start=True, stop=True)
                pe.full(last.then_inc(pe_done, 1), "us", l, u, 0)
                return
            kt = FKS if br == "s" else FKW
            bk = [pe.open("us", l, u, g) for g in range(2)]
            for g, ps in enumerate(bk):
                last = nc.tensor.matmul(ps[:, 0:n], FT[half(h), FQR + g, tok(i)], FT[half(h), kt, 0:n], start=True, stop=False)
            pe.fence(last.then_inc(pe_done, 1))
            for g, ps in enumerate(bk):
                last = nc.tensor.matmul(ps[:, n - 128:n], idn, C("caus"), start=False, stop=True)
                pe.full(last.then_inc(pe_done, 1), "us", l, u, g)

        def pe_unit_t(pe, l, u):
            br, i, h = UNITS[u]
            n = ukeys(br, i)
            for g in range(2):
                pe.wait_ge(act_done, at("UE", l, u, g))
                ps = pe.open("ut", l, u, g)
                for j in range(n // 128):
                    last = nc.tensor.transpose(ps[:, 128 * j:128 * j + 128], PP[g][:, 128 * j:128 * j + 128], idn)
                pe.full(last.then_inc(pe_done, 1), "ut", l, u, g)

        def pe_unit_v(pe, l, u):
            br, i, h = UNITS[u]
            nk = ukeys(br, i) // 128
            ps = pe.open("uv", l, u)
            for g in range(2):
                pe.wait_ge((dve_done, act_done)[g], at("UT", l, u, g))
                for j in range(nk):
                    v = MKV[:, j, 256 + 64 * (2 * g + h):320 + 64 * (2 * g + h)] if br == "m" else \
                        PN[:, j, (768 if br == "s" else 896) + 64 * h:(832 if br == "s" else 960) + 64 * h]
                    last = nc.tensor.matmul(ps[:, 64 * g:64 * g + 64], PT[g][:, 128 * j:128 * j + 128], v, start=(j == 0), stop=(j == nk - 1))
            pe.full(last.then_inc(pe_done, 1), "uv", l, u)

        def act_n(act, l):
            barrier(act, ("R", l))
            act.wait_ge(stored["R"][l], at("stR", l))
            act.wait_ge(dve_done, at("ntails", l))
            take_project_tm(act, l, "T3", PN[:, :, 0:512], nc.scalar.copy)
            act.wait_ge(dve_done, at("HID", l, DB - 1))
            act.wait_ge(dve_done, at("peb", l))
            for c in range(2):
                act(nc.scalar.activation(HIDD[:, :, c, :], HIDD[:, :, c, :], ACT.Gelu_apprx_tanh, bias=peb[:, c:c + 1]).then_inc(act_done, 1), "G", l)
            take_project_tm(act, l, "T4", PN[:, :, 512:1024], nc.scalar.copy)
            act.wait_ge(dve_done, at("HIDP", l))
            for c in range(2):
                act(nc.scalar.activation(HIDP[0:64, 64 * c:64 * c + 64], HIDP[0:64, 64 * c:64 * c + 64], ACT.Gelu_apprx_tanh,
                                       bias=peb[0:64, c:c + 1]).then_inc(act_done, 1), "GP", l)
            act.wait_ge(dve_done, at("nss", l))
            act(nc.scalar.activation(nss, nss, ACT.Ln, bias=eps, scale=1.0 / HD).then_inc(act_done, 1))
            act(nc.scalar.activation(nss, nss, ACT.Exp, scale=-0.5).then_inc(act_done, 1), "nrs", l)
            take_project_tm(act, l, "T6", PN[:, :, 1292:1804], nc.scalar.copy)
            for k, (o, n) in enumerate(((0, 512), (512, 512), (1024, 32))):
                act.wait_ge(pe_done, at("full", "kn", l, k))
                ps = bank("kn", l, k)
                act(nc.scalar.activation(KQ[:, o:o + n], ps[:, 0:n], ACT.Ln, bias=eps, scale=1.0 / HD).then_inc(act_done, 1))
                act.free("kn", l, k)
            act(nc.scalar.activation(KQ, KQ, ACT.Exp, scale=-0.5).then_inc(act_done, 1), "KR", l)
            act.wait_ge(dve_done, at("mss", l))
            act(nc.scalar.activation(mss, mss, ACT.Ln, bias=eps, scale=1.0 / HD).then_inc(act_done, 1))
            act(nc.scalar.activation(mss, mss, ACT.Exp, scale=-0.5).then_inc(act_done, 1), "mrs", l)
            take_project_tm(act, l, "T5", PN[:, :, 1024:1292], nc.scalar.copy)
            act(nc.scalar.activation(PN[:, :, 1024:1280], PN[:, :, 1024:1280], ACT.Silu).then_inc(act_done, 1))
            act(nc.scalar.activation(PN[:, :, 1548:1804], PN[:, :, 1548:1804], ACT.Silu).then_inc(act_done, 1))
            act(nc.scalar.activation(GS, PN[:, :, 1280:1292], ACT.Tanh, scale=0.5).then_inc(act_done, 1), "GS", l)
            for i in range(TILES):
                n = rows(i)
                act.wait_ge(pe_done, at("full", "fa", l, i))
                ps = bank("fa", l, i)
                act(nc.scalar.mul(FT[:, 0:4, tok(i)], ps[:, 0:4 * n].rearrange("p (a t) -> p a t", a=4), SCALE).then_inc(act_done, 1), "FA", l)
                act.free("fa", l, i)
            act.wait_ge(dve_done, at("cmn", l))
            act.wait_ge(pe_done, at("full", "cs", l))
            ps = bank("cs", l)
            act(nc.scalar.activation(PR[:, 0:NCMP], ps[:, 0:NCMP], ACT.Exp, bias=cmn, accum_out=csm).then_inc(act_done, 1), "csm", l)
            act.free("cs", l)
            act.wait_ge(dve_done, at("PCx", l))
            act(nc.scalar.activation(PP[1], PP[1], ACT.Exp).then_inc(act_done, 1), "PCe", l)
            for u, (br, i, h) in enumerate(UNITS):
                n = ukeys(br, i)
                if u == 0:
                    act.wait_ge(pe_done, at("full", "pct", l))
                else:
                    act.wait_ge(pe_done, at("full", "ut", l, u - 1, 1))
                act.wait_ge(dve_done, at("UM", l, u))
                for g in range(2):
                    act.wait_ge(pe_done, at("full", "us", l, u, 0 if br == "m" else g))
                    ps = bank("us", l, u, 0 if br == "m" else g)
                    s = ps[:, 256 * g:256 * g + 256] if br == "m" else ps[:, 0:n]
                    act(nc.scalar.activation(PP[g][:, 0:n], s, ACT.Exp, bias=pm2[u % 2][:, g:g + 1], accum_out=ps2[u % 2][:, g:g + 1]).then_inc(act_done, 1),
                      "UE", l, u, g)
                    if br != "m" or g:
                        act.free("us", l, u, 0 if br == "m" else g)
                g = 1
                act.wait_ge(pe_done, at("full", "ut", l, u, g))
                ps = bank("ut", l, u, g)
                if u == 0:
                    act.wait_ge(pe_done, at("full", "pco", l, 1))
                else:
                    act.wait_ge(pe_done, at("full", "uv", l, u - 1))
                act(nc.scalar.copy(PT[g][:, 0:n], ps[:, 0:n]).then_inc(act_done, 1), "UT", l, u, g)
                act.free("ut", l, u, g)
                if u % 3 == 2:
                    act.wait_ge(dve_done, at("EX", l, u // 3))
                    act(nc.scalar.activation(EB, EB, ACT.Exp).then_inc(act_done, 1), "EB", l, u // 3)
            act.wait_ge(stored["N"][l], at("stN", l))
            phase_end(act, "N", l)

        def dve_n(dve, l):
            barrier(dve, ("R", l))
            dve.wait_ge(stored["R"][l], at("stR", l))
            dve(nc.vector.memset(PN[:, 4, :], 0.0).then_inc(dve_done, 1), "ntails", l)
            dve(nc.vector.memset(VBD, 0.0).then_inc(dve_done, 1))
            dve(nc.vector.memset(OR, 0.0).then_inc(dve_done, 1))
            dve(nc.vector.memset(HIDP, 0.0).then_inc(dve_done, 1))
            dve(nc.vector.memset(KVT, 0.0).then_inc(dve_done, 1))
            dve.wait_ge(pe_done, at("full", "ph", l))
            ps = bank("ph", l)
            ph = ps[:, 0:4].rearrange("p (c r) -> p c r", c=2)
            lo, hi = half(0), half(1)
            dve(nc.vector.tensor_copy(PEH[lo], ph[hi, :, 1]).then_inc(dve_done, 1))
            dve(nc.vector.tensor_copy(PEH[hi], ph[lo, :, 0]).then_inc(dve_done, 1))
            dve(nc.vector.tensor_tensor(peb[lo], ph[lo, :, 0], PEH[lo], ALU.add).then_inc(dve_done, 1))
            dve(nc.vector.tensor_tensor(peb[hi], ph[hi, :, 1], PEH[hi], ALU.add).then_inc(dve_done, 1), "peb", l)
            dve.free("ph", l)
            dve.wait_ge(act_done, at("PT3", l))
            for i in range(TILES):
                dve(nc.vector.tensor_tensor(PP[0], PN[:, i, 0:512], PN[:, i, 0:512], ALU.mult).then_inc(dve_done, 1))
                dve(nc.vector.reduce_sum(nss[:, 8 * i:8 * i + 8], PP[0].rearrange("p (h d) -> p h d", d=HD), axis=AX.X).then_inc(dve_done, 1))
            dve.name("nss", l)
            for b in range(DB):
                dve_cmp_kv(dve, l, b)
            for c in range(2):
                dve.wait_ge(pe_done, at("full", "kvt", l, c))
                ps = bank("kvt", l, c)
                for h in range(2):
                    dve(nc.vector.tensor_copy(KVT[half(h), c, h, :], ps[half(h), :]).then_inc(dve_done, 1), "KVT", l)
                dve.free("kvt", l, c)
            hid = HIDP[0:64].rearrange("p (c h n) -> p c h n", c=2, h=2)
            tmp = TMPP[0:64].rearrange("p (c h n) -> p c h n", c=2, h=2)
            dve.wait_ge(pe_done, at("full", "abp", l))
            ps = bank("abp", l)
            pv = ps[:, 0:128].rearrange("p (c h n) -> p c h n", c=2, h=2)
            dve(nc.vector.tensor_copy(tmp, pv[64:128]).then_inc(dve_done, 1))
            dve(nc.vector.tensor_tensor(hid[:, :, :, 0:31], pv[0:64, :, :, 0:31], tmp[:, :, :, 1:32], ALU.add).then_inc(dve_done, 1), "HIDP", l)
            dve.free("abp", l)
            for i in range(TILES):
                dve_head_norm(dve, l, i)
            dve_cmp_kv(dve, l, "p")
            dve(nc.vector.tensor_tensor(KQ, KC, KC, ALU.mult).then_inc(dve_done, 1), "KQ", l)
            dve.wait_ge(act_done, at("PT6", l))
            mq = PN[:, :, 1292:1548]
            for i in range(TILES):
                dve(nc.vector.tensor_tensor(PP[i % 2][:, 0:256], mq[:, i, :], mq[:, i, :], ALU.mult).then_inc(dve_done, 1))
                dve(nc.vector.reduce_sum(mss[:, 4 * i:4 * i + 4], PP[i % 2][:, 0:256].rearrange("p (h d) -> p h d", d=HD), axis=AX.X).then_inc(dve_done, 1))
            dve.name("mss", l)
            dve.wait_ge(act_done, at("KR", l))
            dve(nc.vector.scalar_tensor_tensor(KC, KC, Q("kcg"), KQ, ALU.mult, ALU.mult).then_inc(dve_done, 1), "KC", l)
            dve.wait_ge(act_done, at("mrs", l))
            m4 = mq.rearrange("p i (h d) -> p i h d", d=HD)
            dve(nc.vector.tensor_tensor(m4, m4, bc(mss.rearrange("p (i h) -> p i h", i=TILES), 3, HD), ALU.mult).then_inc(dve_done, 1))
            dve(nc.vector.tensor_tensor(m4, m4, bc(bc(Q("mqg"), 1, NH), 1, TILES), ALU.mult).then_inc(dve_done, 1), "mqn", l)
            for i in range(TILES):
                n = rows(i)
                dve.wait_ge(pe_done, at("full", "fb", l, i))
                ps = bank("fb", l, i)
                dve.wait_ge(pe_done, at("used", "w", l, "T5"))
                dve(nc.vector.tensor_scalar(FT[:, 4:6, tok(i)], ps[:, 0:2 * n].rearrange("p (a t) -> p a t", a=2), SCALE, None, ALU.mult).then_inc(dve_done, 1))
                dve(nc.vector.tensor_copy(FT[:, 6:8, tok(i)], ps[:, 2 * n:4 * n].rearrange("p (a t) -> p a t", a=2)).then_inc(dve_done, 1))
                dve.free("fb", l, i)
            dve_decode_cmp(dve, l)
            dve.wait_ge(act_done, at("GS", l))
            dve(nc.vector.tensor_scalar(GS, GS, 0.5, 0.5, ALU.mult, ALU.add).then_inc(dve_done, 1))
            dve_prompt(dve, l)
            dve_decode_out(dve, l)
            dve(nc.vector.tensor_tensor(PN[:, :, 0:256], PN[:, :, 0:256], PN[:, :, 1024:1280], ALU.mult).then_inc(dve_done, 1), "y", l, 2)
            dve(nc.vector.tensor_tensor(PN[:, :, 1292:1548], PN[:, :, 1292:1548], PN[:, :, 1548:1804], ALU.mult).then_inc(dve_done, 1), "y", l, 6)
            dve_yT(dve, l, 2)
            dve_yT(dve, l, 6)
            dve.wait_ge(stored["N"][l], at("stN", l))
            phase_end(dve, "N", l)

        def dve_cmp_kv(dve, l, b):
            dve.wait_ge(pe_done, at("full", "kv", l, b))
            ps = bank("kv", l, b)
            if b == "p":
                dve(nc.vector.tensor_copy(KC[:, 1024:1056], ps[:, 0:32]).then_inc(dve_done, 1))
                for hd in range(NH):
                    dve(nc.vector.tensor_copy(VBD[32 * hd:32 * hd + 32, 64 * hd:64 * hd + 64], ps[0:32, 128 + 64 * (hd % 2):192 + 64 * (hd % 2)]).then_inc(dve_done, 1))
            else:
                dve(nc.vector.tensor_copy(KC[:, 128 * b:128 * b + 128], ps[:, 0:128]).then_inc(dve_done, 1))
                dve(nc.vector.tensor_copy(VC[:, b, :], ps[:, 128:256]).then_inc(dve_done, 1))
            dve.free("kv", l, b)

        def dve_head_norm(dve, l, i):
            if i == 0:
                dve.wait_ge(act_done, at("nrs", l))
            x = PN[:, i, 0:512].rearrange("p (h d) -> p h d", h=8)
            dve(nc.vector.tensor_tensor(x, x, bc(nss[:, 8 * i:8 * i + 8], 2, HD), ALU.mult).then_inc(dve_done, 1))
            dve(nc.vector.tensor_tensor(PN[:, i, 0:512], PN[:, i, 0:512], Q("qkg"), ALU.mult).then_inc(dve_done, 1))
            cs, sn = (bc(C(n)[:, 32 * i:32 * i + 32], 1, 8) for n in ("cos", "sin"))
            R4 = [r.rearrange("p (h d) -> p h d", h=8) for r in RT]
            for r, (a, b) in zip(R4, ((0, cs), (32, sn), (0, sn), (32, cs))):
                dve(nc.vector.tensor_tensor(r, x[:, :, a:a + 32], b, ALU.mult).then_inc(dve_done, 1))
            q = QR[:, i, :].rearrange("p (h d) -> p h d", h=4)
            for dst, s in ((q, slice(0, 4)), (x[:, 4:8], slice(4, 8))):
                dve(nc.vector.tensor_tensor(dst[:, :, 0:32], R4[0][:, s], R4[1][:, s], ALU.subtract).then_inc(dve_done, 1))
                dve(nc.vector.tensor_tensor(dst[:, :, 32:64], R4[2][:, s], R4[3][:, s], ALU.add).then_inc(dve_done, 1), "rope", l, i)

        def dve_decode_cmp(dve, l):
            for a in (QNZ, QBD, QBDM, QN2):
                dve(nc.vector.memset(a, 0.0).then_inc(dve_done, 1))
            dve(nc.vector.memset(PR[:, NCMP:128], 0.0).then_inc(dve_done, 1))
            dve(nc.vector.memset(SB[:, 16:22, :], NEG).then_inc(dve_done, 1))
            dve.wait_ge(act_done, at("FA", l))
            z = QNZ.rearrange("p (b a c) -> p b a c", b=4, a=2)
            for h in range(2):
                for a in range(2):
                    dve(nc.vector.tensor_copy(z[half(h), :, a, 16 * a + 8 * h:16 * a + 8 * h + 8].rearrange("p b (g t) -> p b g t", g=2),
                                            FT[half(h), FQN:FQN + 2, DT].rearrange("p g (b a t) -> p a b g t", b=4, a=2)[:, a]).then_inc(dve_done, 1))
            dve.name("QZ", l)
            qb = QBD.rearrange("p (b h s g t) -> p h s b g t", b=DB, h=2, s=2, g=2)
            qm = QBDM.rearrange("p (b q h s t) -> p h s b q t", b=DB, q=2, h=2, s=2)
            q2 = QN2.rearrange("p (b h g t) -> p h b g t", b=DB, h=2, g=2)
            for h in range(2):
                src = FT[half(h), FQR:FQR + 2, DT].rearrange("p g (b t) -> p b g t", b=DB)
                srm = FT[half(h), FMQ:FMQ + 2, DT].rearrange("p q (b t) -> p b q t", b=DB)
                dve(nc.vector.tensor_copy(q2[half(h), h], src).then_inc(dve_done, 1))
                for s in range(2):
                    dve(nc.vector.tensor_copy(qb[half(s), h, s], src).then_inc(dve_done, 1))
                    dve(nc.vector.tensor_copy(qm[half(s), h, s], srm).then_inc(dve_done, 1), "QBD", l)
            dve.wait_ge(pe_done, at("full", "cs", l))
            ps = bank("cs", l)
            dve(nc.vector.reduce_max(cmn, ps[:, 0:NCMP], axis=AX.X, negate=True).then_inc(dve_done, 1), "cmn", l)
            dve.wait_ge(act_done, at("csm", l))
            dve(nc.vector.reciprocal(csm, csm).then_inc(dve_done, 1))
            dve(nc.vector.tensor_scalar(PR[:, 0:NCMP], PR[:, 0:NCMP], csm, None, ALU.mult).then_inc(dve_done, 1), "PR", l)
            dve.wait_ge(pe_done, at("full", "ct", l))
            ps = bank("ct", l)
            dve(nc.vector.tensor_copy(PRT, ps[:, 0:128]).then_inc(dve_done, 1))
            dve.free("ct", l)
            p4, g4 = (a.rearrange("p (r g t) -> p r g t", g=2, t=4) for a in (PRT, PG))
            for g in range(2):
                dve(nc.vector.tensor_tensor(g4[:, :, g, :], p4[:, :, 0, :], p4[:, :, 1, :], ALU.add).then_inc(dve_done, 1), "PG", l)
            dve.wait_ge(pe_done, at("full", "im", l))
            ps = bank("im", l)
            dve(nc.vector.tensor_tensor(IM, ps[:, 0:NSLC], C("forced"), ALU.add).then_inc(dve_done, 1))
            dve.free("im", l)
            dve(nc.vector.max(mx8[:, 0:8], IM).then_inc(dve_done, 1))
            dve(nc.vector.match_replace(BI, mx8[:, 0:8], IM, -1.0).then_inc(dve_done, 1))
            dve(nc.vector.max(mx8[:, 8:16], BI).then_inc(dve_done, 1))
            dve(nc.vector.match_replace(IM, mx8[:, 8:16], BI, -1.0).then_inc(dve_done, 1))
            dve(nc.vector.tensor_scalar(BI, IM, 0.0, None, ALU.is_ge).then_inc(dve_done, 1), "BI", l)
            dve.wait_ge(pe_done, at("full", "co", l))
            ps = bank("co", l)
            for h in range(2):
                dve(nc.vector.tensor_copy(OTA[half(h), 0].rearrange("p g (b t) -> p b g t", b=DB),
                                        ps[half(h), 0:128].rearrange("p (b h g t) -> p h b g t", b=DB, h=2, g=2)[:, h]).then_inc(dve_done, 1))
            dve.free("co", l)
            dve.wait_ge(pe_done, at("full", "bt", l))
            ps = bank("bt", l)
            dve(nc.vector.tensor_copy(BT[0:NSLC], ps[0:NSLC, 0:128]).then_inc(dve_done, 1), "BT", l)
            dve.free("bt", l)
            dve.wait_ge(pe_done, at("full", "sb", l))
            ps = bank("sb", l)
            dve(nc.vector.tensor_scalar(SELB, ps[:, 0:128], NEG, None, ALU.mult).then_inc(dve_done, 1))
            dve.free("sb", l)

        def dve_decode_row(dve, l, b, step):
            if step == 0:
                dve_decode_scores(dve, l, b)
            elif step == 1:
                dve.wait_ge(pe_done, at("full", "mxt", l, b))
                ps = bank("mxt", l, b)
                dve(nc.vector.reduce_max(m48[0:48], ps[0:48, 0:128], axis=AX.X).then_inc(dve_done, 1))
                dve.free("mxt", l, b)
                dve(nc.vector.tensor_scalar(DG[0:48], idn[0:48, 0:48], m48[0:48], None, ALU.mult).then_inc(dve_done, 1), "DG", l, b)
            elif step == 2:
                dve.wait_ge(pe_done, at("full", "mxb", l, b))
                ps = bank("mxb", l, b)
                for k, (a, e) in enumerate(GR3):
                    dve(nc.vector.tensor_tensor(EB[:, a:e, :], SB[:, a:e, :], bc(ps[:, 16 * k:16 * k + 16], 1, e - a), ALU.subtract).then_inc(dve_done, 1), "EX", l, b)
                dve.free("mxb", l, b)
            else:
                dve_decode_values(dve, l, b)

        def dve_decode_scores(dve, l, b):
            dve.wait_ge(pe_done, at("full", "ds", l, b))
            ps = bank("ds", l, b)
            S = ps[:, 0:384].rearrange("p (s c) -> p s c", s=24)
            nb = C("newb", 32)[:, 16 * b:16 * b + 16]
            dve(nc.vector.tensor_tensor(SB[:, 0:16, :], S[:, 0:16, :], bc(SELB[:, 16 * b:16 * b + 16], 1, 16), ALU.add).then_inc(dve_done, 1))
            dve(nc.vector.tensor_tensor(SB[:, 17:21, :], S[:, 17:21, :], C("winb").rearrange("p (s c) -> p s c", s=4), ALU.add).then_inc(dve_done, 1))
            for s in (16, 21):
                dve(nc.vector.tensor_tensor(SB[0:32, s, :], S[0:32, s, :], nb, ALU.add).then_inc(dve_done, 1))
            dve(nc.vector.tensor_copy(SB[:, 22:24, :], S[:, 22:24, :]).then_inc(dve_done, 1))
            dve.free("ds", l, b)
            for k, (a, e) in enumerate(GR3):
                dve(nc.vector.reduce_max(MX[:, 16 * k:16 * k + 16], SB[:, a:e, :].rearrange("p s c -> p c s"), axis=AX.X).then_inc(dve_done, 1), "MX", l, b)

        def dve_decode_values(dve, l, b):
            dve.wait_ge(act_done, at("EB", l, b))
            for k, (a, e) in enumerate(GR3):
                dve(nc.vector.reduce_sum(ES[:, 16 * k:16 * k + 16], EB[:, a:e, :].rearrange("p s c -> p c s"), axis=AX.X).then_inc(dve_done, 1), "ES", l, b)
            dve.wait_ge(pe_done, at("full", "dp", l, b))
            ps = bank("dp", l, b)
            q = 32 * (b % 4)
            dve(nc.vector.tensor_copy(OR[q:q + 16, b // 4, :], ps[0:16, :]).then_inc(dve_done, 1), "OR", l)
            dve.free("dp", l, b)
            dve.wait_ge(pe_done, at("full", "dd", l, b))
            ps = bank("dd", l, b)
            dve(nc.vector.tensor_copy(DEN3[:, b, :], ps[:, 0:48]).then_inc(dve_done, 1))
            dve.free("dd", l, b)

        def dve_decode_out(dve, l):
            for k in range(2):
                dve.wait_ge(pe_done, at("full", "ot", l, k))
                ps = bank("ot", l, k)
                p4 = ps[:, :].rearrange("p (a b c) -> p a b c", a=4, b=4)
                ts = slice(16 * k, 16 * k + 16)
                for h in range(2):
                    for r in range(2):
                        dve(nc.vector.tensor_copy(OTA[half(h), 1 + r, :, ts].rearrange("p g (b t) -> p b g t", b=4),
                                                p4[half(h), r, :, 8 * h:8 * h + 8].rearrange("p b (g t) -> p b g t", g=2)).then_inc(dve_done, 1))
                        o = 4 * (2 * r + h)
                        dve(nc.vector.tensor_copy(OTM[half(h), r, ts].rearrange("p (b t) -> p b t", b=4), p4[half(h), 2 + r, :, o:o + 4]).then_inc(dve_done, 1))
                dve.free("ot", l, k)
            dve(nc.vector.reciprocal(DEN3, DEN3).then_inc(dve_done, 1))
            for h in range(2):
                for r in range(2):
                    o = OTA[half(h), 1 + r].rearrange("p g (b t) -> p b g t", b=DB)
                    dve(nc.vector.tensor_tensor(o, o, DEN3[half(h), :, 16 * r + 8 * h:16 * r + 8 * h + 8].rearrange("p b (g t) -> p b g t", g=2), ALU.mult).then_inc(dve_done, 1))
                o = OTM[half(h)].rearrange("p q (b t) -> p b q t", b=DB)
                dve(nc.vector.tensor_tensor(o, o, DEN3[half(h), :, 32:48].rearrange("p b (q h t) -> p h b q t", q=2, h=2)[:, h], ALU.mult).then_inc(dve_done, 1))
            dve.name("OTn", l)
            dve.wait_ge(pe_done, at("full", "oa", l))
            dve.wait_ge(pe_done, at("full", "ob", l))
            oa, ob = bank("oa", l), bank("ob", l)
            acc, mo = PN[0:32, 4, 0:256].rearrange("p (h d) -> p h d", h=4), PN[0:32, 4, 1292:1548]
            dve(nc.vector.tensor_copy(mo, ob[0:32, 256:512]).then_inc(dve_done, 1))
            tmp = PP[0][0:32, 0:256].rearrange("p (h d) -> p h d", h=4)
            for r, src in enumerate((oa[0:32, 0:256], oa[0:32, 256:512], ob[0:32, 0:256])):
                dve(nc.vector.tensor_tensor(acc if r == 0 else tmp, src.rearrange("p (h d) -> p h d", h=4),
                                          bc(GS[0:32, 4, 4 * r:4 * r + 4], 2, HD), ALU.mult).then_inc(dve_done, 1))
                if r:
                    dve(nc.vector.tensor_tensor(acc, acc, tmp, ALU.add).then_inc(dve_done, 1))
            dve.free("oa", l)
            dve.free("ob", l)

        def dve_prompt(dve, l):
            dve.wait_ge(pe_done, at("full", "pcs", l))
            ps = bank("pcs", l)
            s4 = PP[1].rearrange("p (i h e) -> p i h e", i=4, h=4)
            s16 = PP[1].rearrange("p (r e) -> p r e", r=16)
            dve(nc.vector.tensor_tensor(s4, ps[:, :].rearrange("p (i h e) -> p i h e", i=4, h=4),
                                      bc(C("cmpb").rearrange("p (i e) -> p i e", i=4), 2, 4), ALU.add).then_inc(dve_done, 1))
            dve.free("pcs", l)
            dve(nc.vector.reduce_max(nmx, s16, axis=AX.X).then_inc(dve_done, 1))
            dve(nc.vector.tensor_scalar(nmx, nmx, -1e29, None, ALU.max).then_inc(dve_done, 1))
            dve(nc.vector.tensor_tensor(s16, s16, bc(nmx, 2, 32), ALU.subtract).then_inc(dve_done, 1), "PCx", l)
            dve.wait_ge(act_done, at("PCe", l))
            dve(nc.vector.reduce_sum(ncs, s16, axis=AX.X).then_inc(dve_done, 1))
            dve(nc.vector.tensor_scalar(ncs, ncs, 1e-30, None, ALU.max).then_inc(dve_done, 1))
            dve(nc.vector.reciprocal(ncs, ncs).then_inc(dve_done, 1))
            n4 = ncs.rearrange("p (i h) -> p i h", i=4)
            dve(nc.vector.tensor_tensor(n4, n4, GS[:, 0:4, 0:4], ALU.mult).then_inc(dve_done, 1))
            dve(nc.vector.tensor_tensor(s16, s16, bc(ncs, 2, 32), ALU.mult).then_inc(dve_done, 1), "PC", l)
            dve.wait_ge(pe_done, at("full", "pct", l))
            ps = bank("pct", l)
            dve(nc.vector.tensor_copy(PT[1], ps[:, :]).then_inc(dve_done, 1), "PCT", l)
            dve.free("pct", l)
            for hf in range(2):
                dve.wait_ge(pe_done, at("full", "pco", l, hf))
                ps = bank("pco", l, hf)
                dve(nc.vector.tensor_copy(PN[:, 2 * hf:2 * hf + 2, 0:256], ps[:, :].rearrange("p (i c) -> p i c", i=2)).then_inc(dve_done, 1))
                dve.free("pco", l, hf)
            dve_unit_m(dve, l, 0)
            for u, (br, i, h) in enumerate(UNITS):
                dve_decode_row(dve, l, u // 3, u % 3)
                if u + 1 < len(UNITS):
                    dve_unit_m(dve, l, u + 1)
                n = ukeys(br, i)
                dve.wait_ge(pe_done, at("full", "ut", l, u, 0))
                ps = bank("ut", l, u, 0)
                if u:
                    dve.wait_ge(pe_done, at("full", "uv", l, u - 1))
                dve(nc.vector.tensor_copy(PT[0][:, 0:n], ps[:, 0:n]).then_inc(dve_done, 1), "UT", l, u, 0)
                dve.free("ut", l, u, 0)
                dve.wait_ge(act_done, at("UE", l, u, 1))
                c2 = CO[:, 2 * (u % 8):2 * (u % 8) + 2]
                dve(nc.vector.reciprocal(c2, ps2[u % 2]).then_inc(dve_done, 1))
                if br != "m":
                    r = 4 if br == "s" else 8
                    dve(nc.vector.tensor_tensor(c2, c2, GS[:, i, r:r + 4].rearrange("p (g h) -> p h g", g=2)[:, h], ALU.mult).then_inc(dve_done, 1))
                dve.wait_ge(pe_done, at("full", "uv", l, u))
                ps = bank("uv", l, u)
                pv = ps[:, 0:128].rearrange("p (g d) -> p g d", g=2)
                base = 1292 if br == "m" else 0
                dst = PN[:, i, base:base + 256].rearrange("p (g h d) -> p h g d", g=2, h=2)[:, h]
                if br == "m":
                    dve(nc.vector.tensor_tensor(dst, pv, bc(c2, 2, HD), ALU.mult).then_inc(dve_done, 1))
                else:
                    t = CO2.rearrange("p (g d) -> p g d", g=2)
                    dve(nc.vector.tensor_tensor(t, pv, bc(c2, 2, HD), ALU.mult).then_inc(dve_done, 1))
                    dve(nc.vector.tensor_tensor(dst, dst, t, ALU.add).then_inc(dve_done, 1))
                dve.free("uv", l, u)
                if u % 3 == 2:
                    dve_decode_row(dve, l, u // 3, 3)

        CO2 = cv(128)

        def dve_unit_m(dve, l, u):
            br, i, h = UNITS[u]
            n = ukeys(br, i)
            if br == "m":
                dve.wait_ge(pe_done, at("full", "us", l, u, 0))
                ps = bank("us", l, u, 0)
                dve(nc.vector.reduce_max(pm2[u % 2], ps[:, :].rearrange("p (g n) -> p g n", g=2), axis=AX.X, negate=True).then_inc(dve_done, 1), "UM", l, u)
            else:
                for g in range(2):
                    dve.wait_ge(pe_done, at("full", "us", l, u, g))
                    ps = bank("us", l, u, g)
                    dve(nc.vector.reduce_max(pm2[u % 2][:, g:g + 1], ps[:, 0:n], axis=AX.X, negate=True).then_inc(dve_done, 1), "UM", l, u)

        PE_STAGES = (pe_m, pe_r, pe_n,)
        ACT_STAGES = (act_m, act_r, act_n,)
        DVE_STAGES = (dve_m, dve_r, dve_n,)
        POOL_STAGES = (pool_m, pool_r, pool_n,)

        def pe_out(pe, l):
            for t0 in (0, 2, 4, 6):
                pe.wait_ge(dve_done, at("YT", l, t0))
            for hf in range(2):
                pe.wait_ge(sem_of_slot("wout", l, hf), at("here", "wout", l, hf))
                w = slot("wout", l, hf).rearrange("p (k c) -> p k c", k=KT)
                for i in range(TILES):
                    ps = pe.open("out", l, hf, i)
                    for k in range(KT):
                        last = nc.tensor.matmul(ps[0:rows(i), :], YT[:, k, tok(i)], w[:, k, :], start=(k == 0), stop=(k == KT - 1))
                    pe.full(last.then_inc(pe_done, 1), "out", l, hf, i)
                pe.name("used", "wout", l, hf)

        def dve_out(dve, l):
            dve.wait_ge(x_reloaded[l], at("xr", l))
            for hf in range(2):
                for i in range(TILES):
                    dve.wait_ge(pe_done, at("full", "out", l, hf, i))
                    ps = bank("out", l, hf, i)
                    xs = X[0:rows(i), i, 512 * hf:512 * hf + 512]
                    dve(nc.vector.tensor_tensor(xs, ps[0:rows(i), :], xs, ALU.add).then_inc(dve_done, 1))
                    dve.free("out", l, hf, i)
            dve.name("x", l + 1)

        block = ctx.enter_context(nc.Block())

        @block.sync
        def _(eng):
            sp = Line(plan, eng, "sp")
            sp.dma("x", sp.eng.dma_start(X, io["x"]).then_inc(x_in, 16), "x", 0)
            sp.dma("const", sp.eng.dma_start(cst[:, :], io["const"]).then_inc(const_in, 16), "const")
            sp.dma("prm0", sp.eng.dma_start(prm[:, :], io["prm"][0]).then_inc(prm_in[0], 16), "prm", 0)
            sp.dma("ptab", sp.eng.dma_start(ptab[:, :], io["ptab"]).then_inc(ptab_in, 16), "ptab")
            sp.dma("memx0", sp.eng.dma_start(E["memx"], io["memx"]).then_inc(memx_in[0], 16), "memx", 0)
            sync_stream(sp)

        @block.gpsimd
        def _(eng):
            pool = Line(plan, eng, "pool")
            for l in range(DEPTH):
                if l:
                    for who in ("pe", "dve", "act"):
                        pool.wait_ge(done[who], at(who, "N", l - 1))
                    pool.dma(f"prm{l}", pool.eng.dma_start(prm[:, :], io["prm"][l]).then_inc(prm_in[l], 16), "prm", l)
                    pool.wait_ge(stored["N"][l - 1], at("stN", l - 1))
                    pool.dma(f"memx{l}", pool.eng.dma_start(E["memx"], io["memx"]).then_inc(memx_in[l], 16), "memx", l)
                    pool.wait_ge(dve_done, at("x", l))
                    pool.dma(f"ys{l}", pool.eng.dma_start(io["y"], X).then_inc(y_kept[l], 16), "ys", l)
                for st in POOL_STAGES:
                    st(pool, l)
            pool.wait_ge(dve_done, at("x", DEPTH))
            pool.dma("st_end", pool.eng.dma_start(io["y"], X).then_inc(y_stored, 16), "end")
            pool.wait_ge(y_stored, at("end"))
            for l in range(DEPTH):
                for ph in "EMRN":
                    pool.wait_ge(stored[ph][l], at("st" + ph, l))

        @block.tensor
        def _(eng):
            pe = Line(plan, eng, "pe", chained=False)
            for l in range(DEPTH):
                pe_norm(pe, l)
                pe_memkv(pe, l)
                for st in PE_STAGES:
                    st(pe, l)
                pe_out(pe, l)

        @block.scalar
        def _(eng):
            act = Line(plan, eng, "act")
            for l in range(DEPTH):
                act_norm(act, l)
                act_memkv(act, l)
                phase_end(act, "E", l)
                for st in ACT_STAGES:
                    st(act, l)

        @block.vector
        def _(eng):
            dve = Line(plan, eng, "dve")
            for l in range(DEPTH):
                dve_norm(dve, l)
                dve_memkv(dve, l)
                phase_end(dve, "E", l)
                for st in DVE_STAGES:
                    st(dve, l)
                dve_out(dve, l)


def layout(inp):
    f = np.float32
    I = {k: np.asarray(v) for k, v in inp.items()}
    o = {"const": CONST}

    def rep(a):
        return np.broadcast_to(a, (128,) + a.shape)

    w = I["w_in"]
    A0 = 0
    B0 = 1288
    C0_ = B0 + 1292
    D0 = C0_ + 1152
    ar = np.arange
    gk = np.concatenate([ar(64) + 64 * (2 * kv + g) for g in range(2) for kv in range(2)])
    gh = np.array([2 * kv + g for g in range(2) for kv in range(2)])
    cols = {
        "F0": A0 + ar(512), "T0": np.concatenate([A0 + 512 + ar(256), A0 + 776 + ar(256)]),
        "T1": np.concatenate([A0 + 1032 + ar(256), A0 + 768 + ar(8)]),
        "F1": C0_ + ar(512), "F2": C0_ + 512 + ar(384), "T2": C0_ + 896 + ar(256),
        "T3": np.concatenate([B0 + gk, B0 + 512 + ar(128), B0 + 768 + ar(128)]),
        "T4": np.concatenate([B0 + 256 + ar(256), B0 + 640 + ar(128), B0 + 896 + ar(128)]),
        "T5": np.concatenate([B0 + 1036 + gk] + [B0 + 1024 + 4 * br + gh for br in range(3)]),
        "T6": D0 + ar(512)}
    parts = []
    for n, wd in CHUNKS:
        ww = w[:, :, cols[n]].reshape(DEPTH, KT, 128, wd).transpose(0, 2, 1, 3).reshape(DEPTH, 128, KT * wd)
        parts.append(ww)
    o["win_"] = np.ascontiguousarray(np.concatenate(parts, 2))
    rowsel = np.concatenate([ar(256), 256 + gk, 512 + ar(256), 768 + ar(256)])
    wo = I["w_out"][:, rowsel]
    o["wout"] = np.ascontiguousarray(wo.reshape(DEPTH, KT, 128, 2, 512).transpose(0, 3, 2, 1, 4).reshape(DEPTH, 2, 128, 4096))
    o["wmem"] = np.ascontiguousarray(I["w_mem_kv"].reshape(DEPTH, KT, 128, 512).transpose(0, 2, 1, 3).reshape(DEPTH, 128, 4096))
    w1 = I["nsa_cmp_w1"]
    r = w1.reshape(DEPTH, 2, 2, 16, 64, 64)
    w1p = r.reshape(DEPTH, 2, 2, 8, 2, 64, 64).transpose(0, 4, 5, 1, 3, 2, 6)
    w1p = w1p.reshape(DEPTH, 128, 2048)
    w1f = r.transpose(0, 4, 1, 3, 2, 5).reshape(DEPTH, 64, 4096)
    o["w1f"] = np.ascontiguousarray(np.concatenate([w1f, w1f], 1))
    pe = I["nsa_pe"].reshape(DEPTH, 2, 2, 8, 2, 64).transpose(0, 4, 5, 1, 2, 3).reshape(DEPTH, 128, 32)
    w2 = I["nsa_cmp_w2"].transpose(0, 2, 1, 3).reshape(DEPTH, 64, 128)
    fm = lambda a, n: a.reshape(n, 128).T
    prm = []
    for l in range(DEPTH):
        qk = I["nsa_qk_g"][l]
        P = {
            "g": fm(I["norm_g"][l], 8), "mg": fm(I["mem_norm_g"][l], 8),
            "cw": I["mlstm_conv_w"][l].reshape(4, 4, 128).transpose(2, 1, 0).reshape(128, 16), "cb": fm(I["mlstm_conv_b"][l], 4),
            "gb": rep(I["mlstm_gate_b"][l].reshape(8)), "mlg": rep(I["mlstm_norm_g"][l]),
            "qkg": rep(np.concatenate([qk[0]] * 4 + [qk[2]] * 2 + [qk[3]] * 2)), "kcg": np.concatenate([qk[1], qk[1]])[:, None],
            "mqg": rep(I["mem_qk_g"][l, 0]), "mkg": rep(I["mem_qk_g"][l, 1]), "mu": fm(I["rwkv_mu"][l], 7),
            "w0": fm(I["rwkv_w0"][l], 2), "a0": fm(I["rwkv_a0"][l], 2),
            "kk": fm(I["rwkv_kk"][l, 0], 2), "ka": fm(I["rwkv_kk"][l, 1], 2), "rk": fm(I["rwkv_kk"][l, 2], 2),
            "ln0": rep(I["rwkv_ln"][l, 0]), "ln1": rep(I["rwkv_ln"][l, 1]),
            "lora": np.concatenate([I["rwkv_w2"][l], I["rwkv_a2"][l]], 0), "w2": np.concatenate([w2[l], w2[l]], 0),
            "pe": pe[l], "w1p": w1p[l]}
        prm.append(np.concatenate([P[n].astype(f, copy=False) for n, _ in PARAMS], 1))
    o["prm"] = np.ascontiguousarray(np.stack(prm))
    x = np.zeros((128, TILES, D), f)
    x[:, 0:4] = I["x_prompt"].reshape(4, 128, D).transpose(1, 0, 2)
    x[0:DTOK, 4] = I["x_sample"].reshape(DTOK, D)
    o["x"] = x
    o["memx"] = np.ascontiguousarray(I["mem_prompt"].reshape(2, 128, D).transpose(1, 0, 2))
    o["ptab"] = np.ascontiguousarray(I["page_table"].reshape(1, DB * NPAGE))
    cc = I["cache_cmp_kv"].reshape(DEPTH, NPOOL, 8, 8, 2, 2, 2, 64)
    o["cmpL"] = np.ascontiguousarray(cc.transpose(0, 1, 4, 7, 3, 6, 2, 5).reshape(DEPTH, NPOOL, 128, 256))
    sc = I["cache_slc_kv"].reshape(DEPTH, NPOOL, 8, 8, 2, 2, 2, 64)
    o["slcK"] = np.ascontiguousarray(sc[..., 0, :].transpose(0, 1, 4, 6, 2, 5, 3).reshape(DEPTH, NPOOL, 128, 128))
    o["slcV"] = np.ascontiguousarray(sc[..., 1, :].reshape(DEPTH, NPOOL, 8, 2048))
    wc = I["cache_win_kv"].reshape(DEPTH, DB, 128, 2, 2, 2, 2, 64)
    wK = wc[..., 0, :].transpose(0, 1, 4, 6, 5, 3, 2).reshape(DEPTH, DB, 128, 512)
    wV = wc[..., 1, :].reshape(DEPTH, DB, 128, 512)
    mc = I["cache_mem_kv"].reshape(DEPTH, DB, 128, 2, 4, 2, 64)
    mK = mc[..., 0, :].transpose(0, 1, 3, 5, 4, 2).reshape(DEPTH, DB, 128, 512)
    mV = mc[..., 1, :].reshape(DEPTH, DB, 128, 512)
    o["wmL"] = np.ascontiguousarray(np.concatenate([wK, wV, mK, mV], 3))
    o["winraw"] = np.ascontiguousarray(I["cache_win_kv"].reshape(DEPTH, DB, WIN, 256))
    mC = I["state_mlstm_C"].reshape(DEPTH, DB, 2, 2, 64, 64)
    o["mC0"] = np.ascontiguousarray(mC.transpose(0, 3, 4, 2, 1, 5).reshape(DEPTH, 128, 2, 8, 64))
    mn = I["state_mlstm_n"].reshape(DEPTH, DB, 2, 2, 64)
    o["mn0"] = np.ascontiguousarray(mn.transpose(0, 3, 4, 2, 1).reshape(DEPTH, 128, 2, 8))
    o["mm0"] = np.ascontiguousarray(I["state_mlstm_m"].transpose(0, 2, 1))
    o["mconv0"] = np.ascontiguousarray(I["state_mlstm_conv"].reshape(DEPTH, DB, 3, 4, 128).transpose(0, 4, 3, 1, 2))
    rS = I["state_rwkv_S"].reshape(DEPTH, DB, 2, 2, 64, 64)
    o["rS0"] = np.ascontiguousarray(rS.transpose(0, 3, 5, 1, 2, 4).reshape(DEPTH, 128, 8, 128))
    o["rsh0"] = np.ascontiguousarray(I["state_rwkv_shift"].reshape(DEPTH, DB, NRT, 128).transpose(0, 3, 2, 1))
    return o


def unlayout(r):
    A = np.ascontiguousarray

    def rows_of(a, n):
        return a[:, 0:4].transpose(1, 0, 2).reshape(SEQ, n), a[0:DTOK, 4]

    yp, ys = rows_of(r["y"], D)
    outs = [yp.reshape(1, SEQ, D), ys.reshape(DB, DS, D)]

    def kv(name):
        p, s = zip(*[rows_of(r[name][l], 256) for l in range(DEPTH)])
        p = np.stack(p).reshape(DEPTH, 1, SEQ, 2, 2, 64).transpose(0, 1, 2, 4, 3, 5)
        s = np.stack(s).reshape(DEPTH, DB, DS, 2, 2, 64).transpose(0, 1, 2, 4, 3, 5)
        return p, s

    outs += [*kv("cmp"), *kv("slc")]
    p, s = kv("win")
    past = r["winpast"].reshape(DEPTH, DB, WIN - DS, 2, 2, 64)
    outs += [p, np.concatenate([past, s], 2)]
    outs.append(r["mem"].transpose(0, 2, 1, 3).reshape(DEPTH, 1, NMEM, 2, NH, 64).transpose(0, 1, 2, 4, 3, 5))
    C = r["mC"].reshape(DEPTH, 2, 64, 2, 65).transpose(0, 3, 1, 2, 4).reshape(DEPTH, 1, NH, 64, 65)
    outs.append(C[..., 0:64])
    outs.append(r["mCd"].reshape(DEPTH, 2, 64, 2, 8, 64).transpose(0, 4, 3, 1, 2, 5).reshape(DEPTH, DB, NH, 64, 64))
    outs.append(C[..., 64])
    outs.append(r["mnd"].reshape(DEPTH, 2, 64, 2, 8).transpose(0, 4, 3, 1, 2).reshape(DEPTH, DB, NH, 64))
    outs.append(r["mm"][:, 127:128, 3, :])
    outs.append(r["mm"][:, 3:32:4, 4, :])
    cv = r["mconv"].transpose(0, 3, 4, 2, 1).reshape(DEPTH, 9, 3, 512)
    outs += [cv[:, 0:1], cv[:, 1:]]
    S = r["rS"].reshape(DEPTH, 2, 64, 9, 2, 64).transpose(0, 3, 4, 1, 5, 2).reshape(DEPTH, 9, NH, 64, 64)
    outs += [S[:, 8:9], S[:, 0:8]]
    sh = r["rsh"].transpose(0, 3, 2, 1).reshape(DEPTH, 9, 1, 896)
    outs += [sh[:, 8:9], sh[:, 0:8]]
    return tuple(A(o) for o in outs)


def kernel(**inputs):
    from concourse import bacc
    from concourse.bass_utils import run_bass_kernel_spmd

    arrays = layout(inputs)
    plan = Plan()
    for counting in (True, False):
        plan.counting = counting
        nc = bacc.Bacc("TRN2", target_bir_lowering=False, num_devices=1)
        io = {n: nc.dram_tensor("in_" + n, arrays[n].shape, mybir.dt.from_np(arrays[n].dtype), kind="ExternalInput").ap() for n in INS}
        for n, shape in OUTS.items():
            io[n] = nc.dram_tensor("out_" + n, shape, F32, kind="ExternalOutput").ap()
        build(nc, io, plan)
    r = run_bass_kernel_spmd(nc, [{"in_" + n: arrays[n] for n in INS}], core_ids=[0])
    return unlayout({n: r.results[0]["out_" + n] for n in OUTS})
```
